# Optimizing a Trainium2 kernel written in Bass

```python
import jax
import jax.numpy as jnp
from jax import lax
import numpy as np

D_MODEL = 1024
BATCH = 1
SEQ = 1024
DEPTH = 2

MLA_HEADS = 4
MLA_Q_LORA = 256
MLA_KV_LORA = 128
MLA_NOPE = 64
MLA_ROPE = 32
MLA_V = 64
ROPE_THETA = 10000.0
LRU_WIDTH = 256
LRU_BLOCKS = 4
LRU_BLOCK_W = LRU_WIDTH // LRU_BLOCKS
CONV_WIDTH = 4
LRU_C = 8.0
SB_HEADS = 4
SB_HD = 64
HG_HEADS = 4
HG_DK = 64
HG_DV = 64
HG_CHUNK = 64
Q_BLOCK = 128
GROUP_W = MLA_HEADS * MLA_V
D_MIX = MLA_HEADS * MLA_V + LRU_WIDTH + SB_HEADS * SB_HD + HG_HEADS * HG_DV
FFN_HIDDEN = -(-8 * D_MODEL // (3 * 256)) * 256
NORM_EPS = 1e-6
MASK_VALUE = -1e30
LB_FLOOR = 1e-30
IN_WIDTHS = (MLA_Q_LORA, MLA_KV_LORA, MLA_ROPE,
             LRU_WIDTH, LRU_WIDTH,
             SB_HEADS * SB_HD, SB_HEADS * SB_HD, SB_HEADS * SB_HD,
             HG_HEADS * HG_DK, HG_HEADS * HG_DK, HG_HEADS * HG_DV, HG_HEADS * HG_DV)
D_IN = sum(IN_WIDTHS)

kernel_name = 'hybrid_parallel_mla_rglru_stickbreak_hgrn2'

def rmsnorm(x, g):
    xf = x.astype(jnp.float32)
    y = xf * lax.rsqrt(jnp.mean(xf * xf, axis=-1, keepdims=True) + NORM_EPS)
    return (y * g.astype(jnp.float32)).astype(x.dtype)

def rope(x, positions):
    half = x.shape[-1] // 2
    inv_freq = ROPE_THETA ** (-jnp.arange(half, dtype=jnp.float32) / half)
    ang = positions.astype(jnp.float32)[..., None] * inv_freq
    ang = ang.reshape(ang.shape[:2] + (1,) * (x.ndim - 3) + (half,))
    cos, sin = jnp.cos(ang), jnp.sin(ang)
    xf = x.astype(jnp.float32)
    x1, x2 = xf[..., :half], xf[..., half:]
    return jnp.concatenate([x1 * cos - x2 * sin, x2 * cos + x1 * sin], axis=-1).astype(x.dtype)

def to_q_blocks(t):
    b, h, s, d = t.shape
    return t.reshape(b, h, s // Q_BLOCK, Q_BLOCK, d).transpose(2, 0, 1, 3, 4)

def from_q_blocks(t):
    n, b, h, qb, d = t.shape
    return t.transpose(1, 2, 0, 3, 4).reshape(b, h, n * qb, d)

def causal_softmax_attention(q, k, v, scale):
    s_len = q.shape[2]
    kpos = jnp.arange(s_len)

    def block(args):
        qb, start = args
        s = jnp.einsum('bhqd,bhkd->bhqk', qb, k).astype(jnp.float32) * scale
        qpos = start + jnp.arange(Q_BLOCK)
        s = jnp.where(kpos[None, :] <= qpos[:, None], s, MASK_VALUE)
        p = jax.nn.softmax(s, axis=-1).astype(v.dtype)
        return jnp.einsum('bhqk,bhkd->bhqd', p, v)

    starts = jnp.arange(s_len // Q_BLOCK) * Q_BLOCK
    return from_q_blocks(lax.map(block, (to_q_blocks(q), starts)))

def stick_breaking_attention(q, k, v):
    s_len = q.shape[2]
    kpos = jnp.arange(s_len)

    def block(args):
        qb, start = args
        z = jnp.einsum('bhqd,bhkd->bhqk', qb, k).astype(jnp.float32) * (SB_HD ** -0.5)
        qpos = start + jnp.arange(Q_BLOCK)
        strict = kpos[None, :] < qpos[:, None]
        log_beta = jax.nn.log_sigmoid(z)
        log_keep = jnp.where(strict, jax.nn.log_sigmoid(-z), 0.0)
        later = lax.cumsum(log_keep, axis=3, reverse=True) - log_keep
        w = jnp.where(strict, jnp.exp(log_beta + later), 0.0)
        return jnp.einsum('bhqk,bhkd->bhqd', w.astype(v.dtype), v)

    starts = jnp.arange(s_len // Q_BLOCK) * Q_BLOCK
    return from_q_blocks(lax.map(block, (to_q_blocks(q), starts)))

def mla_mixer(c_q, c_kv, k_rope, positions, q_norm_g, w_uq, kv_norm_g, w_ukv):
    b, s, _ = c_q.shape
    q = (rmsnorm(c_q, q_norm_g) @ w_uq).reshape(b, s, MLA_HEADS, MLA_NOPE + MLA_ROPE)
    q_nope, q_pe = q[..., :MLA_NOPE], rope(q[..., MLA_NOPE:], positions)
    kv = (rmsnorm(c_kv, kv_norm_g) @ w_ukv).reshape(b, s, MLA_HEADS, MLA_NOPE + MLA_V)
    k_nope, v = kv[..., :MLA_NOPE], kv[..., MLA_NOPE:]
    k_pe = rope(k_rope, positions)
    qh = jnp.concatenate([q_nope, q_pe], axis=-1)
    kh = jnp.concatenate([k_nope, jnp.broadcast_to(k_pe[:, :, None, :], (b, s, MLA_HEADS, MLA_ROPE))], axis=-1)
    out = causal_softmax_attention(qh.transpose(0, 2, 1, 3), kh.transpose(0, 2, 1, 3),
                                   v.transpose(0, 2, 1, 3), (MLA_NOPE + MLA_ROPE) ** -0.5)
    return out.transpose(0, 2, 1, 3).reshape(b, s, MLA_HEADS * MLA_V)

def rglru_mixer(xb, gate, conv_w, conv_b, w_a, b_a, w_x, b_x, lam):
    b, s, w = xb.shape
    xc = lax.conv_general_dilated(xb, conv_w[:, None, :], window_strides=(1,),
                                  padding=((CONV_WIDTH - 1, 0),),
                                  dimension_numbers=('NWC', 'WIO', 'NWC'),
                                  feature_group_count=w) + conv_b
    xblk = xc.reshape(b, s, LRU_BLOCKS, LRU_BLOCK_W)
    rec_gate = jax.nn.sigmoid(jnp.einsum('bsnc,ncd->bsnd', xblk, w_a).reshape(b, s, w) + b_a)
    in_gate = jax.nn.sigmoid(jnp.einsum('bsnc,ncd->bsnd', xblk, w_x).reshape(b, s, w) + b_x)
    log_a = -LRU_C * rec_gate.astype(jnp.float32) * jax.nn.softplus(-lam.astype(jnp.float32))
    a = jnp.exp(log_a)
    u = jnp.sqrt(jnp.maximum(-jnp.expm1(2.0 * log_a), 0.0)) * (in_gate * xc).astype(jnp.float32)

    def combine(left, right):
        a_l, b_l = left
        a_r, b_r = right
        return a_l * a_r, a_r * b_l + b_r

    _, h = lax.associative_scan(combine, (a, u), axis=1)
    return h.astype(xb.dtype) * jax.nn.gelu(gate)

def chunked_gated_recurrence(q, k, v, log_f):
    b, s, h, dk = q.shape
    dv = v.shape[-1]
    n = s // HG_CHUNK

    def chunks(t):
        return t.reshape(b, n, HG_CHUNK, h, t.shape[-1]).transpose(1, 0, 3, 2, 4)

    incl = jnp.tril(jnp.ones((HG_CHUNK, HG_CHUNK), dtype=bool))[:, :, None]

    def step(state, inp):
        qc, kc, vc, gc = inp
        cum = jnp.cumsum(gc, axis=2)
        diff = cum[:, :, :, None, :] - cum[:, :, None, :, :]
        decay = jnp.where(incl, jnp.exp(jnp.where(incl, diff, 0.0)), 0.0)
        scores = jnp.einsum('bhtd,bhsd,bhtsd->bhts', qc, kc, decay)
        o = (jnp.einsum('bhts,bhse->bhte', scores, vc)
             + jnp.einsum('bhtd,bhde->bhte', qc * jnp.exp(cum), state))
        last = cum[:, :, -1, :]
        state = (jnp.exp(last)[..., None] * state
                 + jnp.einsum('bhsd,bhse->bhde', kc * jnp.exp(last[:, :, None, :] - cum), vc))
        return state, o

    state0 = jnp.zeros((b, h, dk, dv), jnp.float32)
    _, o = lax.scan(step, state0, (chunks(q), chunks(k), chunks(v), chunks(log_f)))
    return o.transpose(1, 0, 3, 2, 4).reshape(b, s, h, dv)

def hgrn2_mixer(q, f_logit, i, g, lb, norm_g):
    b, s, _ = q.shape
    lb = lb.astype(jnp.float32)
    fz = f_logit.astype(jnp.float32)
    log_f = jnp.logaddexp(jnp.log(jnp.maximum(lb, LB_FLOOR)), jnp.log1p(-lb) + jax.nn.log_sigmoid(fz))
    key = (1.0 - lb) * jax.nn.sigmoid(-fz)
    heads_k = lambda t: t.reshape(b, s, HG_HEADS, HG_DK)
    o = chunked_gated_recurrence(heads_k(q.astype(jnp.float32)), heads_k(key),
                                 i.astype(jnp.float32).reshape(b, s, HG_HEADS, HG_DV), heads_k(log_f))
    o = rmsnorm(o, norm_g.reshape(HG_HEADS, HG_DV)).reshape(b, s, HG_HEADS * HG_DV)
    return (o * jax.nn.silu(g.astype(jnp.float32))).astype(q.dtype)

def setup_inputs(seed: int = 0) -> dict:
    key = jax.random.key(seed)
    ks = jax.random.split(key, 26)
    nrm = lambda k, shape, scale: jax.random.normal(k, shape, jnp.float32) * scale
    gain = lambda k, shape: 1.0 + 0.05 * jax.random.normal(k, shape, jnp.float32)
    x = jax.random.normal(ks[0], (BATCH, SEQ, D_MODEL), jnp.float32)
    offset = jax.random.randint(ks[1], (BATCH, 1), 0, SEQ, dtype=jnp.int32)
    positions = (offset + jnp.arange(SEQ, dtype=jnp.int32)[None, :]).astype(jnp.int32)
    u = jax.random.uniform(ks[13], (DEPTH, LRU_WIDTH), jnp.float32, minval=0.9, maxval=0.999)
    a0 = u ** (1.0 / LRU_C)
    lru_lambda = jnp.log(a0) - jnp.log1p(-a0)
    return {
        'x': x,
        'positions': positions,
        'ln1_g': gain(ks[2], (DEPTH, D_MODEL)),
        'w_in': nrm(ks[3], (DEPTH, D_MODEL, D_IN), D_MODEL ** -0.5),
        'mla_q_norm_g': gain(ks[4], (DEPTH, MLA_Q_LORA)),
        'mla_w_uq': nrm(ks[5], (DEPTH, MLA_Q_LORA, MLA_HEADS * (MLA_NOPE + MLA_ROPE)), MLA_Q_LORA ** -0.5),
        'mla_kv_norm_g': gain(ks[6], (DEPTH, MLA_KV_LORA)),
        'mla_w_ukv': nrm(ks[7], (DEPTH, MLA_KV_LORA, MLA_HEADS * (MLA_NOPE + MLA_V)), MLA_KV_LORA ** -0.5),
        'lru_conv_w': nrm(ks[8], (DEPTH, CONV_WIDTH, LRU_WIDTH), CONV_WIDTH ** -0.5),
        'lru_conv_b': nrm(ks[9], (DEPTH, LRU_WIDTH), 0.01),
        'lru_w_a': nrm(ks[10], (DEPTH, LRU_BLOCKS, LRU_BLOCK_W, LRU_BLOCK_W), LRU_BLOCK_W ** -0.5),
        'lru_b_a': nrm(ks[11], (DEPTH, LRU_WIDTH), 0.01),
        'lru_w_x': nrm(ks[12], (DEPTH, LRU_BLOCKS, LRU_BLOCK_W, LRU_BLOCK_W), LRU_BLOCK_W ** -0.5),
        'lru_b_x': nrm(ks[14], (DEPTH, LRU_WIDTH), 0.01),
        'lru_lambda': lru_lambda,
        'hgrn_lb_logits': nrm(ks[15], (DEPTH, HG_HEADS * HG_DK), 1.0),
        'hgrn_norm_g': gain(ks[16], (DEPTH, HG_HEADS * HG_DV)),
        'group_norm_g': gain(ks[17], (DEPTH, 3, GROUP_W)),
        'w_out': nrm(ks[18], (DEPTH, D_MIX, D_MODEL), D_MIX ** -0.5),
        'ln2_g': gain(ks[19], (DEPTH, D_MODEL)),
        'w_ffn_gate': nrm(ks[20], (DEPTH, D_MODEL, FFN_HIDDEN), D_MODEL ** -0.5),
        'w_ffn_up': nrm(ks[21], (DEPTH, D_MODEL, FFN_HIDDEN), D_MODEL ** -0.5),
        'w_ffn_down': nrm(ks[22], (DEPTH, FFN_HIDDEN, D_MODEL), FFN_HIDDEN ** -0.5),
        'final_norm_g': gain(ks[23], (D_MODEL,)),
    }

def reference(x, positions, ln1_g, w_in, mla_q_norm_g, mla_w_uq, mla_kv_norm_g, mla_w_ukv,
              lru_conv_w, lru_conv_b, lru_w_a, lru_b_a, lru_w_x, lru_b_x, lru_lambda,
              hgrn_lb_logits, hgrn_norm_g, group_norm_g, w_out, ln2_g,
              w_ffn_gate, w_ffn_up, w_ffn_down, final_norm_g):
    b, s, _ = x.shape
    split_points = np.cumsum(IN_WIDTHS)[:-1].tolist()
    lb_p = jax.nn.softmax(hgrn_lb_logits.astype(jnp.float32), axis=0)
    lower_bounds = jnp.cumsum(lb_p, axis=0) - lb_p[0]
    h = x
    for l in range(DEPTH):
        u = rmsnorm(h, ln1_g[l])
        proj = u @ w_in[l]
        (c_q, c_kv, k_rope, lru_x, lru_gate, sb_q, sb_k, sb_v,
         hg_q, hg_f, hg_i, hg_g) = jnp.split(proj, split_points, axis=-1)
        y_a = mla_mixer(c_q, c_kv, k_rope, positions, mla_q_norm_g[l], mla_w_uq[l],
                        mla_kv_norm_g[l], mla_w_ukv[l])
        y_b = rglru_mixer(lru_x, lru_gate, lru_conv_w[l], lru_conv_b[l], lru_w_a[l], lru_b_a[l],
                          lru_w_x[l], lru_b_x[l], lru_lambda[l])
        sb_heads = lambda t: t.reshape(b, s, SB_HEADS, SB_HD).transpose(0, 2, 1, 3)
        y_c = stick_breaking_attention(sb_heads(sb_q), sb_heads(sb_k), sb_heads(sb_v))
        y_c = y_c.transpose(0, 2, 1, 3).reshape(b, s, SB_HEADS * SB_HD)
        y_d = hgrn2_mixer(hg_q, hg_f, hg_i, hg_g, lower_bounds[l], hgrn_norm_g[l])
        mixed = jnp.concatenate([rmsnorm(y_a, group_norm_g[l, 0]),
                                 rmsnorm(y_b, group_norm_g[l, 1]),
                                 rmsnorm(y_c, group_norm_g[l, 2]),
                                 y_d], axis=-1)
        h = h + mixed @ w_out[l]
        u = rmsnorm(h, ln2_g[l])
        h = h + (jax.nn.silu(u @ w_ffn_gate[l]) * (u @ w_ffn_up[l])) @ w_ffn_down[l]
    return rmsnorm(h, final_norm_g)


_drawn_inputs = setup_inputs


def setup_inputs(seed=0):
    import zlib

    import numpy as np

    out = dict(_drawn_inputs(seed))
    spreads = {}
    factors = {'lru_b_a': 40.219, 'lru_b_x': 29.823, 'hgrn_norm_g': 3.466}
    for name, (base, spread) in spreads.items():
        noise = np.random.default_rng([zlib.crc32(name.encode()), seed]).standard_normal(out[name].shape)
        drawn = base * np.exp(spread * noise) if base else spread * noise
        out[name] = jnp.asarray(drawn.astype(out[name].dtype))
    for name, factor in factors.items():
        out[name] = (out[name] * factor).astype(out[name].dtype)
    return out
```

```python
import math

import numpy as np
import concourse.bass as bass
from concourse import mybir
from contextlib import ExitStack

F32 = mybir.dt.float32
F32R = mybir.dt.float32r
I32 = mybir.dt.int32
U8 = mybir.dt.uint8
ACT = mybir.ActivationFunctionType
ALU = mybir.AluOpType
AX = mybir.AxisListType

P = 128
D = 1024
S = 1024
DEPTH = 2
KT = D // P
TT = S // P
HALF = 512
PAIRS = 2
Q_LORA, KV_LORA, NOPE, ROPE, HD = 256, 128, 64, 32, 64
GROUP_W = 256
FFN = 2816
CONV = 4
LRU_C = 8.0
EPS = 1e-6
MASKED = -1e30
LB_FLOOR = 1e-30
CHUNK = P
NCH = S // CHUNK
LEVELS = 7
D_IN = 2720
C_CQ, C_CKV, C_ROPE, C_X, C_GATE = 0, 256, 384, 416, 672
C_SBQ, C_SBK, C_SBV = 928, 1184, 1440
C_HQ, C_HF, C_HI, C_HG = 1696, 1952, 2208, 2464
MLA_SCALE = (NOPE + ROPE) ** -0.5
SB_SCALE = HD ** -0.5
LN_FLOOR = 2.0 ** -60
LN_SCALE = 1e15

PAIR_ROWS = 9
V_TAP, V_CB, V_BA, V_BX, V_LAM, V_HG = 0, 4, 5, 6, 7, 8
V_LN1, V_LN2, V_QN, V_KVN, V_GN, V_ROWS = 18, 26, 34, 36, 37, 43
VEC_ROWS = [("conv_w", 2 * tap + pr, 1, pr * PAIR_ROWS + V_TAP + tap) for pr in range(PAIRS) for tap in range(CONV)]
VEC_ROWS += [(key, pr, 1, pr * PAIR_ROWS + row) for pr in range(PAIRS)
             for key, row in (("conv_b", V_CB), ("b_a", V_BA), ("b_x", V_BX), ("lam", V_LAM), ("hg", V_HG))]
VEC_ROWS += [("ln1", 0, KT, V_LN1), ("ln2", 0, KT, V_LN2), ("q_norm", 0, 2, V_QN), ("kv_norm", 0, 1, V_KVN),
             ("group_norm", 0, 6, V_GN)]
W_LBA, W_LBC, W_LBD, W_C1, W_T0, W_T1, W_T2, W_T3, W_T4, W_N = 9, 10, 11, 12, 13, 14, 15, 16, 17, 18

K_ID, K_STRICT, K_NEGS, K_NEGC, K_HEADS, K_FREQ, K_SIGN, K_N = 0, 128, 256, 384, 512, 640, 641, 642

TWO_PI_1 = 6.28125
TWO_PI_2 = float(np.float32(np.round((2 * math.pi - 6.28125) * 2 ** 20) / 2 ** 20))
TWO_PI_3 = float(np.float32(2 * math.pi - 6.28125 - TWO_PI_2))
ROUND = 1.5 * 2.0 ** 23
PI_BELOW = 3.1415925


def build(nc, x, positions, vec_in, w_in, w_uq, w_ukv, w_a, w_x, lb_logits, w_out,
          w_gate, w_up, w_down, final_g, consts, level_masks, out):
    h_dram = nc.dram_tensor("h_spill", (D, S), F32).ap()
    ctx = ExitStack()
    with ctx:
        base = (nc.sbuf_base + 31) // 32 * 32
        cursor = [base]

        def fixed(name, shape, dtype=F32):
            size = math.prod(shape[1:]) * (1 if dtype == U8 else 4)
            t = nc.alloc_sbuf_tensor_at(name, shape, dtype, offset=cursor[0])
            cursor[0] += (size + 31) // 32 * 32
            return t

        CO = fixed("constants", [P, K_N])
        LM = fixed("level_mask", [P, LEVELS * 64], U8)
        ones = fixed("ones", [P, P])
        vecs = fixed("vectors", [P, V_ROWS])
        lbt = fixed("lower_bound", [P, 3, 4])
        pv = fixed("pair_vectors", [P, W_N])
        eps = fixed("eps", [P, 1])
        half_pi = fixed("half_pi", [P, 1])
        WA = fixed("w_a_blocks", [P, P])
        WX = fixed("w_x_blocks", [P, P])
        RT = fixed("rope", [P, S])
        raw = [fixed(f"w_raw{i}", [P, 1024]) for i in range(2)]
        whi = [fixed(f"w_hi{i}", [P, 1024], F32R) for i in range(2)]
        wlo = [fixed(f"w_lo{i}", [P, 1024], F32R) for i in range(2)]
        NM = fixed("mla_neg_max", [P, 2, 2])
        RSUM = fixed("mla_row_sum", [P, 4, 2])
        GMS = fixed("group_mean_sq", [P, 2, TT])
        U0 = cursor[0]
        uhi = fixed("u_hi", [P, KT, S], F32R)
        ulo = fixed("u_lo", [P, KT, S], F32R)
        R0 = cursor[0]
        KB = 1024

        def at_u(name, kb, shape, dtype=F32):
            return nc.alloc_sbuf_tensor_at(name, shape, dtype, offset=U0 + kb * KB)

        def at_r(name, kb, shape, dtype=F32):
            return nc.alloc_sbuf_tensor_at(name, shape, dtype, offset=R0 + kb * KB)

        YB = at_r("y_b", 0, [P, PAIRS, S])
        YD = at_r("y_d", 8, [P, PAIRS, S])
        YA = at_r("y_a", 16, [P, TT, GROUP_W])
        YC = at_r("y_c", 24, [P, TT, GROUP_W])
        h = at_r("h", 32, [P, KT, S])

        ps = ctx.enter_context(nc.psum_tensor("ps", [P, 8, HALF], F32))

        def pair(p, rows=slice(0, P)):
            return ps[rows, 2 * p:2 * p + 2, :]

        def wide(ap):
            return ap.rearrange("p (b n) -> p b n", b=2)

        ident = CO[:, K_ID:K_ID + P]

        names = []

        def sem(name):
            s = ctx.enter_context(nc.semaphore(name))
            names.append(s)
            return s

        def sems(name, n):
            return [sem(f"{name}{i}") for i in range(n)]

        def end_of_block():
            nc.all_engine_barrier(sems_to_clear=range(names[0].num, names[-1].num + 1))

        raw_loaded = sems("raw_loaded", 2)
        hi_split = sem("hi_split")
        slot_split = sem("slot_split")
        proj_done = sem("proj_done")
        bank_free = sems("pair_free", 4)
        small_loaded = sem("small_loaded")
        h_moved = sem("h_moved")
        stored = sem("stored")
        sq_ready = sem("sq_ready")
        sq_used = sem("sq_used")
        ms_done = sem("ms_done")
        rstd_part = sem("rstd_part")
        rstd_ready = sem("rstd_ready")
        t_ready = sem("t_ready")
        uhi_done = sem("uhi_done")
        ulo_done = sems("ulo_done", 2)
        act_step = sem("act_step")
        dve_step = sem("dve_step")
        pool_step = sem("pool_step")

        def exp_and_ln():
            nc.scalar.preload_act_table_set("natural_log_exp_and_others")

        def load_slot(sp, n, parts):
            if n >= 4:
                sp.wait_ge(slot_split, n - 3)
            for dst, src in parts:
                sp.dma_start(dst, src).then_inc(raw_loaded[n % 2], 16)

        def split_slot(pool, n, dmas, jobs, width=1024):
            i = n % 2
            pool.wait_ge(raw_loaded[i], 16 * dmas)
            if jobs:
                pool.wait_ge(proj_done, jobs)
            nc.gpsimd.tensor_tensor(whi[i][:, 0:width], raw[i][:, 0:width], ones[:, 0:1].broadcast_to([P, width]),
                                    ALU.mult).then_inc(hi_split, 1)
            pool.wait_ge(hi_split, n - 1)
            nc.gpsimd.tensor_tensor(wlo[i][:, 0:width], raw[i][:, 0:width],
                                    whi[i][:, 0:width].bitcast(F32),
                                    ALU.subtract).then_inc(slot_split, 1)

        def product(pe, bank0, lhs, rhs, kt, before_k=None, rows=P):
            for k in range(kt):
                if before_k is not None:
                    before_k(k)
                lh, ll = lhs(k)
                rh, rl = rhs(k)
                for n, (a, b) in enumerate(((lh, rh), (lh, rl), (ll, rh))):
                    for half in range(2):
                        last = nc.tensor.matmul(ps[0:rows, bank0 + half, :], a, b[:, half * HALF:(half + 1) * HALF],
                                                start=(k == 0 and n == 0), stop=(k == kt - 1 and n == 2))
            return last

        def slot_lhs(n, off=0, step=P, width=P):
            i = n % 2
            return lambda k: (whi[i][:, off + k * step:off + k * step + width],
                              wlo[i][:, off + k * step:off + k * step + width])

        def u_rhs(k):
            return uhi[:, k, :], ulo[:, k, :]

        def project_slot(pe, n, job, p, before_k=None):
            if n >= 2:
                pe.wait_ge(slot_split, n - 1)
            last = product(pe, 2 * p, slot_lhs(n), u_rhs, KT, before_k)
            last.then_inc(proj_done, 1)

        def norm_act(act, SQ, RS, uh, T, p, wait_k, summed, read):
            exp_and_ln()
            for k in range(KT):
                wait_k(act, k)
                if k >= 2:
                    act.wait_ge(sq_used, max(1, k - 2))
                nc.scalar.activation(SQ[k % 2][:, :], h[:, k, :], ACT.Square).then_inc(sq_ready, 1)
            act.wait_ge(*summed)
            nc.scalar.activation(wide(RS[:, :]), pair(p), ACT.Ln, scale=1.0 / D,
                                 bias=eps[:, 0:1]).then_inc(read[0], 1)
            act.wait_ge(*read)
            nc.scalar.activation(RS[:, :], RS[:, :], ACT.Exp, scale=-0.5).then_inc(rstd_ready, 1)
            if uh is None:
                return
            for k in range(KT):
                act.wait_ge(t_ready, k + 1)
                nc.scalar.activation(uh[:, k, :], T[k % 2][:, :], ACT.Copy).then_inc(uhi_done, 1)

        def norm_sum_dve(dve, SQ, ACC):
            for k in range(1, KT):
                dve.wait_ge(sq_ready, k + 1)
                if k >= 2:
                    dve.wait_ge(sq_used, k - 1)
                nc.vector.tensor_tensor(ACC[:, :], SQ[0][:, :] if k == 1 else ACC[:, :], SQ[k % 2][:, :],
                                        ALU.add).then_inc(sq_used, 1)

        def norm_scale_dve(dve, RS, T, ul, uh, gain):
            dve.wait_ge(rstd_ready, 1)
            for k in range(KT):
                if k >= 2:
                    dve.wait_ge(ulo_done[k % 2], k // 2)
                nc.vector.scalar_tensor_tensor(T[k % 2][:, :], h[:, k, :], gain(k), RS[:, :],
                                               ALU.mult, ALU.mult).then_inc(t_ready, 1)
                if k >= 1 and (k - 1) % 2 == 1:
                    lo_tile(dve, nc.vector, k - 1, T, ul, uh)
            lo_tile(dve, nc.vector, KT - 1, T, ul, uh)

        def norm_lo_pool(pool, T, ul, uh):
            for k in range(0, KT, 2):
                lo_tile(pool, nc.gpsimd, k, T, ul, uh)

        def lo_tile(eng, ops, k, T, ul, uh):
            eng.wait_ge(uhi_done, k + 1)
            ops.tensor_tensor(ul[:, k, :], T[k % 2][:, :], uh[:, k, :].bitcast(F32),
                              ALU.subtract).then_inc(ulo_done[k % 2], 1)

        def norm_sum_pe(pe, ACC, p, done):
            pe.wait_ge(sq_used, KT - 1)
            for half in range(2):
                last = nc.tensor.matmul(ps[:, 2 * p + half, :], ones[:, :], ACC[:, half * HALF:(half + 1) * HALF],
                                        start=True, stop=True)
            last.then_inc(done, 1)

        def u_ready(pe):
            return lambda k: pe.wait_ge(ulo_done[k % 2], k // 2 + 1)

        XIN = [at_r(f"x_in{i}", 64 + 4 * i, [P, D]) for i in range(2)]
        LR = at_r("lb_rows", 72, [4, P])
        LMI = at_r("level_mask_int", 92, [P, LEVELS * 64], I32)
        LW = at_r("lb_work", 73, [P, 12, 4])
        PI_ = at_r("pos_int", 76, [1, S], I32)
        PF = at_r("pos_float", 80, [1, S])
        AN = at_r("angle", 84, [64, S])
        RK = at_r("turns", 88, [64, S])
        x_loaded = sems("x_loaded", 2)
        h_written = sem("h_written")
        pos_ready = sem("pos_ready")
        pos_done = sem("pos_done")
        lbT_done = sem("lbT_done")
        ready0 = sem("ready0")
        rope_step = sem("rope_step")
        lb_step = sem("lb_step")
        with nc.Block() as block:
            @block.sync
            def _(sp):
                sp.dma_start(CO[:, :], consts[:, :]).then_inc(small_loaded, 16)
                sp.dma_start(LMI[:, :], level_masks[:, :]).then_inc(small_loaded, 16)
                sp.dma_start(LR[:, :], lb_logits[:, :]).then_inc(small_loaded, 16)
                sp.dma_start(PI_[:, :], positions[:, :]).then_inc(small_loaded, 16)
                for t in range(TT):
                    if t >= 2:
                        sp.wait_ge(proj_done, t - 1)
                    sp.dma_start(XIN[t % 2][:, :], x[t * P:(t + 1) * P, :]).then_inc(x_loaded[t % 2], 16)

            @block.gpsimd
            def _(pool):
                nc.gpsimd.memset(WA[:, :], 0.0).then_inc(pool_step, 1)
                nc.gpsimd.memset(WX[:, :], 0.0).then_inc(pool_step, 1)

            @block.vector
            def _(dve):
                nc.vector.memset(ones[:, :], 1.0).then_inc(ready0, 1)
                nc.vector.memset(eps[:, :], EPS).then_inc(ready0, 1)
                nc.vector.memset(half_pi[:, :], math.pi / 2).then_inc(ready0, 1)
                dve.wait_ge(small_loaded, 64)
                nc.vector.tensor_copy(LM[:, :], LMI[:, :]).then_inc(dve_step, 1)
                nc.vector.tensor_copy(PF[:, :], PI_[:, :]).then_inc(pos_ready, 1)
                n = 0

                def step(ins):
                    nonlocal n
                    n += 1
                    ins.then_inc(lb_step, 1)
                    dve.wait_ge(lb_step, n)

                w = lambda i, a=0, b=2: LW[:, i, a:b]
                dve.wait_ge(lbT_done, 1)
                step(nc.vector.tensor_copy(w(0, 0, 4), ps[:, 7, 0:4]))
                step(nc.vector.tensor_tensor(w(1), w(0), w(0, 2, 4), ALU.max))
                step(nc.vector.tensor_tensor(w(2), w(0), w(1), ALU.subtract))
                step(nc.vector.tensor_tensor(w(2, 2, 4), w(0, 2, 4), w(1), ALU.subtract))
                dve.wait_ge(ready0, 4)
                step(nc.vector.tensor_tensor(w(4), w(3), w(3, 2, 4), ALU.add))
                step(nc.vector.reciprocal(w(4), w(4)))
                step(nc.vector.tensor_tensor(w(5), w(3), w(4), ALU.mult))
                step(nc.vector.tensor_tensor(w(5, 2, 4), w(3, 2, 4), w(4), ALU.mult))
                step(nc.vector.tensor_tensor(w(6), w(5), w(5), ALU.subtract))
                step(nc.vector.tensor_tensor(w(6, 2, 4), w(5), w(5, 2, 4), ALU.add))
                step(nc.vector.tensor_tensor(w(6, 2, 4), w(6, 2, 4), w(5), ALU.subtract))
                step(nc.vector.tensor_scalar(w(7, 0, 4), w(6, 0, 4), LN_FLOOR, None, ALU.max))
                step(nc.vector.tensor_scalar(w(8, 0, 4), w(6, 0, 4), LB_FLOOR, LN_SCALE, ALU.max, ALU.mult))
                step(nc.vector.tensor_scalar(w(8, 0, 4), w(8, 0, 4), LN_SCALE * LN_FLOOR, None, ALU.min))
                step(nc.vector.tensor_scalar(w(9, 0, 4), w(6, 0, 4), -1.0, 1.0, ALU.mult, ALU.add))
                step(nc.vector.tensor_scalar(w(9, 0, 4), w(9, 0, 4), 1e-18, None, ALU.max))
                nc.vector.tensor_scalar(w(10, 0, 4), w(6, 0, 4), LN_FLOOR, None, ALU.is_lt).then_inc(ready0, 1)
                dve.wait_ge(ready0, 6)
                step(nc.vector.tensor_scalar(w(8, 0, 4), w(8, 0, 4),
                                             -(math.log(LN_SCALE) + math.log(LN_FLOOR)), None, ALU.add))
                step(nc.vector.tensor_tensor(w(8, 0, 4), w(8, 0, 4), w(10, 0, 4), ALU.mult))
                step(nc.vector.tensor_tensor(lbt[:, 0, :], w(7, 0, 4), w(8, 0, 4), ALU.add))
                step(nc.vector.tensor_copy(lbt[:, 1, :], w(9, 0, 4)))
                step(nc.vector.tensor_tensor(lbt[:, 2, :], w(9, 0, 4), lbt[:, 0, :], ALU.subtract))
                r = 0

                def turn(ins):
                    nonlocal r
                    r += 1
                    ins.then_inc(rope_step, 1)
                    dve.wait_ge(rope_step, r)

                dve.wait_ge(pos_done, 1)
                turn(nc.vector.tensor_scalar(wide(AN[:, :]), pair(2, slice(0, 64)), CO[0:64, K_FREQ:K_FREQ + 1],
                                             None, ALU.mult))
                turn(nc.vector.tensor_scalar(RK[:, :], AN[:, :], 1.0 / (2 * math.pi), ROUND, ALU.mult, ALU.add))
                turn(nc.vector.tensor_scalar(RK[:, :], RK[:, :], ROUND, None, ALU.subtract))
                for part in (TWO_PI_1, TWO_PI_2, TWO_PI_3):
                    turn(nc.vector.scalar_tensor_tensor(AN[:, :], RK[:, :], -part, AN[:, :], ALU.mult, ALU.add))
                turn(nc.vector.tensor_scalar(AN[:, :], AN[:, :], PI_BELOW, -PI_BELOW, ALU.min, ALU.max))
                dve.wait_ge(ready0, 8)
                turn(nc.vector.tensor_scalar(RT[32:64, :], RT[32:64, :], CO[32:64, K_SIGN:K_SIGN + 1], None,
                                             ALU.mult))

            @block.scalar
            def _(act):
                act.wait_ge(lb_step, 4)
                nc.scalar.activation(LW[:, 3, :], LW[:, 2, :], ACT.Exp).then_inc(ready0, 1)
                act.wait_ge(ready0, 5)
                act.wait_ge(lb_step, 16)
                nc.scalar.activation(LW[:, 7:10, :], LW[:, 7:10, :], ACT.Ln).then_inc(ready0, 1)
                for t in range(TT):
                    act.wait_ge(proj_done, t + 1)
                    nc.scalar.activation(
                        h[:, :, t * P:(t + 1) * P],
                        pair(t % 2).rearrange("p b (k t) -> p (b k) t", t=P), ACT.Copy).then_inc(h_written, 1)
                act.wait_ge(rope_step, 7)
                nc.scalar.activation(RK[0:32, :], AN[0:32, :], ACT.Abs).then_inc(act_step, 1)
                act.wait_ge(act_step, 1)
                nc.scalar.activation(RT[0:32, :], RK[0:32, :], ACT.Sin, scale=-1.0,
                                     bias=half_pi[0:32, 0:1]).then_inc(ready0, 1)
                nc.scalar.activation(RT[32:64, :], AN[32:64, :], ACT.Sin).then_inc(ready0, 1)

            @block.tensor
            def _(pe):
                pe.wait_ge(small_loaded, 64)
                pe.wait_ge(ready0, 3)
                nc.tensor.transpose(ps[:, 7, 0:4], LR[:, :], ident[0:4, 0:4]).then_inc(lbT_done, 1)
                pe.wait_ge(pos_ready, 1)
                for half in range(2):
                    last = nc.tensor.matmul(ps[0:64, 4 + half, :], ones[0:1, 0:64],
                                            PF[0:1, half * HALF:(half + 1) * HALF], start=True, stop=True)
                last.then_inc(pos_done, 1)
                for t in range(TT):
                    pe.wait_ge(x_loaded[t % 2], 16 * (t // 2 + 1))
                    if t >= 2:
                        pe.wait_ge(h_written, t - 1)
                    for k in range(KT):
                        b = 2 * (t % 2) + k // 4
                        last = nc.tensor.transpose(ps[:, b, (k % 4) * P:(k % 4 + 1) * P],
                                                   XIN[t % 2][:, k * P:(k + 1) * P], ident)
                        if k == KT - 1:
                            last.then_inc(proj_done, 1)
        end_of_block()
        SQ = [at_r(f"sq{i}", 64 + 4 * i, [P, S]) for i in range(2)]
        ACC = at_r("acc", 72, [P, S])
        RS = at_r("rs", 76, [P, S])
        T = [at_r(f"t{i}", 80 + 4 * i, [P, S]) for i in range(2)]
        VR = at_r("vector_rows", 88, [V_ROWS, P])
        rowsT_done = sem("rowsT_done")
        vecs_ready = sem("vecs_ready")
        h_rows = h_dram.rearrange("(k p) s -> p k s", p=P)


        bF, bT, bB, bM, bK, bCUM, bQ, bG, bV = (
            at_r(n, 16 + 4 * i, [P, S]) for i, n in enumerate(
                ("f", "soft", "log_sig", "log_f", "key", "cum", "q", "g", "v")))
        VTOK = at_r("v_tok", 52, [P, NCH, P])
        QL = [at_r(f"q_level{i}", 56 + 2 * i, [P, NCH, 64]) for i in range(2)]
        SC = at_r("scores", 60, [P, NCH, 2, P])
        EC = at_r("exp_cum", 68, [P, S])
        ST = at_r("states", 72, [P, NCH, P])
        XP = at_r("x_padded", 76, [P, S + 4])
        XC = at_r("x_conv", 81, [P, S])
        GT = at_r("gate", 85, [P, S])
        TR = at_r("rec_gate", 89, [P, S])
        TI = at_r("in_gate", 93, [P, S])
        GE = at_r("gelu", 97, [P, S])
        TH = at_r("tanh_log_a", 56, [P, S])
        LE = [bF, bT]
        KL = [bB, bM]
        pair_vecs = sem("pair_vecs")
        lam_part = sem("lam_part")
        f_soft = sem("f_soft")
        b_ready = sem("b_ready")
        kx_ready = sem("kx_ready")
        key_ready = sem("key_ready")
        f_soft2 = sem("f_soft2")
        logf_ready = sem("logf_ready")
        cum_ready = sem("cum_ready")
        vT_done = sem("vT_done")
        vtok_ready = sem("vtok_ready")
        e_in = sem("e_in")
        e_ready = sem("e_ready")
        ql_ready = sem("ql_ready")
        level_done = sem("level_done")
        sc_zero = sem("sc_zero")
        sc_ready = sem("sc_ready")
        ec_ready = sem("ec_ready")
        kx2_ready = sem("kx2_ready")
        kdec_ready = sem("kdec_ready")
        ke_ready = sem("ke_ready")
        keT_done = sem("keT_done")
        ket_ready = sem("ket_ready")
        upd_done = sem("upd_done")
        st_zero = sem("st_zero")
        st_ready = sem("st_ready")
        qe_ready = sem("qe_ready")
        qk_ready = sem("qk_ready")
        diag_done = sem("diag_done")
        o_done = sem("o_done")
        od_ready = sem("od_ready")
        o_ready = sem("o_ready")
        osq_ready = sem("osq_ready")
        oms_done = sem("oms_done")
        orstd = sem("orstd")
        gelu_part = sem("gelu_part")
        conv_step = sem("conv_step")
        gates_done = sem("gates_done")
        gates_read = sem("gates_read")
        la_ready = sem("la_ready")
        decay_ready = sem("decay_ready")
        neg_ready = sem("neg_ready")
        root_ready = sem("root_ready")
        gelu_sq = sem("gelu_sq")
        gelu_in = sem("gelu_in")
        gelu_th = sem("gelu_th")
        silu_th = sem("silu_th")
        gate_loaded = sem("gate_loaded")

        def group_bd(l, pr):
            slots = [C_HF, C_HQ, C_HG, C_HI, C_X, C_GATE]

            def chunks(t, n=P):
                return t[:, :].rearrange("p (c t) -> p c t", t=n)

            def col(i):
                return pv[:, i:i + 1]

            with nc.Block() as block:
                @block.sync
                def _(sp):
                    for n, c in enumerate(slots):
                        if n < 2:
                            continue
                        src = w_in[bass.ds(l * D, D), bass.ds(pr * P + c, P)].rearrange("(k p) c -> p k c", p=P)
                        load_slot(sp, n, [(raw[n % 2][:, :].rearrange("p (k c) -> p k c", c=P), src)])
                    for n, (of_pair, of_latent) in ((6, (C_HF + P, C_CQ)), (7, (C_HQ + P, C_CQ + P))):
                        src = w_in[bass.ds(l * D, D), bass.ds(pr * (of_latent - of_pair) + of_pair, P)]
                        load_slot(sp, n, [(raw[n % 2][:, :].rearrange("p (k c) -> p k c", c=P),
                                           src.rearrange("(k p) c -> p k c", p=P))])
                    for W, src in ((WA, w_a), (WX, w_x)):
                        for j in range(2):
                            at = slice(64 * j, 64 * j + 64)
                            sp.dma_start(W[at, at], src[bass.ds((l * 4 + pr * 2 + j) * 64, 64), :])\
                                .then_inc(gate_loaded, 16)

                @block.gpsimd
                def _(pool):
                    nc.gpsimd.memset(SC[:, :, :, :], 0.0).then_inc(sc_zero, 1)
                    nc.gpsimd.memset(ST[:, :, :], 0.0).then_inc(st_zero, 1)
                    nc.gpsimd.memset(XP[:, 0:3], 0.0).then_inc(st_zero, 1)
                    for n in range(2, len(slots) + 2):
                        split_slot(pool, n, n // 2, n - 1)

                @block.tensor
                def _(pe):
                    def level(L):
                        pe.wait_ge(ql_ready, 2 * (L + 1))
                        if L >= 2:
                            pe.wait_ge(sc_ready, 2 * (L - 1))
                        for c in range(NCH):
                            for j in range(2):
                                rows = slice(64 * j, 64 * j + 64)
                                last = nc.tensor.matmul(ps[:, 4 + 2 * (L % 2) + j, c * 64:(c + 1) * 64],
                                                        KL[L % 2][rows, c * P:(c + 1) * P],
                                                        QL[L % 2][rows, c, :], start=True, stop=True)
                        last.then_inc(level_done, 1)

                    project_slot(pe, 0, 0, 0)
                    project_slot(pe, 1, 1, 1)
                    pe.wait_ge(bank_free[0], 1)
                    project_slot(pe, 2, 2, 0)
                    level(0)
                    level(1)
                    pe.wait_ge(bank_free[1], 1)
                    project_slot(pe, 3, 3, 1)
                    level(2)
                    level(3)
                    pe.wait_ge(bank_free[0], 2)
                    project_slot(pe, 4, 4, 0)
                    level(4)
                    level(5)
                    pe.wait_ge(bank_free[1], 2)
                    pe.wait_ge(sc_ready, 10)
                    for c in range(NCH):
                        last = nc.tensor.transpose(ps[:, 4 + c // 4, (c % 4) * P:(c % 4 + 1) * P],
                                                   bV[:, c * P:(c + 1) * P], ident)
                    last.then_inc(vT_done, 1)
                    project_slot(pe, 5, 5, 1)
                    pe.wait_ge(vtok_ready, 1)
                    level(6)
                    pe.wait_ge(gate_loaded, 64)
                    pe.wait_ge(conv_step, 4)
                    pe.wait_ge(bank_free[1], 3)
                    for p, W in ((0, WA), (1, WX)):
                        for half in range(2):
                            last = nc.tensor.matmul(ps[:, 2 * p + half, :], W[:, :],
                                                    XC[:, half * HALF:(half + 1) * HALF], start=True, stop=True)
                    last.then_inc(gates_done, 1)
                    pe.wait_ge(ke_ready, 1)
                    pe.wait_ge(sc_ready, 2 * (LEVELS - 1))
                    for c in range(NCH):
                        last = nc.tensor.transpose(ps[:, 6 + c // 4, (c % 4) * P:(c % 4 + 1) * P],
                                                   bB[:, c * P:(c + 1) * P], ident)
                    last.then_inc(keT_done, 1)
                    pe.wait_ge(ket_ready, 1)
                    pe.wait_ge(sc_ready, 2 * LEVELS)
                    for c in range(NCH):
                        last = nc.tensor.matmul(ps[:, 4 + c // 4, (c % 4) * P:(c % 4 + 1) * P],
                                                bM[:, c * P:(c + 1) * P], VTOK[:, c, :], start=True, stop=True)
                    last.then_inc(upd_done, 1)
                    pe.wait_ge(qk_ready, 1)
                    pe.wait_ge(gates_read, 2)
                    for half in range(2):
                        last = nc.tensor.matmul(ps[:, half, :], CO[:, K_HEADS:K_HEADS + P],
                                                bQ[:, half * HALF:(half + 1) * HALF], start=True, stop=True)
                    last.then_inc(diag_done, 1)
                    pe.wait_ge(qe_ready, 1)
                    for c in range(NCH):
                        out_c = ps[:, 6 + c // 4, (c % 4) * P:(c % 4 + 1) * P]
                        if c >= 1:
                            pe.wait_ge(st_ready, 2 * c)
                            nc.tensor.matmul(out_c, ST[:, c - 1, :], bT[:, c * P:(c + 1) * P],
                                             start=True, stop=False, skip_group_check=True)
                        for j in range(2):
                            rows = slice(64 * j, 64 * j + 64)
                            last = nc.tensor.matmul(ps[rows, 6 + c // 4, (c % 4) * P:(c % 4 + 1) * P],
                                                    VTOK[:, c, rows], SC[:, c, j, :],
                                                    start=(c == 0), stop=True, skip_group_check=True)
                    last.then_inc(o_done, 1)
                    pe.wait_ge(osq_ready, 1)
                    for half in range(2):
                        last = nc.tensor.matmul(ps[:, 2 + half, :], CO[:, K_HEADS:K_HEADS + P],
                                                bQ[:, half * HALF:(half + 1) * HALF], start=True, stop=True)
                    last.then_inc(oms_done, 1)

                @block.scalar
                def _(act):
                    exp_and_ln()
                    act.wait_ge(pair_vecs, 2)
                    nc.scalar.activation(col(W_T0), col(V_LAM), ACT.Abs).then_inc(lam_part, 1)
                    act.wait_ge(lam_part, 1)
                    nc.scalar.activation(col(W_T0), col(W_T0), ACT.Exp, scale=-1.0).then_inc(lam_part, 1)
                    act.wait_ge(bank_free[0], 1)
                    nc.scalar.activation(bT[:, :], bF[:, :], ACT.Abs).then_inc(f_soft, 1)
                    act.wait_ge(f_soft, 1)
                    nc.scalar.activation(bT[:, :], bT[:, :], ACT.Exp, scale=-1.0).then_inc(f_soft, 1)
                    act.wait_ge(f_soft, 2)
                    nc.scalar.activation(bT[:, :], bT[:, :], ACT.Ln, bias=1.0).then_inc(f_soft, 1)
                    act.wait_ge(proj_done, 2)
                    nc.scalar.activation(wide(bQ[:, :]), pair(1), ACT.Copy).then_inc(bank_free[1], 1)
                    act.wait_ge(b_ready, 1)
                    nc.scalar.activation(bT[:, :], bB[:, :], ACT.Abs, bias=col(W_LBD)).then_inc(f_soft2, 1)
                    act.wait_ge(f_soft2, 1)
                    nc.scalar.activation(bT[:, :], bT[:, :], ACT.Exp, scale=-1.0).then_inc(f_soft2, 1)
                    act.wait_ge(f_soft2, 2)
                    nc.scalar.activation(bT[:, :], bT[:, :], ACT.Ln, bias=1.0).then_inc(f_soft2, 1)
                    act.wait_ge(kx_ready, 1)
                    nc.scalar.activation(bK[:, :], bF[:, :], ACT.Exp, bias=col(W_LBC)).then_inc(key_ready, 1)
                    act.wait_ge(cum_ready, NCH)
                    nc.scalar.activation(EC[:, :], bCUM[:, :], ACT.Exp).then_inc(ec_ready, 1)
                    for L in range(LEVELS):
                        act.wait_ge(e_in, 2 * (L + 1))
                        nc.scalar.activation(LE[L % 2][:, :], LE[L % 2][:, :], ACT.Exp).then_inc(e_ready, 1)
                        if L == 1:
                            act.wait_ge(proj_done, 3)
                            nc.scalar.activation(wide(bG[:, :]), pair(0), ACT.Copy).then_inc(bank_free[0], 1)
                        if L == 3:
                            act.wait_ge(proj_done, 4)
                            nc.scalar.activation(wide(bV[:, :]), pair(1), ACT.Copy).then_inc(bank_free[1], 1)
                    act.wait_ge(vT_done, 1)
                    nc.scalar.activation(VTOK[:, :, :].rearrange("p (b c) t -> p b (c t)", b=2), pair(2),
                                         ACT.Copy).then_inc(vtok_ready, 1)
                    act.wait_ge(proj_done, 6)
                    nc.scalar.activation(wide(GT[:, :]), pair(1), ACT.Copy).then_inc(bank_free[1], 1)
                    act.wait_ge(kx2_ready, 1)
                    nc.scalar.activation(bF[:, :], bF[:, :], ACT.Exp).then_inc(kdec_ready, 1)
                    act.wait_ge(bank_free[1], 3)
                    nc.scalar.activation(GE[:, :], GT[:, :], ACT.Square).then_inc(gelu_sq, 1)
                    act.wait_ge(gates_done, 1)
                    nc.scalar.activation(wide(TR[:, :]), pair(0), ACT.Sigmoid, bias=col(V_BA)).then_inc(gates_read, 1)
                    nc.scalar.activation(wide(TI[:, :]), pair(1), ACT.Sigmoid, bias=col(V_BX)).then_inc(gates_read, 1)
                    nc.scalar.activation(XP[:, 0:S], bG[:, :], ACT.Sigmoid).then_inc(silu_th, 1)
                    act.wait_ge(keT_done, 1)
                    nc.scalar.activation(wide(bM[:, :]), pair(3), ACT.Copy).then_inc(ket_ready, 1)
                    act.wait_ge(gelu_in, 1)
                    nc.scalar.activation(GE[:, :], GE[:, :], ACT.Sigmoid, scale=2 * math.sqrt(2 / math.pi))\
                        .then_inc(gelu_th, 1)
                    act.wait_ge(la_ready, 1)
                    act.wait_ge(level_done, LEVELS)
                    nc.scalar.activation(TH[:, :], TR[:, :], ACT.Tanh).then_inc(decay_ready, 1)
                    exp_and_ln()
                    act.wait_ge(dve_step, 1)
                    nc.scalar.activation(XP[:, 0:S], TR[:, :], ACT.Exp).then_inc(decay_ready, 1)
                    act.wait_ge(o_ready, 1)
                    nc.scalar.activation(bQ[:, :], bCUM[:, :], ACT.Square).then_inc(osq_ready, 1)
                    act.wait_ge(oms_done, 1)
                    nc.scalar.activation(wide(bF[:, :]), pair(1), ACT.Ln, scale=1.0 / HD, bias=eps[:, 0:1])\
                        .then_inc(orstd, 1)
                    act.wait_ge(orstd, 1)
                    nc.scalar.activation(bF[:, :], bF[:, :], ACT.Exp, scale=-0.5).then_inc(orstd, 1)
                    act.wait_ge(neg_ready, 1)
                    nc.scalar.activation(TH[:, :], TH[:, :], ACT.Sqrt).then_inc(root_ready, 1)

                @block.vector
                def _(dve):
                    nc.vector.tensor_copy(pv[:, 0:PAIR_ROWS], vecs[:, bass.ds(pr * PAIR_ROWS, PAIR_ROWS)])\
                        .then_inc(pair_vecs, 1)
                    nc.vector.tensor_copy(pv[:, W_LBA:W_LBA + 3].rearrange("p (i o) -> p i o", o=1),
                                          lbt[:, :, bass.ds(l * 2 + pr, 1)]).then_inc(pair_vecs, 1)
                    dve.wait_ge(pair_vecs, 2)
                    n = 2

                    def step(ins):
                        nonlocal n
                        n += 1
                        ins.then_inc(pair_vecs, 1)
                        dve.wait_ge(pair_vecs, n)

                    nc_ts = nc.vector.tensor_scalar
                    step(nc_ts(col(W_T1), col(V_LAM), -1.0, 0.0, ALU.mult, ALU.max))
                    dve.wait_ge(lam_part, 2)
                    step(nc_ts(col(W_T2), col(W_T0), 2.0, None, ALU.add))
                    step(nc.vector.reciprocal(col(W_T2), col(W_T2)))
                    step(nc.vector.tensor_tensor(col(W_T2), col(W_T2), col(W_T0), ALU.mult))
                    step(nc.vector.tensor_tensor(col(W_T3), col(W_T2), col(W_T2), ALU.mult))
                    step(nc_ts(col(W_T4), col(W_T3), 1.0 / 17, 1.0 / 15, ALU.mult, ALU.add))
                    for term in (13, 11, 9, 7, 5, 3, 1):
                        step(nc_ts(col(W_T4), col(W_T4), col(W_T3), 1.0 / term, ALU.mult, ALU.add))
                    step(nc.vector.tensor_tensor(col(W_T4), col(W_T4), col(W_T2), ALU.mult))
                    step(nc.vector.scalar_tensor_tensor(col(W_T4), col(W_T4), 2.0, col(W_T1), ALU.mult, ALU.add))
                    step(nc_ts(col(W_C1), col(W_T4), -LRU_C, None, ALU.mult))
                    dve.wait_ge(proj_done, 1)
                    nc.vector.tensor_copy(wide(bF[:, :]), pair(0)).then_inc(bank_free[0], 1)
                    dve.wait_ge(bank_free[0], 1)
                    dve.wait_ge(f_soft, 3)
                    nc.vector.scalar_tensor_tensor(bB[:, :], bF[:, :], 0.0, bT[:, :], ALU.min, ALU.subtract)\
                        .then_inc(b_ready, 1)
                    dve.wait_ge(b_ready, 1)
                    nc.vector.tensor_tensor(bF[:, :], bB[:, :], bF[:, :], ALU.subtract).then_inc(kx_ready, 1)
                    nc.vector.tensor_scalar(bM[:, :], bB[:, :], col(W_LBC), col(W_LBA), ALU.add, ALU.max)\
                        .then_inc(logf_ready, 1)
                    dve.wait_ge(logf_ready, 1)
                    dve.wait_ge(f_soft2, 3)
                    nc.vector.tensor_tensor(bM[:, :], bM[:, :], bT[:, :], ALU.add).then_inc(logf_ready, 1)
                    dve.wait_ge(logf_ready, 2)
                    for c in range(NCH):
                        at = slice(c * P, (c + 1) * P)
                        nc.vector.tensor_tensor_scan(bCUM[:, at], ones[:, :], bM[:, at], 0.0, ALU.mult, ALU.add)\
                            .then_inc(cum_ready, 1)
                    dve.wait_ge(cum_ready, NCH)

                    def level_in(L):
                        n = 64 >> L
                        cum = bCUM[:, :].rearrange("p (b s n) -> p b s n", s=2, n=n)
                        e = LE[L % 2][:, :].rearrange("p (b s n) -> p b s n", s=2, n=n)
                        mid = cum[:, :, 0, n - 1:n].broadcast_to([P, S // (2 * n), n])
                        if L < 2:
                            dve.wait_ge(key_ready, 1)
                        else:
                            dve.wait_ge(ql_ready, 2 * (L - 1))
                        nc.vector.tensor_tensor(e[:, :, 0, :], mid, cum[:, :, 0, :], ALU.subtract).then_inc(e_in, 1)
                        nc.vector.tensor_tensor(e[:, :, 1, :], cum[:, :, 1, :], mid, ALU.subtract).then_inc(e_in, 1)

                    def level_keys(L):
                        n = 64 >> L
                        dve.wait_ge(e_ready, L + 1)
                        if L == 0:
                            dve.wait_ge(bank_free[1], 1)
                        if L >= 2:
                            dve.wait_ge(level_done, L - 1)
                        e = LE[L % 2][:, :].rearrange("p (b s n) -> p b s n", s=2, n=n)
                        q = bQ[:, :].rearrange("p (b s n) -> p b s n", s=2, n=n)
                        nc.vector.tensor_tensor(QL[L % 2][:, :, :].rearrange("p c (b n) -> p (c b) n", n=n),
                                                q[:, :, 1, :], e[:, :, 1, :], ALU.mult).then_inc(ql_ready, 1)
                        nc.vector.tensor_tensor(KL[L % 2][:, :], bK[:, :], LE[L % 2][:, :], ALU.mult)\
                            .then_inc(ql_ready, 1)

                    def level_scores(L):
                        n = 64 >> L
                        dve.wait_ge(level_done, L + 1)
                        if L == 0:
                            dve.wait_ge(sc_zero, 1)
                        else:
                            dve.wait_ge(sc_ready, 2 * L)
                        m = LM[:, L * 64:(L + 1) * 64].rearrange("p (o b n) -> p o b n", o=1, n=n)
                        for j in range(2):
                            to = SC[:, :, j, :].rearrange("p c (b s n) -> p c b s n", s=2, n=n)[:, :, :, 1, :]
                            of = ps[:, 4 + 2 * (L % 2) + j, :].rearrange("p (c b n) -> p c b n", c=NCH, n=n)
                            nc.vector.copy_predicated(to, m.broadcast_to([P, NCH, 64 // n, n]), of)\
                                .then_inc(sc_ready, 1)

                    level_in(0)
                    level_in(1)
                    for L in range(LEVELS):
                        level_keys(L)
                        if L >= 1:
                            level_scores(L - 1)
                        if L + 2 < LEVELS:
                            level_in(L + 2)
                    cum = chunks(bCUM)
                    dve.wait_ge(e_ready, LEVELS)
                    dve.wait_ge(ql_ready, 2 * LEVELS)
                    nc.vector.tensor_tensor(chunks(bF), cum[:, :, P - 1:P].broadcast_to([P, NCH, P]), cum,
                                            ALU.subtract).then_inc(kx2_ready, 1)
                    dve.wait_ge(proj_done, 5)
                    dve.wait_ge(st_zero, 2)
                    nc.vector.tensor_copy(wide(XP[:, 3:3 + S]), pair(0)).then_inc(bank_free[0], 1)
                    dve.wait_ge(bank_free[0], 3)
                    nc.vector.tensor_scalar(XC[:, :], XP[:, 0:S], col(V_TAP), col(V_CB), ALU.mult, ALU.add)\
                        .then_inc(conv_step, 1)
                    for k in range(1, CONV):
                        dve.wait_ge(conv_step, k)
                        nc.vector.scalar_tensor_tensor(XC[:, :], XP[:, k:k + S], col(V_TAP + k), XC[:, :],
                                                       ALU.mult, ALU.add).then_inc(conv_step, 1)
                    dve.wait_ge(ec_ready, 1)
                    nc.vector.tensor_tensor(bT[:, :], bQ[:, :], EC[:, :], ALU.mult).then_inc(qe_ready, 1)
                    dve.wait_ge(qe_ready, 1)
                    nc.vector.tensor_tensor(bQ[:, :], bQ[:, :], bK[:, :], ALU.mult).then_inc(qk_ready, 1)
                    dve.wait_ge(kdec_ready, 1)
                    dve.wait_ge(level_done, LEVELS)
                    nc.vector.tensor_tensor(bB[:, :], bK[:, :], bF[:, :], ALU.mult).then_inc(ke_ready, 1)
                    level_scores(LEVELS - 1)
                    dve.wait_ge(gelu_sq, 1)
                    nc.vector.tensor_scalar(GE[:, :], GE[:, :], 0.044715, 1.0, ALU.mult, ALU.add)\
                        .then_inc(gelu_part, 1)
                    dve.wait_ge(gelu_part, 1)
                    nc.vector.tensor_tensor(GE[:, :], GE[:, :], GT[:, :], ALU.mult).then_inc(gelu_in, 1)
                    dve.wait_ge(silu_th, 1)
                    nc.vector.tensor_tensor(bG[:, :], XP[:, 0:S], bG[:, :], ALU.mult).then_inc(dve_step, 1)
                    dve.wait_ge(gates_read, 2)
                    nc.vector.tensor_scalar(TR[:, :], TR[:, :], col(W_C1), None, ALU.mult).then_inc(la_ready, 1)
                    nc.vector.tensor_tensor(TI[:, :], TI[:, :], XC[:, :], ALU.mult).then_inc(dve_step, 1)
                    dve.wait_ge(upd_done, 1)
                    dve.wait_ge(st_zero, 1)
                    for c in range(NCH):
                        if c >= 1:
                            dve.wait_ge(st_ready, 2 * c)
                        for j in range(2):
                            r = slice(64 * j, 64 * j + 64)
                            upd = ps[r, 4 + c // 4, (c % 4) * P + 64 * j:(c % 4) * P + 64 * j + 64]
                            if c == 0:
                                ins = nc.vector.tensor_copy(ST[r, 0, r], upd)
                            else:
                                ins = nc.vector.scalar_tensor_tensor(ST[r, c, r], ST[r, c - 1, r],
                                                                     EC[r, (c + 1) * P - 1:(c + 1) * P], upd,
                                                                     ALU.mult, ALU.add)
                            ins.then_inc(st_ready, 1)
                    dve.wait_ge(diag_done, 1)
                    nc.vector.tensor_tensor(wide(bV[:, :]), pair(0), wide(bV[:, :]), ALU.mult).then_inc(od_ready, 1)
                    dve.wait_ge(gelu_th, 1)
                    nc.vector.tensor_tensor(GE[:, :], GE[:, :], GT[:, :], ALU.mult).then_inc(dve_step, 1)
                    dve.wait_ge(decay_ready, 2)
                    nc.vector.tensor_tensor(bK[:, :], XP[:, 0:S], XP[:, 0:S], ALU.mult).then_inc(dve_step, 1)
                    dve.wait_ge(dve_step, 4)
                    nc.vector.scalar_tensor_tensor(bK[:, :], bK[:, :], 1.0, TH[:, :], ALU.add, ALU.mult)\
                        .then_inc(dve_step, 1)
                    dve.wait_ge(dve_step, 5)
                    nc.vector.tensor_scalar(TH[:, :], bK[:, :], -1.0, 0.0, ALU.mult, ALU.max).then_inc(neg_ready, 1)
                    dve.wait_ge(od_ready, 1)
                    dve.wait_ge(o_done, 1)
                    nc.vector.tensor_tensor(wide(bCUM[:, :]), pair(3), wide(bV[:, :]), ALU.add).then_inc(o_ready, 1)
                    dve.wait_ge(root_ready, 1)
                    nc.vector.tensor_tensor(TI[:, :], TI[:, :], TH[:, :], ALU.mult).then_inc(dve_step, 1)
                    dve.wait_ge(orstd, 2)
                    nc.vector.scalar_tensor_tensor(bCUM[:, :], bCUM[:, :], col(V_HG), bF[:, :], ALU.mult, ALU.mult)\
                        .then_inc(dve_step, 1)
                    dve.wait_ge(dve_step, 7)
                    nc.vector.tensor_tensor(YD[:, bass.ds(pr, 1), :].rearrange("p o s -> p (o s)"),
                                            bCUM[:, :], bG[:, :], ALU.mult).then_inc(dve_step, 1)
                    nc.vector.tensor_tensor_scan(bB[:, :], XP[:, 0:S], TI[:, :], 0.0, ALU.mult, ALU.add)\
                        .then_inc(dve_step, 1)
                    dve.wait_ge(dve_step, 9)
                    nc.vector.tensor_tensor(YB[:, bass.ds(pr, 1), :].rearrange("p o s -> p (o s)"),
                                            bB[:, :], GE[:, :], ALU.mult).then_inc(dve_step, 1)

        SBQ = at_r("sb_q", 32, [P, PAIRS, S])
        SBK = at_r("sb_k", 40, [P, PAIRS, S])
        SBV = at_r("sb_v", 48, [P, PAIRS, TT, P])
        CQH = at_r("c_q_hi", 56, [P, 2, S], F32R)
        CQL = at_r("c_q_lo", 64, [P, 2, S], F32R)
        CKH = at_r("c_kv_hi", 72, [P, S], F32R)
        CKL = at_r("c_kv_lo", 76, [P, S], F32R)
        CQ = at_r("c_q", 80, [P, 2, S])
        CKV = at_r("c_kv", 88, [P, S])
        LSQ = [at_r("latent_sq0", 92, [P, S]), at_r("latent_sq1", 96, [P, S])]
        LRS = at_r("latent_rs", 100, [P, S])
        VF = [at_r(f"v_feature{i}", 16 + 4 * i, [P, S]) for i in range(2)]
        RTMP = at_r("rope_tmp", 24, [P, S])
        KH = at_u("mla_k", 0, [P, 4, S])
        QH = at_u("mla_q", 16, [P, 4, S])
        MV = at_u("mla_v", 32, [P, PAIRS, TT, P])
        lat_read = sem("lat_read")
        lat_sq = sem("lat_sq")
        lat_sum = sem("lat_sum")
        lat_rs = sem("lat_rs")
        lat_t = sem("lat_t")
        lat_hi = sem("lat_hi")
        lat_lo = sem("lat_lo")
        rope_part = sem("rope_part")
        key_rope = sem("key_rope")

        LAT_JOBS = ["cq0", "cq1", "ckv", "kr", "sbq0", "sbk0", "sum_q", "sbv0", "sum_kv", "sbq1", "vT_s0", "sbk1",
                    "sbv1", "qn0", "kn0", "qp0", "vv0", "vT_s1", "qn1", "kn1", "qp1", "vv1", "vT_m0", "vT_m1"]
        JOB = {name: j for j, name in enumerate(LAT_JOBS)}
        LAT_SLOTS = ["cq0", "cq1", "ckv", "kr", "sbq0", "sbk0", "sbv0", "sbq1", "sbk1", "sbv1", "mla0", "mla1"]
        LAT_SLOTS += ["out0", "out1"]
        SLOT = {name: n for n, name in enumerate(LAT_SLOTS)}
        SLOT_END = {name: JOB.get(name, JOB["vv0"] if name == "mla0" else JOB["vv1"]) for name in LAT_SLOTS[:-2]}
        MLA_N, MLA_PE, MLA_K, MLA_V = 0, P, 512, 640

        def latents(l):
            def mla_parts(l, n, pr):
                uq = raw[n % 2][:, 0:512].rearrange("p (k c) -> p k c", k=2)
                ukv = raw[n % 2][:, 512:768].rearrange("p (t j c) -> p t j c", t=2, j=2)
                parts = []
                for j in range(2):
                    c = (2 * pr + j) * (NOPE + ROPE)

                    def q_cols(a, width):
                        return w_uq[bass.ds(l * Q_LORA, Q_LORA), a:a + width].rearrange("(k p) c -> p k c", p=P)

                    parts += [(uq[:, :, 64 * j:64 * j + 64], q_cols(c, 64)),
                              (uq[:, :, P + 32 * j:P + 32 * j + 32], q_cols(c + 64, 32)),
                              (uq[:, :, P + 64 + 32 * j:P + 80 + 32 * j], q_cols(c + 80, 16)),
                              (uq[:, :, P + 80 + 32 * j:P + 96 + 32 * j], q_cols(c + 64, 16))]
                    for t in range(2):
                        c2 = (2 * pr + j) * (NOPE + HD) + 64 * t
                        parts.append((ukv[:, t, j, :], w_ukv[bass.ds(l * KV_LORA, KV_LORA), c2:c2 + 64]))
                return parts

            with nc.Block() as block:
                @block.sync
                def _(sp):
                    cols = {"cq0": C_CQ, "cq1": C_CQ + P, "ckv": C_CKV, "sbq0": C_SBQ, "sbq1": C_SBQ + P,
                            "sbk0": C_SBK, "sbk1": C_SBK + P, "sbv0": C_SBV, "sbv1": C_SBV + P}
                    for n, name in enumerate(LAT_SLOTS):
                        to = raw[n % 2][:, :].rearrange("p (k c) -> p k c", c=P)

                        def w_cols(c, width):
                            return w_in[bass.ds(l * D, D), c:c + width].rearrange("(k p) c -> p k c", p=P)

                        if n < 2:
                            continue
                        if name[:3] == "out":
                            m = int(name[-1])
                            parts = [(to, w_out[bass.ds(l * D, D), m * P:(m + 1) * P]
                                      .rearrange("(k p) c -> p k c", p=P))]
                        elif name in cols:
                            parts = [(to, w_cols(cols[name], P))]
                        elif name == "kr":
                            parts = []
                            for r in range(2):
                                parts += [(to[:, :, 64 * r:64 * r + 32], w_cols(C_ROPE, 32)),
                                          (to[:, :, 64 * r + 32:64 * r + 48], w_cols(C_ROPE + 16, 16)),
                                          (to[:, :, 64 * r + 48:64 * r + 64], w_cols(C_ROPE, 16))]
                        else:
                            parts = mla_parts(l, n, int(name[-1]))
                        load_slot(sp, n, parts)

                @block.gpsimd
                def _(pool):
                    dmas = [0, 0]
                    for n, name in enumerate(LAT_SLOTS):
                        if n < 2:
                            continue
                        dmas[n % 2] += 6 if name == "kr" else 12 if name.startswith("mla") else 1
                        jobs = SLOT_END[LAT_SLOTS[n - 2]] + 1
                        split_slot(pool, n, dmas[n % 2], jobs, 768 if name.startswith("mla") else 1024)

                @block.tensor
                def _(pe):
                    for j, name in enumerate(LAT_JOBS):
                        p = j % 4
                        if j >= 4:
                            pe.wait_ge(bank_free[p], j // 4)
                        if name in SLOT:
                            project_slot(pe, SLOT[name], j, p)
                        elif name in ("sum_q", "sum_kv"):
                            q = name == "sum_q"
                            pe.wait_ge(lat_sq, 2 if q else 3)
                            for half in range(2):
                                at = slice(half * HALF, (half + 1) * HALF)
                                for k in range(2 if q else 1):
                                    last = nc.tensor.matmul(ps[:, 2 * p + half, :], ones[:, :], LSQ[k][:, at],
                                                            start=(k == 0), stop=(k == 1 or not q))
                            last.then_inc(proj_done, 1)
                        elif name[:2] == "vT":
                            src = VF[int(name[-1])]
                            pe.wait_ge(bank_free[JOB[("sbv" if name[3] == "s" else "vv") + name[-1]] % 4],
                                       JOB[("sbv" if name[3] == "s" else "vv") + name[-1]] // 4 + 1)
                            for c in range(TT):
                                last = nc.tensor.transpose(ps[:, 2 * p + c // 4, (c % 4) * P:(c % 4 + 1) * P],
                                                           src[:, c * P:(c + 1) * P], ident)
                            last.then_inc(proj_done, 1)
                        else:
                            kind, pr = name[:2], int(name[-1])
                            n = SLOT[f"mla{pr}"]
                            pe.wait_ge(slot_split, n - 1)
                            pe.wait_ge(lat_lo, 3)
                            off = {"qn": MLA_N, "qp": MLA_PE, "kn": MLA_K, "vv": MLA_V}[kind]
                            if kind in ("qn", "qp"):
                                last = product(pe, 2 * p, slot_lhs(n, off, 256),
                                               lambda k: (CQH[:, k, :], CQL[:, k, :]), 2)
                            else:
                                last = product(pe, 2 * p, slot_lhs(n, off), lambda k: (CKH[:, :], CKL[:, :]), 1)
                            last.then_inc(proj_done, 1)

                @block.scalar
                def _(act):
                    def read(name, to):
                        j = JOB[name]
                        act.wait_ge(proj_done, j + 1)
                        return nc.scalar.activation(to, pair(j % 4), ACT.Copy)

                    def done(name, ins):
                        ins.then_inc(bank_free[JOB[name] % 4], 1)

                    exp_and_ln()
                    done("cq0", read("cq0", wide(CQ[:, 0, :])))
                    done("cq1", read("cq1", wide(CQ[:, 1, :])))
                    act.wait_ge(bank_free[0], 1)
                    act.wait_ge(bank_free[1], 1)
                    nc.scalar.activation(LSQ[0][:, :], CQ[:, 0, :], ACT.Square).then_inc(lat_sq, 1)
                    nc.scalar.activation(LSQ[1][:, :], CQ[:, 1, :], ACT.Square).then_inc(lat_sq, 1)
                    done("ckv", read("ckv", wide(CKV[:, :])))
                    done("sbq0", read("sbq0", wide(SBQ[:, 0, :])))
                    done("sbk0", read("sbk0", wide(SBK[:, 0, :])))
                    act.wait_ge(proj_done, JOB["sum_q"] + 1)
                    nc.scalar.activation(wide(LRS[:, :]), pair(JOB["sum_q"] % 4), ACT.Ln, scale=1.0 / Q_LORA,
                                         bias=eps[:, 0:1]).then_inc(bank_free[JOB["sum_q"] % 4], 1)
                    act.wait_ge(bank_free[2], 2)
                    nc.scalar.activation(LRS[:, :], LRS[:, :], ACT.Exp, scale=-0.5).then_inc(lat_rs, 1)
                    nc.scalar.activation(LSQ[0][:, :], CKV[:, :], ACT.Square).then_inc(lat_sq, 1)
                    done("sbv0", read("sbv0", wide(VF[0][:, :])))
                    for k in range(2):
                        act.wait_ge(lat_t, k + 1)
                        nc.scalar.activation(CQH[:, k, :], CQ[:, k, :], ACT.Copy).then_inc(lat_hi, 1)
                    act.wait_ge(proj_done, JOB["sum_kv"] + 1)
                    nc.scalar.activation(wide(LRS[:, :]), pair(JOB["sum_kv"] % 4), ACT.Ln, scale=1.0 / KV_LORA,
                                         bias=eps[:, 0:1]).then_inc(bank_free[JOB["sum_kv"] % 4], 1)
                    act.wait_ge(bank_free[0], 3)
                    nc.scalar.activation(LRS[:, :], LRS[:, :], ACT.Exp, scale=-0.5).then_inc(lat_rs, 1)
                    done("sbq1", read("sbq1", wide(SBQ[:, 1, :])))
                    act.wait_ge(lat_t, 3)
                    nc.scalar.activation(CKH[:, :], CKV[:, :], ACT.Copy).then_inc(lat_hi, 1)
                    done("vT_s0", read("vT_s0", SBV[:, 0, :, :].rearrange("p (b c) t -> p b (c t)", b=2)))
                    done("sbk1", read("sbk1", wide(SBK[:, 1, :])))
                    done("sbv1", read("sbv1", wide(VF[1][:, :])))
                    for pr in range(PAIRS):
                        for name, to in ((f"qn{pr}", QH), (f"kn{pr}", KH)):
                            j = JOB[name]
                            act.wait_ge(proj_done, j + 1)
                            nc.scalar.activation(wide(to[0:64, 2 * pr, :]), pair(j % 4, slice(0, 64)), ACT.Copy)\
                                .then_inc(lat_read, 1)
                            act.wait_ge(lat_read, 2 * pr + (1 if to is QH else 2))
                            nc.scalar.activation(wide(to[0:64, 2 * pr + 1, :]), pair(j % 4, slice(64, P)), ACT.Copy)\
                                .then_inc(bank_free[j % 4], 1)
                        done(f"vv{pr}", read(f"vv{pr}", wide(VF[pr][:, :])))
                        if pr == 0:
                            done("vT_s1", read("vT_s1", SBV[:, 1, :, :].rearrange("p (b c) t -> p b (c t)", b=2)))
                    for pr in range(PAIRS):
                        done(f"vT_m{pr}", read(f"vT_m{pr}", MV[:, pr, :, :].rearrange(
                            "p (b c) t -> p b (c t)", b=2)))
                    act.wait_ge(key_rope, 1)
                    for hd in range(4):
                        nc.scalar.activation(KH[64:96, hd, :], RT[64:96, :], ACT.Copy).then_inc(lat_read, 1)

                @block.vector
                def _(dve):
                    dve.wait_ge(proj_done, JOB["kr"] + 1)
                    cos, sin = RT[0:32, :], RT[32:64, :]
                    nc.vector.tensor_tensor(wide(RT[64:96, :]), pair(3, slice(0, 32)), wide(cos), ALU.mult)\
                        .then_inc(rope_part, 1)
                    nc.vector.tensor_tensor(wide(RTMP[64:96, :]), pair(3, slice(32, 64)), wide(sin), ALU.mult)\
                        .then_inc(bank_free[3], 1)
                    dve.wait_ge(rope_part, 1)
                    dve.wait_ge(bank_free[3], 1)
                    nc.vector.tensor_tensor(RT[64:96, :], RT[64:96, :], RTMP[64:96, :], ALU.add).then_inc(key_rope, 1)
                    dve.wait_ge(lat_rs, 1)
                    for k in range(2):
                        nc.vector.scalar_tensor_tensor(CQ[:, k, :], CQ[:, k, :], vecs[:, V_QN + k:V_QN + k + 1],
                                                       LRS[:, :], ALU.mult, ALU.mult).then_inc(lat_t, 1)
                    for k in range(2):
                        dve.wait_ge(lat_hi, k + 1)
                        nc.vector.tensor_tensor(CQL[:, k, :], CQ[:, k, :], CQH[:, k, :].bitcast(F32),
                                                ALU.subtract).then_inc(lat_lo, 1)
                    dve.wait_ge(lat_rs, 2)
                    nc.vector.scalar_tensor_tensor(CKV[:, :], CKV[:, :], vecs[:, V_KVN:V_KVN + 1],
                                                   LRS[:, :], ALU.mult, ALU.mult).then_inc(lat_t, 1)
                    dve.wait_ge(lat_hi, 3)
                    nc.vector.tensor_tensor(CKL[:, :], CKV[:, :], CKH[:, :].bitcast(F32),
                                            ALU.subtract).then_inc(lat_lo, 1)
                    n = 1
                    for pr in range(PAIRS):
                        j = JOB[f"qp{pr}"]
                        dve.wait_ge(proj_done, j + 1)
                        for i in range(2):
                            if pr + i:
                                dve.wait_ge(rope_part, n)
                            else:
                                dve.wait_ge(key_rope, 1)
                            nc.vector.tensor_tensor(wide(QH[64:96, 2 * pr + i, :]), pair(j % 4, slice(32 * i, 32 * i + 32)),
                                                    wide(cos), ALU.mult).then_inc(rope_part, 1)
                            ins = nc.vector.tensor_tensor(wide(RTMP[64:96, :]),
                                                          pair(j % 4, slice(64 + 32 * i, 96 + 32 * i)), wide(sin),
                                                          ALU.mult)
                            if i == 0:
                                ins.then_inc(rope_part, 1)
                                n += 2
                                dve.wait_ge(rope_part, n)
                            else:
                                ins.then_inc(bank_free[j % 4], 1)
                                n += 1
                                dve.wait_ge(rope_part, n)
                                dve.wait_ge(bank_free[j % 4], j // 4 + 1)
                            nc.vector.tensor_tensor(QH[64:96, 2 * pr + i, :], QH[64:96, 2 * pr + i, :],
                                                    RTMP[64:96, :], ALU.add).then_inc(rope_part, 1)
                            n += 1

        SQP = at_u("sb_q_pair", 40, [P, S])
        SKP = at_u("sb_k_pair", 44, [P, S])
        QHP = [at_u(f"mla_q_pair{i}", 48 + 4 * i, [P, S]) for i in range(2)]
        KHP = [at_u(f"mla_k_pair{i}", 56 + 4 * i, [P, S]) for i in range(2)]
        ZS = [at_r(f"sb_z{i}", 56 + 4 * i, [P, S]) for i in range(2)]
        TA = [at_r(f"sb_soft{i}", 64 + 4 * i, [P, S]) for i in range(2)]
        RW = [at_r(f"sb_weight{i}", 72 + 4 * i, [P, S]) for i in range(2)]
        PM = [at_r(f"mla_prob{i}", 80 + 4 * i, [P, S]) for i in range(2)]
        PTS = [at_r(f"sb_weight_t{i}", 88 + 4 * i, [P, TT, P]) for i in range(2)]
        PTM = [at_r(f"mla_prob_t{i}", 96 + 4 * i, [P, TT, P]) for i in range(2)]
        copied = sem("copied")
        sb_scored = sem("sb_scored")
        mla_scored = sem("mla_scored")
        zs_ready = sem("zs_ready")
        soft_step = sem("soft_step")
        soft_ready = sem("soft_ready")
        sp_ready = sem("sp_ready")
        cum_sp_ready = sem("cum_sp_ready")
        lw_ready = sem("lw_ready")
        w_ready = sem("w_ready")
        m_masked = sem("m_masked")
        nm_part = sem("nm_part")
        nm_ready = sem("nm_ready")
        pm_ready = sem("pm_ready")
        unit_done = sem("unit_done")
        unit_read = sems("unit_read", 3)
        pv_done = sem("pv_done")
        pv_read = sem("pv_read")
        rinv = sem("rinv")

        JOBS = 2 * TT

        def keys_of(i):
            return i // 2 + 1

        UNITS = []
        for s_ in range(JOBS + 2):
            for kind, i in (("m", s_ - 1), ("s", s_ - 2)):
                if 0 <= i < JOBS:
                    UNITS += [(kind, i, b) for b in range(0, keys_of(i), 4)]

        def units_of(kind, i):
            return [u for u, unit in enumerate(UNITS) if unit[:2] == (kind, i)]

        def zs_count(i):
            return sum(2 if keys_of(j) > 1 else 1 for j in range(i + 1))

        def group_ac(pr):
            with nc.Block() as block:
                @block.tensor
                def _(pe):
                    def transposes(kind, i, src):
                        for u in units_of(kind, i):
                            if u >= 3:
                                pe.wait_ge(unit_read[u % 3], u // 3)
                            b0 = UNITS[u][2]
                            for b in range(b0, min(b0 + 4, keys_of(i))):
                                last = nc.tensor.transpose(ps[:, u % 3, (b - b0) * P:(b - b0 + 1) * P],
                                                           src[:, b * P:(b + 1) * P], ident)
                            last.then_inc(unit_done, 1)

                    def values(kind, i, pt, v, col):
                        for u in units_of(kind, i):
                            pe.wait_ge(unit_read[u % 3], u // 3 + 1)
                        for b in range(keys_of(i)):
                            last = nc.tensor.matmul(ps[:, 3, col:col + HD], pt[:, b, :],
                                                    v[:, bass.ds(pr, 1), b, (i % 2) * HD:(i % 2 + 1) * HD]
                                                    .rearrange("p o c -> p (o c)"),
                                                    start=(b == 0), stop=(b == keys_of(i) - 1))
                        return last

                    pe.wait_ge(copied, 6)
                    for s in range(JOBS + 3):
                        n = keys_of(s) * P
                        q_at = slice((s // 2) * P, (s // 2 + 1) * P)
                        if s < JOBS:
                            rows = slice(64 * (s % 2), 64 * (s % 2) + 64)
                            if s >= 1:
                                pe.wait_ge(zs_ready, zs_count(s - 1))
                            for a in range(0, n, HALF):
                                e = min(n, a + HALF)
                                last = nc.tensor.matmul(ps[:, 4 + a // HALF, 0:e - a], SQP[rows, q_at],
                                                        SKP[rows, a:e], start=True, stop=True)
                            last.then_inc(sb_scored, 1)
                        if s >= 3:
                            pe.wait_ge(pv_read, s - 2)
                        if 2 <= s < JOBS + 2:
                            last = values("m", s - 2, PTM[s % 2], MV, 0)
                            if s == 2:
                                last.then_inc(pv_done, 1)
                        if 1 <= s <= JOBS:
                            pe.wait_ge(pm_ready, s)
                            transposes("m", s - 1, PM[(s - 1) % 2])
                        if s < JOBS:
                            if s >= 1:
                                pe.wait_ge(pm_ready, s)
                            for a in range(0, n, HALF):
                                e = min(n, a + HALF)
                                last = nc.tensor.matmul(ps[:, 6 + a // HALF, 0:e - a], QHP[s % 2][0:96, q_at],
                                                        KHP[s % 2][0:96, a:e], start=True, stop=True)
                            last.then_inc(mla_scored, 1)
                        if s >= 3:
                            values("s", s - 3, PTS[(s - 3) % 2], SBV, HD).then_inc(pv_done, 1)
                        if 2 <= s < JOBS + 2:
                            pe.wait_ge(w_ready, s - 1)
                            transposes("s", s - 2, RW[s % 2])

                @block.vector
                def _(dve):
                    nc.vector.tensor_copy(SQP[:, :], SBQ[:, bass.ds(pr, 1), :].rearrange("p o s -> p (o s)"))\
                        .then_inc(copied, 1)
                    nc.vector.tensor_copy(SKP[:, :], SBK[:, bass.ds(pr, 1), :].rearrange("p o s -> p (o s)"))\
                        .then_inc(copied, 1)
                    for s in range(JOBS + 4):
                        if s >= 3:
                            dve.wait_ge(pv_done, s - 2)
                            if s - 3 < JOBS:
                                i = s - 3
                                nc.vector.reciprocal(RSUM[:, i % 4, 1:2], RSUM[:, i % 4, 0:1]).then_inc(rinv, 1)
                                dve.wait_ge(rinv, i + 1)
                                ins = nc.vector.tensor_scalar(
                                    YA[:, i // 2, bass.ds(pr * P + (i % 2) * HD, HD)], ps[:, 3, 0:HD],
                                    RSUM[:, i % 4, 1:2], None, ALU.mult)
                            if s >= 4:
                                if s - 3 < JOBS:
                                    ins.then_inc(dve_step, 1)
                                i = s - 4
                                ins = nc.vector.tensor_copy(YC[:, i // 2, bass.ds(pr * P + (i % 2) * HD, HD)],
                                                            ps[:, 3, HD:2 * HD])
                            ins.then_inc(pv_read, 1)
                        if s < JOBS:
                            n = keys_of(s) * P
                            z, sc = ZS[s % 2], pair(2).rearrange("p b n -> p (b n)")
                            dve.wait_ge(sb_scored, s + 1)
                            if s >= 2:
                                dve.wait_ge(lw_ready, s - 1)
                            if n > P:
                                nc.vector.tensor_scalar(z[:, 0:n - P], sc[:, 0:n - P], SB_SCALE, None, ALU.mult)\
                                    .then_inc(zs_ready, 1)
                            nc.vector.scalar_tensor_tensor(z[:, n - P:n], sc[:, n - P:n], SB_SCALE,
                                                           CO[:, K_NEGS:K_NEGS + P], ALU.mult, ALU.add)\
                                .then_inc(zs_ready, 1)
                        if 1 <= s <= JOBS:
                            i = s - 1
                            n = keys_of(i) * P
                            t, z, r = TA[i % 2], ZS[i % 2], RW[i % 2]
                            dve.wait_ge(soft_ready, i + 1)
                            nc.vector.scalar_tensor_tensor(t[:, 0:n], z[:, 0:n], 0.0, t[:, 0:n], ALU.max, ALU.add)\
                                .then_inc(sp_ready, 1)
                            dve.wait_ge(sp_ready, i + 1)
                            if i >= 2:
                                dve.wait_ge(unit_done, units_of("s", i - 2)[-1] + 1)
                            nc.vector.tensor_tensor_scan(r[:, 0:n][:, ::-1], ones[:, 0:1].broadcast_to([P, n]), t[:, 0:n][:, ::-1], 0.0,
                                                         ALU.mult, ALU.add).then_inc(cum_sp_ready, 1)
                        if s < JOBS:
                            n = keys_of(s) * P
                            sc = pair(3).rearrange("p b n -> p (b n)")
                            dve.wait_ge(mla_scored, s + 1)
                            nc.vector.tensor_tensor(sc[:, n - P:n], sc[:, n - P:n], CO[:, K_NEGC:K_NEGC + P],
                                                    ALU.add).then_inc(m_masked, 1)
                            dve.wait_ge(m_masked, s + 1)
                            if s >= 2:
                                dve.wait_ge(pm_ready, s - 1)
                            nc.vector.tensor_reduce(NM[:, s % 2, 0:1], sc[:, 0:n], AX.X, ALU.max, negate=True)\
                                .then_inc(nm_part, 1)
                            dve.wait_ge(nm_part, s + 1)
                            nc.vector.tensor_scalar(NM[:, s % 2, 1:2], NM[:, s % 2, 0:1], MLA_SCALE, None, ALU.mult)\
                                .then_inc(nm_ready, 1)
                        if 2 <= s < JOBS + 2:
                            i = s - 2
                            if i >= 2:
                                dve.wait_ge(pv_done, i)
                            for u in units_of("s", i):
                                dve.wait_ge(unit_done, u + 1)
                                b0 = UNITS[u][2]
                                b1 = min(b0 + 4, keys_of(i))
                                nc.vector.tensor_copy(PTS[i % 2][:, b0:b1, :].rearrange("p b c -> p (b c)"),
                                                      ps[:, u % 3, 0:(b1 - b0) * P]).then_inc(unit_read[u % 3], 1)

                @block.gpsimd
                def _(pool):
                    for i in range(2):
                        nc.gpsimd.tensor_copy(KHP[i][0:96, :], KH[0:96, bass.ds(pr * 2 + i, 1), :]
                                              .rearrange("p o s -> p (o s)")).then_inc(copied, 1)
                    for i in range(JOBS):
                        n = keys_of(i) * P
                        pool.wait_ge(cum_sp_ready, i + 1)
                        nc.gpsimd.tensor_tensor(RW[i % 2][:, 0:n], ZS[i % 2][:, 0:n], RW[i % 2][:, 0:n],
                                                ALU.subtract).then_inc(lw_ready, 1)

                @block.scalar
                def _(act):
                    exp_and_ln()
                    for i in range(2):
                        nc.scalar.activation(QHP[i][0:96, :], QH[0:96, bass.ds(pr * 2 + i, 1), :]
                                             .rearrange("p o s -> p (o s)"), ACT.Copy).then_inc(copied, 1)
                    for s in range(JOBS + 2):
                        if s >= 2:
                            i = s - 2
                            r = RW[i % 2][:, 0:keys_of(i) * P]
                            act.wait_ge(lw_ready, i + 1)
                            nc.scalar.activation(r, r, ACT.Exp).then_inc(w_ready, 1)
                        if s < JOBS:
                            n = keys_of(s) * P
                            t = TA[s % 2][:, 0:n]
                            act.wait_ge(zs_ready, zs_count(s))
                            if s >= 2:
                                act.wait_ge(cum_sp_ready, s - 1)
                            nc.scalar.activation(t, ZS[s % 2][:, 0:n], ACT.Abs).then_inc(soft_step, 1)
                            act.wait_ge(soft_step, 2 * s + 1)
                            nc.scalar.activation(t, t, ACT.Exp, scale=-1.0).then_inc(soft_step, 1)
                            act.wait_ge(soft_step, 2 * s + 2)
                            nc.scalar.activation(t, t, ACT.Ln, bias=1.0).then_inc(soft_ready, 1)
                        if 1 <= s <= JOBS:
                            i = s - 1
                            if i >= 2:
                                act.wait_ge(pv_done, i - 1)
                            for u in units_of("m", i):
                                act.wait_ge(unit_done, u + 1)
                                b0 = UNITS[u][2]
                                b1 = min(b0 + 4, keys_of(i))
                                nc.scalar.activation(PTM[i % 2][:, b0:b1, :].rearrange("p b c -> p (b c)"),
                                                     ps[:, u % 3, 0:(b1 - b0) * P], ACT.Copy)\
                                    .then_inc(unit_read[u % 3], 1)
                        if s < JOBS:
                            act.wait_ge(nm_ready, s + 1)
                            if s >= 2:
                                act.wait_ge(unit_done, units_of("m", s - 2)[-1] + 1)
                            if s >= 4:
                                act.wait_ge(rinv, s - 3)
                            nc.scalar.activation(PM[s % 2][:, 0:n], pair(3).rearrange("p b n -> p (b n)")[:, 0:n],
                                                 ACT.Exp, scale=MLA_SCALE, bias=NM[:, s % 2, 1:2],
                                                 accum_out=RSUM[:, s % 4, 0:1]).then_inc(pm_ready, 1)

        HIDH = [at_r(f"hidden_hi{i}", 8 * i, [P, 2, S], F32R) for i in range(2)]
        HIDL = [at_r(f"hidden_lo{i}", 16 + 8 * i, [P, 2, S], F32R) for i in range(2)]
        SG = [at_r(f"silu{i}", 64 + 4 * i, [P, S]) for i in range(2)]
        HT = [at_r(f"hidden{i}", 72 + 4 * i, [P, S]) for i in range(2)]
        DRAW = [at_r(f"down_raw{i}", 80 + 4 * i, [P, D]) for i in range(2)]
        DHI = [at_r(f"down_hi{i}", 88 + 4 * i, [P, D], F32R) for i in range(2)]
        DLO = [at_r(f"down_lo{i}", 96 + 4 * i, [P, D], F32R) for i in range(2)]
        GSQ = at_r("group_squares", 80, [P, 2 * TT, GROUP_W])
        h_loaded = sem("h_loaded")
        group_sq = sem("group_sq")
        group_part = sem("group_part")
        group_rstd = sem("group_rstd")
        group_scaled = sem("group_scaled")
        mix_hi = sem("mix_hi")
        mix_lo = sem("mix_lo")
        mixD_lo = sem("mixD_lo")
        b_sq = sem("b_sq")
        b_rstd = sem("b_rstd")
        b_t = sem("b_t")
        down_loaded = sems("down_loaded", 2)
        down_hi = sem("down_hi")
        down_split = sem("down_split")
        down_done = sem("down_done")
        hid_hi = sem("hid_hi")
        hid_lo = sem("hid_lo")

        J_B, J_OUT, J_NORM, J_FFN = 4, 5, 13, 14
        CHUNKS = FFN // 256
        AC_TILES = [(YA, 0, 0, 0), (YA, 0, 1, 1), (YC, 1, 0, 4), (YC, 1, 1, 5)]

        def ffn_pair(q):
            return (J_FFN + q) % 4

        def ffn_used(i, q):
            if isinstance(i, int) and i == 0:
                return (J_FFN + q) // 4
            return 3 * (i - 1) + (J_FFN + 4 + q) // 4

        def down_read(i):
            return bank_free[ffn_pair(3)], 3 * i + (J_FFN + 11) // 4 + 2

        def output_ffn(l):
            def load_gate_up(sp, i, q):
                src = (w_gate, w_up)[q % 2]
                to = raw[q % 2][:, :].rearrange("p (k c) -> p k c", c=P)
                sp.wait_ge(slot_split, 4 * i + (KT + q - 3))
                sp.dma_start(to, src[bass.ds(l * D, D), bass.ds(i * 256 + (q // 2) * P, P)]
                             .rearrange("(k p) c -> p k c", p=P)).then_inc(raw_loaded[q % 2], 16)

            def load_down(sp, i, t):
                sp.dma_start(DRAW[t][:, :], w_down[bass.ds(l * FFN + i * 256 + t * P, P), :])\
                    .then_inc(down_loaded[t], 16)

            def split_gate_up(pool, i, q):
                pool.wait_ge(raw_loaded[q % 2], 32 * i + 16 * (KT // 2 + q // 2))
                pool.wait_ge(proj_done, 4 * i + (J_FFN + q - 1))
                nc.gpsimd.tensor_tensor(whi[q % 2][:, :], raw[q % 2][:, :],
                                        ones[:, 0:1].broadcast_to([P, 1024]), ALU.mult).then_inc(hi_split, 1)
                pool.wait_ge(hi_split, 4 * i + (KT + q - 1))
                nc.gpsimd.tensor_tensor(wlo[q % 2][:, :], raw[q % 2][:, :], whi[q % 2][:, :].bitcast(F32),
                                        ALU.subtract).then_inc(slot_split, 1)

            def split_down(pool, i, t):
                pool.wait_ge(down_loaded[t], 16 * i + 16)
                pool.wait_ge(*down_read(i - 1))
                nc.gpsimd.tensor_tensor(DHI[t][:, :], DRAW[t][:, :],
                                        ones[:, 0:1].broadcast_to([P, 1024]), ALU.mult).then_inc(down_hi, 1)
                pool.wait_ge(down_hi, 2 * i + (t + 1))
                nc.gpsimd.tensor_tensor(DLO[t][:, :], DRAW[t][:, :], DHI[t][:, :].bitcast(F32),
                                        ALU.subtract).then_inc(down_split, 1)

            def pe_gate_up(pe, i, q, before_k=None):
                p = ffn_pair(q)
                pe.wait_ge(bank_free[p], ffn_used(i, q))
                pe.wait_ge(slot_split, 4 * i + (KT + q - 1))
                last = product(pe, 2 * p, slot_lhs(q), u_rhs, KT, before_k)
                last.then_inc(proj_done, 1)

            def pe_down(pe, i, b, last_chunk=0):
                pe.wait_ge(down_split, 2 * i + 2)
                pe.wait_ge(hid_lo, 2 * i + 2)
                for m in range(KT):
                    p = ffn_pair(4 + m)
                    pe.wait_ge(bank_free[p], ffn_used(i + 1, 4 + m) - last_chunk)
                    hi, lo = (whi, wlo) if last_chunk else (DHI, DLO)
                    last = product(pe, 2 * p, lambda k: (hi[k][:, m * P:(m + 1) * P], lo[k][:, m * P:(m + 1) * P]),
                                   lambda k: (HIDH[b][:, k, :], HIDL[b][:, k, :]), 2)
                    last.then_inc(down_done, 1)

            def act_chunk(act, i, b, first=False):
                for t in range(2):
                    pg, pu = ffn_pair(2 * t), ffn_pair(2 * t + 1)
                    act.wait_ge(proj_done, 4 * i + (J_FFN + 2 * t + 1))
                    if not first:
                        act.wait_ge(hid_lo, 2 * i + (t - 1))
                    nc.scalar.activation(wide(SG[t][:, :]), pair(pg), ACT.Silu).then_inc(bank_free[pg], 1)
                    act.wait_ge(bank_free[pu], ffn_used(i, 2 * t + 1) + 1)
                    if not first:
                        act.wait_ge(*down_read(i - 2))
                    nc.scalar.activation(HIDH[b][:, t, :], HT[t][:, :], ACT.Copy).then_inc(hid_hi, 1)

            def dve_chunk(dve, i, b, first=False):
                for t in range(2):
                    pg, pu = ffn_pair(2 * t), ffn_pair(2 * t + 1)
                    dve.wait_ge(proj_done, 4 * i + (J_FFN + 2 * t + 2))
                    dve.wait_ge(bank_free[pg], ffn_used(i, 2 * t) + 1)
                    if not first:
                        dve.wait_ge(hid_lo, 2 * i + (t - 1))
                    nc.vector.tensor_tensor(wide(HT[t][:, :]), pair(pu), wide(SG[t][:, :]), ALU.mult)\
                        .then_inc(bank_free[pu], 1)
                    dve.wait_ge(hid_hi, 2 * i + (t + 1))
                    nc.vector.tensor_tensor(HIDL[b][:, t, :], HT[t][:, :], HIDH[b][:, t, :].bitcast(F32),
                                            ALU.subtract).then_inc(hid_lo, 1)

            def dve_down(dve, i):
                for m in range(KT):
                    p = ffn_pair(4 + m)
                    dve.wait_ge(down_done, KT * i + (m + 1))
                    nc.vector.tensor_tensor(wide(h[:, m, :]), pair(p), wide(h[:, m, :]), ALU.add)\
                        .then_inc(bank_free[p], 1)

            with nc.Block() as block:
                @block.sync
                def _(sp):
                    for k in range(KT):
                        sp.dma_start(h[:, k, :], h_dram[k * P:(k + 1) * P, :]).then_inc(h_loaded, 16)
                    for m in range(2, KT):
                        src = w_out[bass.ds(l * D, D), m * P:(m + 1) * P].rearrange("(k p) c -> p k c", p=P)
                        load_slot(sp, m, [(raw[m % 2][:, :].rearrange("p (k c) -> p k c", c=P), src)])
                    for q in range(4):
                        load_gate_up(sp, 0, q)
                    for k in range(2):
                        sp.wait_ge(ulo_done[k], KT // 2)
                    with sp.Fori(0, (CHUNKS - 1) // 2) as r:
                        for b in range(2):
                            i = 2 * r + (b + 1)
                            load_gate_up(sp, i, 0)
                            load_gate_up(sp, i, 1)
                            load_down(sp, i - 1, 0)
                            load_down(sp, i - 1, 1)
                            load_gate_up(sp, i, 2)
                            load_gate_up(sp, i, 3)
                    sp.wait_ge(down_split, 2 * (CHUNKS - 1))
                    for t in range(2):
                        load_down(sp, CHUNKS - 1, t)

                @block.gpsimd
                def _(pool):
                    for t in range(PAIRS):
                        pool.wait_ge(mix_hi, t + 1)
                        nc.gpsimd.tensor_tensor(ulo[:, 6 + t, :], YD[:, t, :], uhi[:, 6 + t, :].bitcast(F32),
                                                ALU.subtract).then_inc(mixD_lo, 1)
                    for m in range(2, KT):
                        split_slot(pool, m, m // 2, J_OUT + m - 1)
                    split_gate_up(pool, 0, 0)
                    split_gate_up(pool, 0, 1)
                    norm_lo_pool(pool, T, ulo, uhi)
                    split_gate_up(pool, 0, 2)
                    split_gate_up(pool, 0, 3)
                    with pool.Fori(0, (CHUNKS - 1) // 2) as r:
                        for b in range(2):
                            i = 2 * r + (b + 1)
                            split_gate_up(pool, i, 0)
                            split_gate_up(pool, i, 1)
                            split_down(pool, i - 1, 0)
                            split_down(pool, i - 1, 1)
                            split_gate_up(pool, i, 2)
                            split_gate_up(pool, i, 3)
                    for t in range(2):
                        pool.wait_ge(down_loaded[t], 16 * CHUNKS)
                        pool.wait_ge(proj_done, J_FFN + 4 * (CHUNKS - 1) + 3 + t)
                        nc.gpsimd.tensor_tensor(whi[t][:, :], DRAW[t][:, :], ones[:, 0:1].broadcast_to([P, 1024]),
                                                ALU.mult).then_inc(down_hi, 1)
                        pool.wait_ge(down_hi, 2 * (CHUNKS - 1) + t + 1)
                        nc.gpsimd.tensor_tensor(wlo[t][:, :], DRAW[t][:, :], whi[t][:, :].bitcast(F32),
                                                ALU.subtract).then_inc(down_split, 1)

                @block.tensor
                def _(pe):
                    for j, (y, g, half, _) in enumerate(AC_TILES):
                        pe.wait_ge(group_scaled, g + 1)
                        for t in range(TT):
                            last = nc.tensor.transpose(ps[:, 2 * j + t // 4, (t % 4) * P:(t % 4 + 1) * P],
                                                       y[:, t, half * P:(half + 1) * P], ident)
                        last.then_inc(proj_done, 1)
                    pe.wait_ge(b_sq, 2)
                    pe.wait_ge(bank_free[0], 1)
                    for half in range(2):
                        for t in range(2):
                            last = nc.tensor.matmul(ps[:, half, :], ones[:, :], SQ[t][:, half * HALF:(half + 1) * HALF],
                                                    start=(t == 0), stop=(t == 1))
                    last.then_inc(proj_done, 1)
                    for p in range(1, 4):
                        pe.wait_ge(bank_free[p], 1)
                    pe.wait_ge(mixD_lo, 2)
                    pe.wait_ge(mix_lo, 2)
                    for m in range(KT):
                        j = J_OUT + m
                        pe.wait_ge(bank_free[j % 4], j // 4)
                        project_slot(pe, m, j, j % 4)
                    pe.wait_ge(bank_free[J_NORM % 4], J_NORM // 4)
                    norm_sum_pe(pe, ACC, J_NORM % 4, proj_done)
                    pe_gate_up(pe, 0, 0, u_ready(pe))
                    for q in range(1, 4):
                        pe_gate_up(pe, 0, q)
                    with pe.Fori(0, (CHUNKS - 1) // 2) as r:
                        for b in range(2):
                            i = 2 * r + (b + 1)
                            for q in range(4):
                                pe_gate_up(pe, i, q)
                            pe_down(pe, i - 1, b)
                    pe_down(pe, CHUNKS - 1, (CHUNKS - 1) % 2, last_chunk=1)

                @block.scalar
                def _(act):
                    exp_and_ln()
                    for t in range(PAIRS):
                        nc.scalar.activation(uhi[:, 6 + t, :], YD[:, t, :], ACT.Copy).then_inc(mix_hi, 1)
                    for g, y in enumerate((YA, YC)):
                        for t in range(TT):
                            nc.scalar.activation(GSQ[:, g * TT + t, :], y[:, t, :], ACT.Square,
                                                 accum_out=GMS[:, g, t:t + 1]).then_inc(group_sq, 1)
                    act.wait_ge(group_sq, 2 * TT)
                    nc.scalar.activation(GMS[:, :, :], GMS[:, :, :], ACT.Ln, scale=1.0 / GROUP_W,
                                         bias=eps[:, 0:1]).then_inc(group_part, 1)
                    act.wait_ge(group_part, 1)
                    nc.scalar.activation(GMS[:, :, :], GMS[:, :, :], ACT.Exp, scale=-0.5).then_inc(group_rstd, 1)
                    for t in range(PAIRS):
                        nc.scalar.activation(SQ[t][:, :], YB[:, t, :], ACT.Square).then_inc(b_sq, 1)
                    for j, (_, g, half, tile) in enumerate(AC_TILES):
                        gain = vecs[:, V_GN + 4 * g + half:V_GN + 4 * g + half + 1]
                        act.wait_ge(proj_done, j + 1)
                        nc.scalar.activation(wide(uhi[:, tile, :]), pair(j), ACT.Copy, scale=gain).then_inc(mix_hi, 1)
                    act.wait_ge(proj_done, J_B + 1)
                    nc.scalar.activation(wide(RS[:, :]), pair(0), ACT.Ln, scale=1.0 / GROUP_W,
                                         bias=eps[:, 0:1]).then_inc(bank_free[0], 1)
                    act.wait_ge(bank_free[0], 2)
                    nc.scalar.activation(RS[:, :], RS[:, :], ACT.Exp, scale=-0.5).then_inc(b_rstd, 1)
                    for t in range(PAIRS):
                        act.wait_ge(b_t, t + 1)
                        nc.scalar.activation(uhi[:, 2 + t, :], T[t][:, :], ACT.Copy).then_inc(mix_hi, 1)

                    def h_final(act, k):
                        j = J_OUT + k
                        act.wait_ge(bank_free[j % 4], j // 4 + 1)

                    norm_act(act, SQ, RS, uhi, T, J_NORM % 4, h_final, (proj_done, J_NORM + 1),
                             (bank_free[J_NORM % 4], J_NORM // 4 + 1))
                    act_chunk(act, 0, 0, first=True)
                    with act.Fori(0, (CHUNKS - 1) // 2) as r:
                        for b in range(2):
                            act_chunk(act, 2 * r + (b + 1), (b + 1) % 2)

                @block.vector
                def _(dve):
                    dve.wait_ge(group_rstd, 1)
                    for g, y in enumerate((YA, YC)):
                        nc.vector.tensor_tensor(
                            y[:, :, :], y[:, :, :],
                            GMS[:, g, :].rearrange("p (t o) -> p t o", o=1).broadcast_to([P, TT, GROUP_W]),
                            ALU.mult).then_inc(group_scaled, 1)
                    for j, (_, g, half, tile) in enumerate(AC_TILES):
                        gain = vecs[:, V_GN + 4 * g + half:V_GN + 4 * g + half + 1]
                        dve.wait_ge(mix_hi, PAIRS + j + 1)
                        nc.vector.scalar_tensor_tensor(wide(ulo[:, tile, :]), pair(j), gain,
                                                       wide(uhi[:, tile, :].bitcast(F32)),
                                                       ALU.mult, ALU.subtract).then_inc(bank_free[j], 1)
                    dve.wait_ge(b_rstd, 1)
                    for t in range(PAIRS):
                        nc.vector.scalar_tensor_tensor(T[t][:, :], YB[:, t, :], vecs[:, V_GN + 2 + t:V_GN + 3 + t],
                                                       RS[:, :], ALU.mult, ALU.mult).then_inc(b_t, 1)
                    for t in range(PAIRS):
                        dve.wait_ge(mix_hi, PAIRS + 4 + t + 1)
                        nc.vector.tensor_tensor(ulo[:, 2 + t, :], T[t][:, :], uhi[:, 2 + t, :].bitcast(F32),
                                                ALU.subtract).then_inc(mix_lo, 1)
                    dve.wait_ge(h_loaded, 16 * KT)
                    for m in range(KT):
                        j = J_OUT + m
                        dve.wait_ge(proj_done, j + 1)
                        nc.vector.tensor_tensor(wide(h[:, m, :]), pair(j % 4), wide(h[:, m, :]), ALU.add)\
                            .then_inc(bank_free[j % 4], 1)
                    norm_sum_dve(dve, SQ, ACC)
                    norm_scale_dve(dve, RS, T, ulo, uhi, lambda k: vecs[:, V_LN2 + k:V_LN2 + k + 1])
                    dve_chunk(dve, 0, 0, first=True)
                    with dve.Fori(0, (CHUNKS - 1) // 2) as r:
                        for b in range(2):
                            i = 2 * r + (b + 1)
                            dve_chunk(dve, i, (b + 1) % 2)
                            dve_down(dve, i - 1)
                    dve_down(dve, CHUNKS - 1)

        OT = at_u("out_tokens", 0, [P, TT, D])
        FR = at_r("final_rows", 88, [KT, P])
        fg_done = sem("fg_done")
        fg_ready = sem("fg_ready")
        out_ready = sem("out_ready")

        def final():
            with nc.Block() as block:
                @block.sync
                def _(sp):
                    sp.dma_start(FR[:, :], final_g[:, :]).then_inc(small_loaded, 16)
                    for k in range(KT):
                        sp.wait_ge(out_ready, k + 1)
                        sp.dma_start(out.rearrange("(t p) f -> p t f", p=P)[:, :, k * P:(k + 1) * P],
                                     OT[:, :, k * P:(k + 1) * P]).then_inc(stored, 16)
                    sp.wait_ge(stored, 16 * KT)

                @block.tensor
                def _(pe):
                    pe.wait_ge(small_loaded, 16)
                    nc.tensor.transpose(ps[:, 0, 0:KT], FR[:, :], ident[0:KT, 0:KT]).then_inc(fg_done, 1)
                    norm_sum_pe(pe, ACC, 3, ms_done)
                    pe.wait_ge(fg_ready, 1)
                    for k in range(KT):
                        pe.wait_ge(t_ready, k + 1)
                        if k >= 3:
                            pe.wait_ge(out_ready, k - 2)
                        for t in range(TT):
                            last = nc.tensor.transpose(ps[:, 2 * (k % 3) + t // 4, (t % 4) * P:(t % 4 + 1) * P],
                                                       T[k % 2][:, t * P:(t + 1) * P], ident)
                        last.then_inc(proj_done, 1)

                @block.scalar
                def _(act):
                    norm_act(act, SQ, RS, None, T, 3, lambda e, k: None, (ms_done, 1), (rstd_part, 1))
                    for k in range(KT):
                        act.wait_ge(proj_done, k + 1)
                        nc.scalar.activation(OT[:, :, k * P:(k + 1) * P],
                                             pair(k % 3).rearrange("p b (t c) -> p (b t) c", c=P), ACT.Copy)\
                            .then_inc(out_ready, 1)

                @block.vector
                def _(dve):
                    dve.wait_ge(fg_done, 1)
                    nc.vector.tensor_copy(vecs[:, 0:KT], ps[:, 0, 0:KT]).then_inc(fg_ready, 1)
                    norm_sum_dve(dve, SQ, ACC)
                    dve.wait_ge(rstd_ready, 1)
                    dve.wait_ge(fg_ready, 1)
                    for k in range(KT):
                        if k >= 2:
                            dve.wait_ge(proj_done, k - 1)
                        nc.vector.scalar_tensor_tensor(T[k % 2][:, :], h[:, k, :], vecs[:, k:k + 1], RS[:, :],
                                                       ALU.mult, ALU.mult).then_inc(t_ready, 1)

        with nc.Fori(0, DEPTH) as l:
            with nc.Block() as block:
                @block.sync
                def _(sp):
                    for key, first, count, to in VEC_ROWS:
                        src = vec_in[key]
                        per = src.shape[0] // DEPTH
                        sp.dma_start(VR[to:to + count, :], src[bass.ds(l * per + first, count), :])\
                            .then_inc(small_loaded, 16)
                    for n, c in enumerate((C_HF, C_HQ)):
                        src = w_in[bass.ds(l * D, D), c:c + P].rearrange("(k p) c -> p k c", p=P)
                        sp.dma_start(raw[n][:, :].rearrange("p (k c) -> p k c", c=P), src).then_inc(raw_loaded[n], 16)
                    sp.dma_start(h_rows, h[:, :, :]).then_inc(h_moved, 16)
                    sp.wait_ge(h_moved, 16)

                @block.tensor
                def _(pe):
                    norm_sum_pe(pe, ACC, 3, ms_done)
                    pe.wait_ge(small_loaded, 16 * len(VEC_ROWS))
                    nc.tensor.transpose(ps[:, 0, 0:V_ROWS], VR[:, :], ident[0:V_ROWS, 0:V_ROWS])\
                        .then_inc(rowsT_done, 1)

                @block.scalar
                def _(act):
                    norm_act(act, SQ, RS, uhi, T, 3, lambda e, k: None, (ms_done, 1), (rstd_part, 1))

                @block.vector
                def _(dve):
                    norm_sum_dve(dve, SQ, ACC)
                    dve.wait_ge(rowsT_done, 1)
                    nc.vector.tensor_copy(vecs[:, :], ps[:, 0, 0:V_ROWS]).then_inc(vecs_ready, 1)
                    dve.wait_ge(vecs_ready, 1)
                    norm_scale_dve(dve, RS, T, ulo, uhi, lambda k: vecs[:, V_LN1 + k:V_LN1 + k + 1])

                @block.gpsimd
                def _(pool):
                    for n in range(2):
                        split_slot(pool, n + 2, 1, 0)
                    norm_lo_pool(pool, T, ulo, uhi)
            end_of_block()

            with nc.Fori(0, PAIRS) as pr:
                group_bd(l, pr)
                end_of_block()

            latents(l)
            end_of_block()

            with nc.Fori(0, PAIRS) as pr:
                group_ac(pr)
                end_of_block()

            output_ffn(l)
            end_of_block()

        final()


def constants():
    c = np.zeros((P, K_N), np.float32)
    q, k = np.arange(P)[:, None], np.arange(P)[None, :]
    c[:, K_ID:K_ID + P] = q == k
    c[:, K_STRICT:K_STRICT + P] = k < q
    c[:, K_NEGS:K_NEGS + P] = np.where(k < q, 0.0, MASKED)
    c[:, K_NEGC:K_NEGC + P] = np.where(k <= q, 0.0, MASKED)
    c[:, K_HEADS:K_HEADS + P] = q // HD == k // HD
    half = ROPE // 2
    freq = np.float32(10000.0) ** (-np.arange(half, dtype=np.float32) / np.float32(half))
    c[0:64, K_FREQ] = freq[np.arange(64) % 32 % half]
    c[32:64, K_SIGN] = np.where(np.arange(32) < half, -1.0, 1.0)
    lm = np.zeros((P, LEVELS, 64), np.int32)
    for L in range(LEVELS):
        n = 64 >> L
        for j in range(64):
            block = j // n
            lm[block * 2 * n:block * 2 * n + n, L, j] = 1
    return c, lm.reshape(P, LEVELS * 64)


def kernel(x, positions, ln1_g, w_in, mla_q_norm_g, mla_w_uq, mla_kv_norm_g, mla_w_ukv,
           lru_conv_w, lru_conv_b, lru_w_a, lru_b_a, lru_w_x, lru_b_x, lru_lambda,
           hgrn_lb_logits, hgrn_norm_g, group_norm_g, w_out, ln2_g,
           w_ffn_gate, w_ffn_up, w_ffn_down, final_norm_g):
    import concourse.bacc as bacc
    from concourse.bass_utils import run_bass_kernel_spmd

    arrays = dict(
        x=x.reshape(S, D), positions=positions.reshape(1, S),
        ln1=ln1_g.reshape(-1, P), ln2=ln2_g.reshape(-1, P), q_norm=mla_q_norm_g.reshape(-1, P),
        kv_norm=mla_kv_norm_g.reshape(-1, P), group_norm=group_norm_g.reshape(-1, P),
        conv_w=lru_conv_w.reshape(-1, P), conv_b=lru_conv_b.reshape(-1, P), b_a=lru_b_a.reshape(-1, P),
        b_x=lru_b_x.reshape(-1, P), lam=lru_lambda.reshape(-1, P), hg=hgrn_norm_g.reshape(-1, P),
        w_in=w_in.reshape(-1, D_IN), w_uq=mla_w_uq.reshape(-1, mla_w_uq.shape[-1]),
        w_ukv=mla_w_ukv.reshape(-1, mla_w_ukv.shape[-1]),
        w_a=lru_w_a.reshape(-1, 64), w_x=lru_w_x.reshape(-1, 64),
        lb_logits=hgrn_lb_logits.reshape(-1, P), w_out=w_out.reshape(-1, D),
        w_gate=w_ffn_gate.reshape(-1, FFN), w_up=w_ffn_up.reshape(-1, FFN), w_down=w_ffn_down.reshape(-1, D),
        final_g=final_norm_g.reshape(-1, P))
    arrays["consts"], arrays["level_masks"] = constants()
    arrays = {name: np.ascontiguousarray(a) for name, a in arrays.items()}
    nc = bacc.Bacc("TRN2", target_bir_lowering=False, num_devices=1)
    ap = {name: nc.dram_tensor(name, a.shape, mybir.dt.from_np(a.dtype), kind="ExternalInput").ap()
          for name, a in arrays.items()}
    out = nc.dram_tensor("out", (S, D), F32, kind="ExternalOutput").ap()
    vec_in = {key: ap.pop(key) for key in ("ln1", "ln2", "q_norm", "kv_norm", "group_norm", "conv_w",
                                           "conv_b", "b_a", "b_x", "lam", "hg")}
    build(nc, vec_in=vec_in, out=out, **ap)
    r = run_bass_kernel_spmd(nc, [arrays], core_ids=[0])
    return r.results[0]["out"].reshape(1, S, D)
```

```python
import math

import numpy as np
import concourse.bass as bass
from concourse import mybir
from contextlib import ExitStack

F32 = mybir.dt.float32
F32R = mybir.dt.float32r
I32 = mybir.dt.int32
U8 = mybir.dt.uint8
ACT = mybir.ActivationFunctionType
ALU = mybir.AluOpType
AX = mybir.AxisListType

P = 128
D = 1024
S = 1024
DEPTH = 2
KT = D // P
TT = S // P
HALF = 512
PAIRS = 2
Q_LORA, KV_LORA, NOPE, ROPE, HD = 256, 128, 64, 32, 64
GROUP_W = 256
FFN = 2816
CONV = 4
LRU_C = 8.0
EPS = 1e-6
MASKED = -1e30
LB_FLOOR = 1e-30
NCH = S // P
LEVELS = 7
D_IN = 2720
C_CQ, C_CKV, C_ROPE, C_X, C_GATE = 0, 256, 384, 416, 672
C_SBQ, C_SBK, C_SBV = 928, 1184, 1440
C_HQ, C_HF, C_HI, C_HG = 1696, 1952, 2208, 2464
MLA_SCALE = (NOPE + ROPE) ** -0.5
SB_SCALE = HD ** -0.5
LN_FLOOR = 2.0 ** -60
LN_SCALE = 1e15

PAIR_ROWS = 9
V_TAP, V_CB, V_BA, V_BX, V_LAM, V_HG = 0, 4, 5, 6, 7, 8
V_LN1, V_LN2, V_QN, V_KVN, V_GN, V_ROWS = 18, 26, 34, 36, 37, 43
W_LBA, W_LBC, W_LBD, W_C1, W_T0, W_T1, W_T2, W_T3, W_T4, W_N = 9, 10, 11, 12, 13, 14, 15, 16, 17, 18

K_ID, K_NEGS, K_NEGC, K_HEADS, K_FREQ, K_SIGN, K_N = 0, 128, 256, 384, 512, 513, 514

TWO_PI_1 = 6.28125
TWO_PI_2 = float(np.float32(np.round((2 * math.pi - 6.28125) * 2 ** 20) / 2 ** 20))
TWO_PI_3 = float(np.float32(2 * math.pi - 6.28125 - TWO_PI_2))
ROUND = 1.5 * 2.0 ** 23
PI_BELOW = 3.1415925


def build(nc, x, positions, vec_table, w_in, w_uq, w_ukv, w_a, w_x, lb_logits, w_out,
          w_gate, w_up, w_down, consts, level_masks, out):
    h_dram = nc.dram_tensor("h_spill", (D, S), F32).ap()
    ctx = ExitStack()
    with ctx:
        base = (nc.sbuf_base + 31) // 32 * 32
        cursor = [base]

        def fixed(name, shape, dtype=F32):
            size = math.prod(shape[1:]) * (1 if dtype == U8 else 4)
            t = nc.alloc_sbuf_tensor_at(name, shape, dtype, offset=cursor[0])
            cursor[0] += (size + 31) // 32 * 32
            return t

        CO = fixed("constants", [P, K_N])
        LM = fixed("level_mask", [P, LEVELS * 64], U8)
        ones = fixed("ones", [P, P])
        vecs = fixed("vectors", [P, V_ROWS])
        lbt = fixed("lower_bound", [P, 3, 4])
        pv = fixed("pair_vectors", [P, W_N])
        eps = fixed("eps", [P, 1])
        half_pi = fixed("half_pi", [P, 1])
        WA = fixed("w_a_blocks", [P, P])
        WX = fixed("w_x_blocks", [P, P])
        RT = fixed("rope", [P, S])
        raw = [fixed(f"w_raw{i}", [P, 1024]) for i in range(2)]
        whi = [fixed(f"w_hi{i}", [P, 1024], F32R) for i in range(2)]
        wlo = [fixed(f"w_lo{i}", [P, 1024], F32R) for i in range(2)]
        NM = fixed("mla_neg_max", [P, 2, 2])
        RSUM = fixed("mla_row_sum", [P, 4, 2])
        GMS = fixed("group_mean_sq", [P, 2, TT])
        RS = fixed("rs", [P, S])
        U0 = cursor[0]
        uhi = fixed("u_hi", [P, KT, S], F32R)
        ulo = fixed("u_lo", [P, KT, S], F32R)
        R0 = cursor[0]
        KB = 1024

        def at_u(name, kb, shape, dtype=F32):
            return nc.alloc_sbuf_tensor_at(name, shape, dtype, offset=U0 + kb * KB)

        def at_r(name, kb, shape, dtype=F32):
            return nc.alloc_sbuf_tensor_at(name, shape, dtype, offset=R0 + kb * KB)

        YB = at_r("y_b", 0, [P, PAIRS, S])
        YD = at_r("y_d", 8, [P, PAIRS, S])
        YA = at_r("y_a", 16, [P, TT, GROUP_W])
        YC = at_r("y_c", 24, [P, TT, GROUP_W])
        h = at_r("h", 32, [P, KT, S])

        ps = ctx.enter_context(nc.psum_tensor("ps", [P, 8, HALF], F32))

        def pair(p, rows=slice(0, P)):
            return ps[rows, 2 * p:2 * p + 2, :]

        def wide(ap):
            return ap.rearrange("p (b n) -> p b n", b=2)

        ident = CO[:, K_ID:K_ID + P]
        h_rows = h_dram.rearrange("(k p) s -> k p s", p=P)

        names = []

        def sem(name):
            s = ctx.enter_context(nc.semaphore(name))
            names.append(s)
            return s

        def sems(name, n):
            return [sem(f"{name}{i}") for i in range(n)]

        def end_of_block():
            nc.all_engine_barrier(sems_to_clear=range(names[0].num, names[-1].num + 1))

        raw_loaded = sems("raw_loaded", 2)
        hi_split = sem("hi_split")
        slot_split = sem("slot_split")
        proj_done = sem("proj_done")
        bank_free = sems("pair_free", 4)
        small_loaded = sem("small_loaded")
        h_moved = sem("h_moved")
        stored = sem("stored")
        ms_done = sem("ms_done")
        rs_part = sem("rs_part")
        rstd_ready = sem("rstd_ready")
        act_step = sem("act_step")
        dve_step = sem("dve_step")
        pool_step = sem("pool_step")

        def exp_and_ln():
            nc.scalar.preload_act_table_set("natural_log_exp_and_others")

        def load_slot(sp, n, parts):
            if n >= 4:
                sp.wait_ge(slot_split, n - 3)
            for dst, src in parts:
                sp.dma_start(dst, src).then_inc(raw_loaded[n % 2], 16)

        def split_slot(pool, n, dmas, jobs, width=1024):
            i = n % 2
            pool.wait_ge(raw_loaded[i], 16 * dmas)
            if jobs:
                pool.wait_ge(proj_done, jobs)
            nc.gpsimd.tensor_tensor(whi[i][:, 0:width], raw[i][:, 0:width], ones[:, 0:1].broadcast_to([P, width]),
                                    ALU.mult).then_inc(hi_split, 1)
            pool.wait_ge(hi_split, n - 1)
            nc.gpsimd.tensor_tensor(wlo[i][:, 0:width], raw[i][:, 0:width],
                                    whi[i][:, 0:width].bitcast(F32),
                                    ALU.subtract).then_inc(slot_split, 1)

        def product(pe, bank0, lhs, rhs, kt, before_k=None, order=None):
            order = list(range(kt)) if order is None else order
            for k in order:
                if before_k is not None:
                    before_k(k)
                lh, ll = lhs(k)
                rh, rl = rhs(k)
                for n, (a, b) in enumerate(((lh, rh), (lh, rl), (ll, rh))):
                    for half in range(2):
                        last = nc.tensor.matmul(ps[:, bank0 + half, :], a, b[:, half * HALF:(half + 1) * HALF],
                                                start=(k == order[0] and n == 0), stop=(k == order[-1] and n == 2))
            return last

        def slot_lhs(n, off=0, step=P, width=P):
            i = n % 2
            return lambda k: (whi[i][:, off + k * step:off + k * step + width],
                              wlo[i][:, off + k * step:off + k * step + width])

        def u_rhs(k):
            return uhi[:, k, :], ulo[:, k, :]

        def project_slot(pe, n, job, p, before_k=None, order=None):
            if n >= 2:
                pe.wait_ge(slot_split, n - 1)
            last = product(pe, 2 * p, slot_lhs(n), u_rhs, KT, before_k, order)
            if job is not None:
                last.then_inc(proj_done, 1)

        def norm_sems(name):
            return tuple(sem(f"{name}_{part}") for part in ("sq", "acc", "hi", "lo"))

        def norm_act(act, F, m, SQ, hi, gain):
            sq, acc, hi_done, _ = F
            if m >= 2:
                act.wait_ge(acc, max(1, m - 2))
            nc.scalar.activation(SQ[m % 2][:, :], h[:, m, :], ACT.Square).then_inc(sq, 1)
            nc.scalar.activation(hi, h[:, m, :], ACT.Copy, scale=gain).then_inc(hi_done, 1)

        def norm_pool(pool, F, m, SQ, ACC):
            sq, acc, _, _ = F
            if m == 0:
                return
            pool.wait_ge(sq, m + 1)
            if m >= 2:
                pool.wait_ge(acc, m - 1)
            nc.gpsimd.tensor_tensor(ACC[:, :], SQ[0][:, :] if m == 1 else ACC[:, :], SQ[m % 2][:, :],
                                    ALU.add).then_inc(acc, 1)

        def norm_dve(dve, F, m, hi, lo, gain):
            _, _, hi_done, lo_done = F
            dve.wait_ge(hi_done, m + 1)
            nc.vector.scalar_tensor_tensor(lo, h[:, m, :], gain, hi.bitcast(F32), ALU.mult, ALU.subtract)\
                .then_inc(lo_done, 1)

        def norm_pe(pe, F, ACC, p, done):
            pe.wait_ge(F[1], KT - 1)
            for half in range(2):
                last = nc.tensor.matmul(ps[:, 2 * p + half, :], ones[:, :], ACC[:, half * HALF:(half + 1) * HALF],
                                        start=True, stop=True)
            last.then_inc(done, 1)

        def norm_rs(act, p, read):
            nc.scalar.activation(wide(RS[:, :]), pair(p), ACT.Ln, scale=1.0 / D,
                                 bias=eps[:, 0:1]).then_inc(read[0], 1)
            act.wait_ge(*read)
            nc.scalar.activation(RS[:, :], RS[:, :], ACT.Exp, scale=-0.5).then_inc(rstd_ready, 1)

        def ln1(m):
            return vecs[:, V_LN1 + m:V_LN1 + m + 1]

        def load_bd_slots(sp, row0):
            for n, c in enumerate((C_HF, C_HQ)):
                src = w_in[row0:row0 + D, c:c + P].rearrange("(k p) c -> p k c", p=P)
                sp.dma_start(raw[n][:, :].rearrange("p (k c) -> p k c", c=P), src).then_inc(raw_loaded[n], 16)

        XIN = [at_u(f"x_in{i}", 32 + 4 * i, [P, D]) for i in range(TT)]
        XSQ = [at_u(f"x_sq{i}", 4 * i, [P, D]) for i in range(2)]
        RD = at_r("rs_diagonal", 64, [P, TT, P])
        XMS = at_r("x_mean_sq", 72, [P, TT])
        LMI = at_r("level_mask_int", 92, [P, LEVELS * 64], I32)
        LW = at_r("lb_work", 73, [P, 12, 4])
        PI_ = at_r("pos_int", 76, [1, S], I32)
        PF = at_r("pos_float", 80, [1, S])
        AN = at_r("angle", 84, [64, S])
        RK = at_r("turns", 88, [64, S])
        x_loaded = sems("x_loaded", TT)
        x_sq = sem("x_sq")
        x_rs = sem("x_rs")
        rs_diag = sem("rs_diag")
        h_written = sem("h_written")
        pos_ready = sem("pos_ready")
        pos_done = sem("pos_done")
        norm0 = norm_sems("norm0")
        ready0 = sem("ready0")
        rope_step = sem("rope_step")
        lb_step = sem("lb_step")
        with nc.Block() as block:
            @block.sync
            def _(sp):
                sp.dma_start(CO[:, :], consts[:, :]).then_inc(small_loaded, 16)
                sp.dma_start(LMI[:, :], level_masks[:, :]).then_inc(small_loaded, 16)
                sp.dma_start(LW[:, 0, :], lb_logits[:, :]).then_inc(small_loaded, 16)
                sp.dma_start(PI_[:, :], positions[:, :]).then_inc(small_loaded, 16)
                sp.dma_start(vecs[:, :], vec_table[0:P, :]).then_inc(small_loaded, 16)
                for t in range(TT):
                    sp.dma_start(XIN[t][:, :], x[t * P:(t + 1) * P, :]).then_inc(x_loaded[t], 16)
                    if t == 1:
                        load_bd_slots(sp, 0)
                sp.wait_ge(h_written, TT)
                for k in range(KT):
                    sp.dma_start(h_rows[k], h[:, k, :]).then_inc(h_moved, 16)
                sp.wait_ge(h_moved, 16 * KT)

            @block.gpsimd
            def _(pool):
                nc.gpsimd.memset(WA[:, :], 0.0).then_inc(pool_step, 1)
                nc.gpsimd.memset(WX[:, :], 0.0).then_inc(pool_step, 1)
                pool.wait_ge(ready0, 3)
                for n in range(2):
                    split_slot(pool, n + 2, 1, 0)

            @block.vector
            def _(dve):
                nc.vector.memset(ones[:, :], 1.0).then_inc(ready0, 1)
                nc.vector.memset(eps[:, :], EPS).then_inc(ready0, 1)
                nc.vector.memset(half_pi[:, :], math.pi / 2).then_inc(ready0, 1)
                dve.wait_ge(small_loaded, 80)
                nc.vector.tensor_copy(LM[:, :], LMI[:, :]).then_inc(dve_step, 1)
                nc.vector.tensor_copy(PF[:, :], PI_[:, :]).then_inc(pos_ready, 1)
                n = 0

                def step(ins):
                    nonlocal n
                    n += 1
                    ins.then_inc(lb_step, 1)
                    dve.wait_ge(lb_step, n)

                w = lambda i, a=0, b=2: LW[:, i, a:b]
                step(nc.vector.tensor_tensor(w(1), w(0), w(0, 2, 4), ALU.max))
                step(nc.vector.tensor_tensor(w(2), w(0), w(1), ALU.subtract))
                step(nc.vector.tensor_tensor(w(2, 2, 4), w(0, 2, 4), w(1), ALU.subtract))
                dve.wait_ge(ready0, 4)
                step(nc.vector.tensor_tensor(w(4), w(3), w(3, 2, 4), ALU.add))
                step(nc.vector.reciprocal(w(4), w(4)))
                step(nc.vector.tensor_tensor(w(5), w(3), w(4), ALU.mult))
                step(nc.vector.tensor_tensor(w(5, 2, 4), w(3, 2, 4), w(4), ALU.mult))
                step(nc.vector.tensor_tensor(w(6), w(5), w(5), ALU.subtract))
                step(nc.vector.tensor_tensor(w(6, 2, 4), w(5), w(5, 2, 4), ALU.add))
                step(nc.vector.tensor_tensor(w(6, 2, 4), w(6, 2, 4), w(5), ALU.subtract))
                step(nc.vector.tensor_scalar(w(7, 0, 4), w(6, 0, 4), LN_FLOOR, None, ALU.max))
                step(nc.vector.tensor_scalar(w(8, 0, 4), w(6, 0, 4), LB_FLOOR, LN_SCALE, ALU.max, ALU.mult))
                step(nc.vector.tensor_scalar(w(8, 0, 4), w(8, 0, 4), LN_SCALE * LN_FLOOR, None, ALU.min))
                step(nc.vector.tensor_scalar(w(9, 0, 4), w(6, 0, 4), -1.0, 1.0, ALU.mult, ALU.add))
                step(nc.vector.tensor_scalar(w(9, 0, 4), w(9, 0, 4), 1e-18, None, ALU.max))
                nc.vector.tensor_scalar(w(10, 0, 4), w(6, 0, 4), LN_FLOOR, None, ALU.is_lt).then_inc(ready0, 1)
                dve.wait_ge(ready0, 6)
                step(nc.vector.tensor_scalar(w(8, 0, 4), w(8, 0, 4),
                                             -(math.log(LN_SCALE) + math.log(LN_FLOOR)), None, ALU.add))
                step(nc.vector.tensor_tensor(w(8, 0, 4), w(8, 0, 4), w(10, 0, 4), ALU.mult))
                step(nc.vector.tensor_tensor(lbt[:, 0, :], w(7, 0, 4), w(8, 0, 4), ALU.add))
                step(nc.vector.tensor_copy(lbt[:, 1, :], w(9, 0, 4)))
                step(nc.vector.tensor_tensor(lbt[:, 2, :], w(9, 0, 4), lbt[:, 0, :], ALU.subtract))
                r = 0

                def turn(ins):
                    nonlocal r
                    r += 1
                    ins.then_inc(rope_step, 1)
                    dve.wait_ge(rope_step, r)

                dve.wait_ge(pos_done, 1)
                turn(nc.vector.tensor_scalar(wide(AN[:, :]), pair(2, slice(0, 64)), CO[0:64, K_FREQ:K_FREQ + 1],
                                             None, ALU.mult))
                turn(nc.vector.tensor_scalar(RK[:, :], AN[:, :], 1.0 / (2 * math.pi), ROUND, ALU.mult, ALU.add))
                turn(nc.vector.tensor_scalar(RK[:, :], RK[:, :], ROUND, None, ALU.subtract))
                for part in (TWO_PI_1, TWO_PI_2, TWO_PI_3):
                    turn(nc.vector.scalar_tensor_tensor(AN[:, :], RK[:, :], -part, AN[:, :], ALU.mult, ALU.add))
                turn(nc.vector.tensor_scalar(AN[:, :], AN[:, :], PI_BELOW, -PI_BELOW, ALU.min, ALU.max))
                dve.wait_ge(x_rs, 2)
                nc.vector.tensor_tensor(
                    RD[:, :, :], XMS[:, :].rearrange("p (t o) -> p t o", o=1).broadcast_to([P, TT, P]),
                    ident.rearrange("p (o c) -> p o c", o=1).broadcast_to([P, TT, P]), ALU.mult).then_inc(rs_diag, 1)
                for m in range(KT):
                    norm_dve(dve, norm0, m, uhi[:, m, :], ulo[:, m, :], ln1(m))
                dve.wait_ge(ready0, 8)
                turn(nc.vector.tensor_scalar(RT[32:64, :], RT[32:64, :], CO[32:64, K_SIGN:K_SIGN + 1], None,
                                             ALU.mult))

            @block.scalar
            def _(act):
                act.wait_ge(lb_step, 3)
                nc.scalar.activation(LW[:, 3, :], LW[:, 2, :], ACT.Exp).then_inc(ready0, 1)
                act.wait_ge(ready0, 5)
                act.wait_ge(lb_step, 15)
                nc.scalar.activation(LW[:, 7:10, :], LW[:, 7:10, :], ACT.Ln).then_inc(ready0, 1)
                for t in range(TT):
                    act.wait_ge(x_loaded[t], 16)
                    if t >= 2:
                        act.wait_ge(x_sq, t - 1)
                    nc.scalar.activation(XSQ[t % 2][:, :], XIN[t][:, :], ACT.Square,
                                         accum_out=XMS[:, t:t + 1]).then_inc(x_sq, 1)
                    act.wait_ge(proj_done, t + 1)
                    nc.scalar.activation(
                        h[:, :, t * P:(t + 1) * P],
                        pair(t % 2).rearrange("p b (k t) -> p (b k) t", t=P), ACT.Copy).then_inc(h_written, 1)
                act.wait_ge(x_sq, TT)
                nc.scalar.activation(XMS[:, :], XMS[:, :], ACT.Ln, scale=1.0 / D, bias=eps[:, 0:1]).then_inc(x_rs, 1)
                act.wait_ge(x_rs, 1)
                nc.scalar.activation(XMS[:, :], XMS[:, :], ACT.Exp, scale=-0.5).then_inc(x_rs, 1)
                act.wait_ge(h_written, TT)
                for m in range(KT):
                    nc.scalar.activation(uhi[:, m, :], h[:, m, :], ACT.Copy, scale=ln1(m)).then_inc(norm0[2], 1)
                act.wait_ge(ms_done, 1)
                nc.scalar.activation(wide(RS[:, :]), pair(3), ACT.Copy).then_inc(rs_part, 1)
                act.wait_ge(rope_step, 7)
                nc.scalar.activation(RK[0:32, :], AN[0:32, :], ACT.Abs).then_inc(act_step, 1)
                act.wait_ge(act_step, 1)
                nc.scalar.activation(RT[0:32, :], RK[0:32, :], ACT.Sin, scale=-1.0,
                                     bias=half_pi[0:32, 0:1]).then_inc(ready0, 1)
                nc.scalar.activation(RT[32:64, :], AN[32:64, :], ACT.Sin).then_inc(ready0, 1)

            @block.tensor
            def _(pe):
                pe.wait_ge(small_loaded, 80)
                pe.wait_ge(ready0, 3)
                pe.wait_ge(pos_ready, 1)
                for half in range(2):
                    last = nc.tensor.matmul(ps[0:64, 4 + half, :], ones[0:1, 0:64],
                                            PF[0:1, half * HALF:(half + 1) * HALF], start=True, stop=True)
                last.then_inc(pos_done, 1)
                for t in range(TT):
                    pe.wait_ge(x_loaded[t], 16)
                    if t >= 2:
                        pe.wait_ge(h_written, t - 1)
                    for k in range(KT):
                        b = 2 * (t % 2) + k // 4
                        last = nc.tensor.transpose(ps[:, b, (k % 4) * P:(k % 4 + 1) * P],
                                                   XIN[t][:, k * P:(k + 1) * P], ident)
                    last.then_inc(proj_done, 1)
                def before(k):
                    pe.wait_ge(norm0[3], k + 1)
                    if k == 4:
                        pe.wait_ge(rs_diag, 1)
                        for half in range(2):
                            last = nc.tensor.matmul(ps[:, 6 + half, :], ones[:, :],
                                                    RD[:, half * 4:half * 4 + 4, :].rearrange("p t c -> p (t c)"),
                                                    start=True, stop=True)
                        last.then_inc(ms_done, 1)

                pe.wait_ge(h_written, TT)
                pe.wait_ge(slot_split, 1)
                product(pe, 0, slot_lhs(0), u_rhs, KT, before)
        end_of_block()

        bF, bT, bB, bM, bK, bCUM, bQ, bG, bV = (
            at_r(n, 16 + 4 * i, [P, S]) for i, n in enumerate(
                ("f", "soft", "log_sig", "log_f", "key", "cum", "q", "g", "v")))
        VTOK = at_r("v_tok", 52, [P, NCH, P])
        QL = [at_r(f"q_level{i}", 56 + 2 * i, [P, NCH, 64]) for i in range(2)]
        SC = at_r("scores", 60, [P, NCH, 2, P])
        EC = at_r("exp_cum", 68, [P, S])
        ST = at_r("states", 72, [P, NCH, P])
        XP = at_r("x_padded", 76, [P, S + 4])
        XC = at_r("x_conv", 81, [P, S])
        GT = at_r("gate", 85, [P, S])
        TR = at_r("rec_gate", 89, [P, S])
        TI = at_r("in_gate", 93, [P, S])
        GE = at_r("gelu", 97, [P, S])
        TH = at_r("tanh_log_a", 56, [P, S])
        LE = [bF, bT]
        KL = [bB, bM]
        pair_vecs = sem("pair_vecs")
        lam_part = sem("lam_part")
        f_soft = sem("f_soft")
        b_ready = sem("b_ready")
        kx_ready = sem("kx_ready")
        key_ready = sem("key_ready")
        f_soft2 = sem("f_soft2")
        logf_ready = sem("logf_ready")
        cum_ready = sem("cum_ready")
        vT_done = sem("vT_done")
        vtok_ready = sem("vtok_ready")
        e_in = sem("e_in")
        e_ready = sem("e_ready")
        ql_ready = sem("ql_ready")
        level_done = sem("level_done")
        sc_zero = sem("sc_zero")
        sc_ready = sem("sc_ready")
        ec_ready = sem("ec_ready")
        kx2_ready = sem("kx2_ready")
        kdec_ready = sem("kdec_ready")
        ke_ready = sem("ke_ready")
        keT_done = sem("keT_done")
        ket_ready = sem("ket_ready")
        upd_done = sem("upd_done")
        st_zero = sem("st_zero")
        st_ready = sem("st_ready")
        qe_ready = sem("qe_ready")
        qk_ready = sem("qk_ready")
        diag_done = sem("diag_done")
        o_done = sem("o_done")
        od_ready = sem("od_ready")
        o_ready = sem("o_ready")
        osq_ready = sem("osq_ready")
        oms_done = sem("oms_done")
        orstd = sem("orstd")
        gelu_part = sem("gelu_part")
        pool_scaled = sem("pool_scaled")
        conv_step = sem("conv_step")
        gates_done = sem("gates_done")
        gates_read = sem("gates_read")
        la_ready = sem("la_ready")
        decay_ready = sem("decay_ready")
        neg_ready = sem("neg_ready")
        root_ready = sem("root_ready")
        gelu_sq = sem("gelu_sq")
        gelu_in = sem("gelu_in")
        gelu_th = sem("gelu_th")
        silu_th = sem("silu_th")
        gate_loaded = sem("gate_loaded")

        def group_bd(l, pr):
            slots = [C_HF, C_HQ, C_HG, C_HI, C_X, C_GATE]

            def chunks(t, n=P):
                return t[:, :].rearrange("p (c t) -> p c t", t=n)

            def col(i):
                return pv[:, i:i + 1]

            with nc.Block() as block:
                @block.sync
                def _(sp):
                    for n, c in enumerate(slots):
                        if n < 2:
                            continue
                        src = w_in[bass.ds(l * D, D), bass.ds(pr * P + c, P)].rearrange("(k p) c -> p k c", p=P)
                        load_slot(sp, n, [(raw[n % 2][:, :].rearrange("p (k c) -> p k c", c=P), src)])
                    for n, (of_pair, of_latent) in ((6, (C_HF + P, C_CQ)), (7, (C_HQ + P, C_CQ + P))):
                        src = w_in[bass.ds(l * D, D), bass.ds(pr * (of_latent - of_pair) + of_pair, P)]
                        load_slot(sp, n, [(raw[n % 2][:, :].rearrange("p (k c) -> p k c", c=P),
                                           src.rearrange("(k p) c -> p k c", p=P))])
                    for W, src in ((WA, w_a), (WX, w_x)):
                        for j in range(2):
                            at = slice(64 * j, 64 * j + 64)
                            sp.dma_start(W[at, at], src[bass.ds((l * 4 + pr * 2 + j) * 64, 64), :])\
                                .then_inc(gate_loaded, 16)

                @block.gpsimd
                def _(pool):
                    nc.gpsimd.memset(SC[:, :, :, :], 0.0).then_inc(sc_zero, 1)
                    nc.gpsimd.memset(ST[:, :, :], 0.0).then_inc(st_zero, 1)
                    nc.gpsimd.memset(XP[:, 0:3], 0.0).then_inc(st_zero, 1)
                    for n in range(2, len(slots) + 2):
                        split_slot(pool, n, n // 2, n - 2)
                        if n in (4, 5, 7):
                            t, (read, count) = {4: (bG, (bank_free[0], 2)), 5: (bV, (bank_free[1], 2)),
                                                7: (GT, (bank_free[1], 3))}[n]
                            pool.wait_ge(read, count)
                            nc.gpsimd.tensor_tensor(t[:, :], t[:, :], RS[:, :], ALU.mult).then_inc(pool_scaled, 1)

                @block.tensor
                def _(pe):
                    def level(L, chunk):
                        if chunk == 0:
                            pe.wait_ge(ql_ready, 2 * (L + 1))
                            if L >= 2:
                                pe.wait_ge(sc_ready, 2 * (L - 1))
                        for j in range(2):
                            rows = slice(64 * j, 64 * j + 64)
                            last = nc.tensor.matmul(ps[:, 4 + 2 * (L % 2) + j, chunk * 64:(chunk + 1) * 64],
                                                    KL[L % 2][rows, chunk * P:(chunk + 1) * P],
                                                    QL[L % 2][rows, chunk, :], start=True, stop=True)
                        if chunk == NCH - 1:
                            last.then_inc(level_done, 1)

                    def two_levels(L):
                        def before(k):
                            for chunk in (2 * (k % 4), 2 * (k % 4) + 1):
                                level(L + k // 4, chunk)
                        return before

                    def level_0(k):
                        for chunk in {2: (0, 1), 3: (2, 3)}.get(k, (k,) if k >= 4 else ()):
                            level(0, chunk)

                    project_slot(pe, 1, 1, 1)
                    pe.wait_ge(bank_free[0], 1)
                    project_slot(pe, 2, 2, 0)
                    pe.wait_ge(bank_free[1], 1)
                    project_slot(pe, 3, 3, 1, level_0)
                    pe.wait_ge(bank_free[0], 2)
                    project_slot(pe, 4, 4, 0, two_levels(1))
                    pe.wait_ge(bank_free[1], 2)
                    project_slot(pe, 5, 5, 1, two_levels(3))
                    for c in range(NCH):
                        level(5, c)
                    pe.wait_ge(pool_scaled, 2)
                    pe.wait_ge(sc_ready, 10)
                    for c in range(NCH):
                        last = nc.tensor.transpose(ps[:, 4 + c // 4, (c % 4) * P:(c % 4 + 1) * P],
                                                   bV[:, c * P:(c + 1) * P], ident)
                    last.then_inc(vT_done, 1)
                    pe.wait_ge(gate_loaded, 64)
                    pe.wait_ge(conv_step, 4)
                    pe.wait_ge(bank_free[1], 3)
                    for i in range(4):
                        p, half = divmod(i, 2)
                        last = nc.tensor.matmul(ps[:, 2 * p + half, :], (WA, WX)[p][:, :],
                                                XC[:, half * HALF:(half + 1) * HALF], start=True, stop=True)
                        if i == 3:
                            last.then_inc(gates_done, 1)
                        if i == 1:
                            pe.wait_ge(vtok_ready, 1)
                        for chunk in ((), (0, 1, 2), (3, 4, 5), (6, 7))[i]:
                            level(6, chunk)
                    pe.wait_ge(ke_ready, 1)
                    pe.wait_ge(sc_ready, 2 * (LEVELS - 1))
                    for c in range(NCH):
                        last = nc.tensor.transpose(ps[:, 6 + c // 4, (c % 4) * P:(c % 4 + 1) * P],
                                                   bB[:, c * P:(c + 1) * P], ident)
                    last.then_inc(keT_done, 1)
                    pe.wait_ge(ket_ready, 1)
                    pe.wait_ge(sc_ready, 2 * LEVELS)
                    for c in range(NCH):
                        last = nc.tensor.matmul(ps[:, 4 + c // 4, (c % 4) * P:(c % 4 + 1) * P],
                                                bM[:, c * P:(c + 1) * P], VTOK[:, c, :], start=True, stop=True)
                    last.then_inc(upd_done, 1)
                    pe.wait_ge(qk_ready, 1)
                    pe.wait_ge(gates_read, 2)
                    for half in range(2):
                        last = nc.tensor.matmul(ps[:, half, :], CO[:, K_HEADS:K_HEADS + P],
                                                bQ[:, half * HALF:(half + 1) * HALF], start=True, stop=True)
                    last.then_inc(diag_done, 1)
                    pe.wait_ge(qe_ready, 1)
                    for c in range(NCH):
                        out_c = ps[:, 6 + c // 4, (c % 4) * P:(c % 4 + 1) * P]
                        if c >= 1:
                            pe.wait_ge(st_ready, 2 * c)
                            nc.tensor.matmul(out_c, ST[:, c - 1, :], bT[:, c * P:(c + 1) * P],
                                             start=True, stop=False, skip_group_check=True)
                        for j in range(2):
                            rows = slice(64 * j, 64 * j + 64)
                            last = nc.tensor.matmul(ps[rows, 6 + c // 4, (c % 4) * P:(c % 4 + 1) * P],
                                                    VTOK[:, c, rows], SC[:, c, j, :],
                                                    start=(c == 0), stop=True, skip_group_check=True)
                    last.then_inc(o_done, 1)
                    def head_sums(k):
                        if k == 2:
                            pe.wait_ge(osq_ready, 1)
                            for half in range(2):
                                last = nc.tensor.matmul(ps[:, 2 + half, :], CO[:, K_HEADS:K_HEADS + P],
                                                        bQ[:, half * HALF:(half + 1) * HALF], start=True, stop=True)
                            last.then_inc(oms_done, 1)

                    pe.wait_ge(od_ready, 1)
                    project_slot(pe, len(slots), None, 0, head_sums)

                @block.scalar
                def _(act):
                    exp_and_ln()
                    act.wait_ge(pair_vecs, 2)
                    nc.scalar.activation(col(W_T0), col(V_LAM), ACT.Abs).then_inc(lam_part, 1)
                    act.wait_ge(lam_part, 1)
                    nc.scalar.activation(col(W_T0), col(W_T0), ACT.Exp, scale=-1.0).then_inc(lam_part, 1)
                    act.wait_ge(bank_free[0], 1)
                    nc.scalar.activation(bT[:, :], bF[:, :], ACT.Abs).then_inc(f_soft, 1)
                    act.wait_ge(f_soft, 1)
                    nc.scalar.activation(bT[:, :], bT[:, :], ACT.Exp, scale=-1.0).then_inc(f_soft, 1)
                    act.wait_ge(f_soft, 2)
                    nc.scalar.activation(bT[:, :], bT[:, :], ACT.Ln, bias=1.0).then_inc(f_soft, 1)
                    act.wait_ge(b_ready, 1)
                    nc.scalar.activation(bT[:, :], bB[:, :], ACT.Abs, bias=col(W_LBD)).then_inc(f_soft2, 1)
                    act.wait_ge(f_soft2, 1)
                    nc.scalar.activation(bT[:, :], bT[:, :], ACT.Exp, scale=-1.0).then_inc(f_soft2, 1)
                    act.wait_ge(f_soft2, 2)
                    nc.scalar.activation(bT[:, :], bT[:, :], ACT.Ln, bias=1.0).then_inc(f_soft2, 1)
                    act.wait_ge(kx_ready, 1)
                    nc.scalar.activation(bK[:, :], bF[:, :], ACT.Exp, bias=col(W_LBC)).then_inc(key_ready, 1)
                    act.wait_ge(cum_ready, NCH)
                    nc.scalar.activation(EC[:, :], bCUM[:, :], ACT.Exp).then_inc(ec_ready, 1)
                    for L in range(LEVELS):
                        act.wait_ge(e_in, 2 * (L + 1))
                        nc.scalar.activation(LE[L % 2][:, :], LE[L % 2][:, :], ACT.Exp).then_inc(e_ready, 1)
                        if L == 1:
                            act.wait_ge(proj_done, 2)
                            nc.scalar.activation(wide(bG[:, :]), pair(0), ACT.Copy).then_inc(bank_free[0], 1)
                        if L == 3:
                            act.wait_ge(proj_done, 3)
                            nc.scalar.activation(wide(bV[:, :]), pair(1), ACT.Copy).then_inc(bank_free[1], 1)
                    act.wait_ge(vT_done, 1)
                    nc.scalar.activation(VTOK[:, :, :].rearrange("p (b c) t -> p b (c t)", b=2), pair(2),
                                         ACT.Copy).then_inc(vtok_ready, 1)
                    act.wait_ge(proj_done, 5)
                    nc.scalar.activation(wide(GT[:, :]), pair(1), ACT.Copy).then_inc(bank_free[1], 1)
                    act.wait_ge(kx2_ready, 1)
                    nc.scalar.activation(bF[:, :], bF[:, :], ACT.Exp).then_inc(kdec_ready, 1)
                    act.wait_ge(gates_done, 1)
                    nc.scalar.activation(wide(TR[:, :]), pair(0), ACT.Sigmoid, bias=col(V_BA)).then_inc(gates_read, 1)
                    nc.scalar.activation(wide(TI[:, :]), pair(1), ACT.Sigmoid, bias=col(V_BX)).then_inc(gates_read, 1)
                    act.wait_ge(pool_scaled, 3)
                    nc.scalar.activation(GE[:, :], GT[:, :], ACT.Square).then_inc(gelu_sq, 1)
                    nc.scalar.activation(XP[:, 0:S], bG[:, :], ACT.Sigmoid).then_inc(silu_th, 1)
                    act.wait_ge(gelu_in, 1)
                    nc.scalar.activation(GE[:, :], GE[:, :], ACT.Sigmoid, scale=2 * math.sqrt(2 / math.pi))\
                        .then_inc(gelu_th, 1)
                    act.wait_ge(la_ready, 1)
                    act.wait_ge(level_done, LEVELS)
                    nc.scalar.activation(TH[:, :], TR[:, :], ACT.Tanh).then_inc(decay_ready, 1)
                    exp_and_ln()
                    act.wait_ge(dve_step, 1)
                    nc.scalar.activation(XP[:, 0:S], TR[:, :], ACT.Exp).then_inc(decay_ready, 1)
                    act.wait_ge(o_ready, 1)
                    nc.scalar.activation(bQ[:, :], bCUM[:, :], ACT.Square).then_inc(osq_ready, 1)
                    act.wait_ge(oms_done, 1)
                    nc.scalar.activation(wide(bF[:, :]), pair(1), ACT.Ln, scale=1.0 / HD, bias=eps[:, 0:1])\
                        .then_inc(orstd, 1)
                    act.wait_ge(orstd, 1)
                    nc.scalar.activation(bF[:, :], bF[:, :], ACT.Exp, scale=-0.5).then_inc(orstd, 1)
                    act.wait_ge(neg_ready, 1)
                    nc.scalar.activation(TH[:, :], TH[:, :], ACT.Sqrt).then_inc(root_ready, 1)

                @block.vector
                def _(dve):
                    nc.vector.tensor_copy(pv[:, 0:PAIR_ROWS], vecs[:, bass.ds(pr * PAIR_ROWS, PAIR_ROWS)])\
                        .then_inc(pair_vecs, 1)
                    nc.vector.tensor_copy(pv[:, W_LBA:W_LBA + 3].rearrange("p (i o) -> p i o", o=1),
                                          lbt[:, :, bass.ds(l * 2 + pr, 1)]).then_inc(pair_vecs, 1)
                    dve.wait_ge(pair_vecs, 2)
                    n = 2

                    def step(ins):
                        nonlocal n
                        n += 1
                        ins.then_inc(pair_vecs, 1)
                        dve.wait_ge(pair_vecs, n)

                    nc_ts = nc.vector.tensor_scalar
                    step(nc_ts(col(W_T1), col(V_LAM), -1.0, 0.0, ALU.mult, ALU.max))
                    dve.wait_ge(lam_part, 2)
                    step(nc_ts(col(W_T2), col(W_T0), 2.0, None, ALU.add))
                    step(nc.vector.reciprocal(col(W_T2), col(W_T2)))
                    step(nc.vector.tensor_tensor(col(W_T2), col(W_T2), col(W_T0), ALU.mult))
                    step(nc.vector.tensor_tensor(col(W_T3), col(W_T2), col(W_T2), ALU.mult))
                    step(nc_ts(col(W_T4), col(W_T3), 1.0 / 17, 1.0 / 15, ALU.mult, ALU.add))
                    for term in (13, 11, 9, 7, 5, 3, 1):
                        step(nc_ts(col(W_T4), col(W_T4), col(W_T3), 1.0 / term, ALU.mult, ALU.add))
                    step(nc.vector.tensor_tensor(col(W_T4), col(W_T4), col(W_T2), ALU.mult))
                    step(nc.vector.scalar_tensor_tensor(col(W_T4), col(W_T4), 2.0, col(W_T1), ALU.mult, ALU.add))
                    step(nc_ts(col(W_C1), col(W_T4), -LRU_C, None, ALU.mult))
                    nc.vector.tensor_tensor(wide(bF[:, :]), pair(0), wide(RS[:, :]), ALU.mult).then_inc(bank_free[0], 1)
                    dve.wait_ge(bank_free[0], 1)
                    dve.wait_ge(f_soft, 3)
                    nc.vector.scalar_tensor_tensor(bB[:, :], bF[:, :], 0.0, bT[:, :], ALU.min, ALU.subtract)\
                        .then_inc(b_ready, 1)
                    dve.wait_ge(b_ready, 1)
                    nc.vector.tensor_tensor(bF[:, :], bB[:, :], bF[:, :], ALU.subtract).then_inc(kx_ready, 1)
                    nc.vector.tensor_scalar(bM[:, :], bB[:, :], col(W_LBC), col(W_LBA), ALU.add, ALU.max)\
                        .then_inc(logf_ready, 1)
                    dve.wait_ge(logf_ready, 1)
                    dve.wait_ge(f_soft2, 3)
                    nc.vector.tensor_tensor(bM[:, :], bM[:, :], bT[:, :], ALU.add).then_inc(logf_ready, 1)
                    dve.wait_ge(logf_ready, 2)
                    for c in range(NCH):
                        at = slice(c * P, (c + 1) * P)
                        nc.vector.tensor_tensor_scan(bCUM[:, at], ones[:, :], bM[:, at], 0.0, ALU.mult, ALU.add)\
                            .then_inc(cum_ready, 1)
                    dve.wait_ge(cum_ready, NCH)

                    def level_in(L):
                        n = 64 >> L
                        cum = bCUM[:, :].rearrange("p (b s n) -> p b s n", s=2, n=n)
                        e = LE[L % 2][:, :].rearrange("p (b s n) -> p b s n", s=2, n=n)
                        mid = cum[:, :, 0, n - 1:n].broadcast_to([P, S // (2 * n), n])
                        if L < 2:
                            dve.wait_ge(key_ready, 1)
                        else:
                            dve.wait_ge(ql_ready, 2 * (L - 1))
                        nc.vector.tensor_tensor(e[:, :, 0, :], mid, cum[:, :, 0, :], ALU.subtract).then_inc(e_in, 1)
                        nc.vector.tensor_tensor(e[:, :, 1, :], cum[:, :, 1, :], mid, ALU.subtract).then_inc(e_in, 1)

                    def level_keys(L):
                        n = 64 >> L
                        dve.wait_ge(e_ready, L + 1)
                        if L == 0:
                            dve.wait_ge(bank_free[1], 1)
                        if L >= 2:
                            dve.wait_ge(level_done, L - 1)
                        e = LE[L % 2][:, :].rearrange("p (b s n) -> p b s n", s=2, n=n)
                        q = bQ[:, :].rearrange("p (b s n) -> p b s n", s=2, n=n)
                        nc.vector.tensor_tensor(QL[L % 2][:, :, :].rearrange("p c (b n) -> p (c b) n", n=n),
                                                q[:, :, 1, :], e[:, :, 1, :], ALU.mult).then_inc(ql_ready, 1)
                        nc.vector.tensor_tensor(KL[L % 2][:, :], bK[:, :], LE[L % 2][:, :], ALU.mult)\
                            .then_inc(ql_ready, 1)

                    def level_scores(L):
                        n = 64 >> L
                        dve.wait_ge(level_done, L + 1)
                        if L == 0:
                            dve.wait_ge(sc_zero, 1)
                        else:
                            dve.wait_ge(sc_ready, 2 * L)
                        m = LM[:, L * 64:(L + 1) * 64].rearrange("p (o b n) -> p o b n", o=1, n=n)
                        for j in range(2):
                            to = SC[:, :, j, :].rearrange("p c (b s n) -> p c b s n", s=2, n=n)[:, :, :, 1, :]
                            of = ps[:, 4 + 2 * (L % 2) + j, :].rearrange("p (c b n) -> p c b n", c=NCH, n=n)
                            nc.vector.copy_predicated(to, m.broadcast_to([P, NCH, 64 // n, n]), of)\
                                .then_inc(sc_ready, 1)

                    def conv():
                        dve.wait_ge(proj_done, 4)
                        dve.wait_ge(st_zero, 2)
                        nc.vector.tensor_tensor(wide(XP[:, 3:3 + S]), pair(0), wide(RS[:, :]), ALU.mult)\
                            .then_inc(bank_free[0], 1)
                        dve.wait_ge(bank_free[0], 3)
                        nc.vector.tensor_scalar(XC[:, :], XP[:, 0:S], col(V_TAP), col(V_CB), ALU.mult, ALU.add)\
                            .then_inc(conv_step, 1)
                        for k in range(1, CONV):
                            dve.wait_ge(conv_step, k)
                            nc.vector.scalar_tensor_tensor(XC[:, :], XP[:, k:k + S], col(V_TAP + k), XC[:, :],
                                                           ALU.mult, ALU.add).then_inc(conv_step, 1)

                    level_in(0)
                    level_in(1)
                    dve.wait_ge(proj_done, 1)
                    nc.vector.tensor_tensor(wide(bQ[:, :]), pair(1), wide(RS[:, :]), ALU.mult)\
                        .then_inc(bank_free[1], 1)
                    for L in range(LEVELS):
                        level_keys(L)
                        if L >= 1:
                            level_scores(L - 1)
                        if L + 2 < LEVELS:
                            level_in(L + 2)
                        if L == 4:
                            conv()
                    cum = chunks(bCUM)
                    dve.wait_ge(e_ready, LEVELS)
                    dve.wait_ge(ql_ready, 2 * LEVELS)
                    nc.vector.tensor_tensor(chunks(bF), cum[:, :, P - 1:P].broadcast_to([P, NCH, P]), cum,
                                            ALU.subtract).then_inc(kx2_ready, 1)
                    dve.wait_ge(ec_ready, 1)
                    nc.vector.tensor_tensor(bT[:, :], bQ[:, :], EC[:, :], ALU.mult).then_inc(qe_ready, 1)
                    dve.wait_ge(qe_ready, 1)
                    nc.vector.tensor_tensor(bQ[:, :], bQ[:, :], bK[:, :], ALU.mult).then_inc(qk_ready, 1)
                    dve.wait_ge(kdec_ready, 1)
                    dve.wait_ge(level_done, LEVELS)
                    nc.vector.tensor_tensor(bB[:, :], bK[:, :], bF[:, :], ALU.mult).then_inc(ke_ready, 1)
                    level_scores(LEVELS - 1)
                    dve.wait_ge(keT_done, 1)
                    nc.vector.tensor_copy(wide(bM[:, :]), pair(3)).then_inc(ket_ready, 1)
                    dve.wait_ge(gelu_sq, 1)
                    nc.vector.tensor_scalar(GE[:, :], GE[:, :], 0.044715, 1.0, ALU.mult, ALU.add)\
                        .then_inc(gelu_part, 1)
                    dve.wait_ge(gelu_part, 1)
                    nc.vector.tensor_tensor(GE[:, :], GE[:, :], GT[:, :], ALU.mult).then_inc(gelu_in, 1)
                    dve.wait_ge(silu_th, 1)
                    nc.vector.tensor_tensor(bG[:, :], XP[:, 0:S], bG[:, :], ALU.mult).then_inc(dve_step, 1)
                    dve.wait_ge(gates_read, 2)
                    nc.vector.tensor_scalar(TR[:, :], TR[:, :], col(W_C1), None, ALU.mult).then_inc(la_ready, 1)
                    nc.vector.tensor_tensor(TI[:, :], TI[:, :], XC[:, :], ALU.mult).then_inc(dve_step, 1)
                    dve.wait_ge(upd_done, 1)
                    dve.wait_ge(st_zero, 1)
                    for c in range(NCH):
                        if c >= 1:
                            dve.wait_ge(st_ready, 2 * c)
                        for j in range(2):
                            r = slice(64 * j, 64 * j + 64)
                            upd = ps[r, 4 + c // 4, (c % 4) * P + 64 * j:(c % 4) * P + 64 * j + 64]
                            if c == 0:
                                ins = nc.vector.tensor_copy(ST[r, 0, r], upd)
                            else:
                                ins = nc.vector.scalar_tensor_tensor(ST[r, c, r], ST[r, c - 1, r],
                                                                     EC[r, (c + 1) * P - 1:(c + 1) * P], upd,
                                                                     ALU.mult, ALU.add)
                            ins.then_inc(st_ready, 1)
                    dve.wait_ge(diag_done, 1)
                    nc.vector.tensor_tensor(wide(bV[:, :]), pair(0), wide(bV[:, :]), ALU.mult).then_inc(od_ready, 1)
                    dve.wait_ge(od_ready, 1)
                    dve.wait_ge(o_done, 1)
                    nc.vector.tensor_tensor(wide(bCUM[:, :]), pair(3), wide(bV[:, :]), ALU.add).then_inc(o_ready, 1)
                    dve.wait_ge(gelu_th, 1)
                    nc.vector.tensor_tensor(GE[:, :], GE[:, :], GT[:, :], ALU.mult).then_inc(dve_step, 1)
                    dve.wait_ge(decay_ready, 2)
                    nc.vector.tensor_tensor(bK[:, :], XP[:, 0:S], XP[:, 0:S], ALU.mult).then_inc(dve_step, 1)
                    dve.wait_ge(dve_step, 4)
                    nc.vector.scalar_tensor_tensor(bK[:, :], bK[:, :], 1.0, TH[:, :], ALU.add, ALU.mult)\
                        .then_inc(dve_step, 1)
                    dve.wait_ge(dve_step, 5)
                    nc.vector.tensor_scalar(TH[:, :], bK[:, :], -1.0, 0.0, ALU.mult, ALU.max).then_inc(neg_ready, 1)
                    dve.wait_ge(orstd, 2)
                    nc.vector.scalar_tensor_tensor(bCUM[:, :], bCUM[:, :], col(V_HG), bF[:, :], ALU.mult, ALU.mult)\
                        .then_inc(dve_step, 1)
                    dve.wait_ge(dve_step, 6)
                    nc.vector.tensor_tensor(YD[:, bass.ds(pr, 1), :].rearrange("p o s -> p (o s)"),
                                            bCUM[:, :], bG[:, :], ALU.mult).then_inc(dve_step, 1)
                    dve.wait_ge(root_ready, 1)
                    nc.vector.tensor_tensor(TI[:, :], TI[:, :], TH[:, :], ALU.mult).then_inc(dve_step, 1)
                    dve.wait_ge(dve_step, 8)
                    nc.vector.tensor_tensor_scan(bB[:, :], XP[:, 0:S], TI[:, :], 0.0, ALU.mult, ALU.add)\
                        .then_inc(dve_step, 1)
                    dve.wait_ge(dve_step, 9)
                    nc.vector.tensor_tensor(YB[:, bass.ds(pr, 1), :].rearrange("p o s -> p (o s)"),
                                            bB[:, :], GE[:, :], ALU.mult).then_inc(dve_step, 1)

        SBQ = at_r("sb_q", 32, [P, PAIRS, S])
        SBK = at_r("sb_k", 40, [P, PAIRS, S])
        SBV = at_r("sb_v", 48, [P, PAIRS, TT, P])
        CQH = at_r("c_q_hi", 56, [P, 2, S], F32R)
        CQL = at_r("c_q_lo", 64, [P, 2, S], F32R)
        CKH = at_r("c_kv_hi", 72, [P, S], F32R)
        CKL = at_r("c_kv_lo", 76, [P, S], F32R)
        CQ = at_r("c_q", 80, [P, 2, S])
        CKV = at_r("c_kv", 88, [P, S])
        LSQ = [at_r("latent_sq0", 92, [P, S]), at_r("latent_sq1", 96, [P, S])]
        LRS = at_r("latent_rs", 100, [P, S])
        VF = [at_r(f"v_feature{i}", 16 + 4 * i, [P, S]) for i in range(2)]
        RTMP = at_r("rope_tmp", 24, [P, S])
        KRS = at_r("rope_key", 28, [P, S])
        KH = at_u("mla_k", 0, [P, 4, S])
        QH = at_u("mla_q", 16, [P, 4, S])
        MV = at_u("mla_v", 32, [P, PAIRS, TT, P])
        lat_read = sem("lat_read")
        lat_sq = sem("lat_sq")
        lat_rs = sem("lat_rs")
        lat_t = sem("lat_t")
        lat_hi = sem("lat_hi")
        lat_lo = sem("lat_lo")
        rope_part = sem("rope_part")
        key_rope = sem("key_rope")

        LAT_JOBS = ["cq0", "cq1", "ckv", "kr", "sbq0", "sbk0", "sum_q", "sbv0", "sum_kv", "sbq1", "vT_s0", "sbk1",
                    "sbv1", "qn0", "kn0", "qp0", "vv0", "vT_s1", "qp1", "qn1", "kn1", "vv1", "vT_m0", "vT_m1"]
        JOB = {name: j for j, name in enumerate(LAT_JOBS)}
        LAT_SLOTS = ["cq0", "cq1", "ckv", "kr", "sbq0", "sbk0", "sbv0", "sbq1", "sbk1", "sbv1", "mla0", "mla1"]
        LAT_SLOTS += ["out0", "out1"]
        SLOT = {name: n for n, name in enumerate(LAT_SLOTS)}
        SLOT_END = {name: JOB.get(name, JOB["vv0"] if name == "mla0" else JOB["vv1"]) for name in LAT_SLOTS[:-2]}
        MLA_N, MLA_PE, MLA_K, MLA_V = 0, P, 512, 640

        def latents(l):
            def mla_parts(l, n, pr):
                uq = raw[n % 2][:, 0:512].rearrange("p (k c) -> p k c", k=2)
                ukv = raw[n % 2][:, 512:768].rearrange("p (t j c) -> p t j c", t=2, j=2)
                parts = []
                for j in range(2):
                    c = (2 * pr + j) * (NOPE + ROPE)

                    def q_cols(a, width):
                        return w_uq[bass.ds(l * Q_LORA, Q_LORA), a:a + width].rearrange("(k p) c -> p k c", p=P)

                    parts += [(uq[:, :, 64 * j:64 * j + 64], q_cols(c, 64)),
                              (uq[:, :, P + 32 * j:P + 32 * j + 32], q_cols(c + 64, 32)),
                              (uq[:, :, P + 64 + 32 * j:P + 80 + 32 * j], q_cols(c + 80, 16)),
                              (uq[:, :, P + 80 + 32 * j:P + 96 + 32 * j], q_cols(c + 64, 16))]
                    for t in range(2):
                        c2 = (2 * pr + j) * (NOPE + HD) + 64 * t
                        parts.append((ukv[:, t, j, :], w_ukv[bass.ds(l * KV_LORA, KV_LORA), c2:c2 + 64]))
                return parts

            with nc.Block() as block:
                @block.sync
                def _(sp):
                    cols = {"cq0": C_CQ, "cq1": C_CQ + P, "ckv": C_CKV, "sbq0": C_SBQ, "sbq1": C_SBQ + P,
                            "sbk0": C_SBK, "sbk1": C_SBK + P, "sbv0": C_SBV, "sbv1": C_SBV + P}
                    for n, name in enumerate(LAT_SLOTS):
                        to = raw[n % 2][:, :].rearrange("p (k c) -> p k c", c=P)

                        def w_cols(c, width):
                            return w_in[bass.ds(l * D, D), c:c + width].rearrange("(k p) c -> p k c", p=P)

                        if n < 2:
                            continue
                        if name[:3] == "out":
                            m = int(name[-1])
                            parts = [(to, w_out[bass.ds(l * D, D), m * P:(m + 1) * P]
                                      .rearrange("(k p) c -> p k c", p=P))]
                        elif name in cols:
                            parts = [(to, w_cols(cols[name], P))]
                        elif name == "kr":
                            parts = []
                            for r in range(2):
                                parts += [(to[:, :, 64 * r:64 * r + 32], w_cols(C_ROPE, 32)),
                                          (to[:, :, 64 * r + 32:64 * r + 48], w_cols(C_ROPE + 16, 16)),
                                          (to[:, :, 64 * r + 48:64 * r + 64], w_cols(C_ROPE, 16))]
                        else:
                            parts = mla_parts(l, n, int(name[-1]))
                        load_slot(sp, n, parts)

                @block.gpsimd
                def _(pool):
                    dmas = [0, 0]
                    for n, name in enumerate(LAT_SLOTS):
                        if n < 2:
                            continue
                        dmas[n % 2] += 6 if name == "kr" else 12 if name.startswith("mla") else 1
                        jobs = SLOT_END[LAT_SLOTS[n - 2]]
                        split_slot(pool, n, dmas[n % 2], jobs, 768 if name.startswith("mla") else 1024)

                @block.tensor
                def _(pe):
                    for j, name in enumerate(LAT_JOBS):
                        if j == 0:
                            continue
                        p = j % 4
                        if j >= 4:
                            pe.wait_ge(bank_free[p], j // 4)
                        if name in SLOT:
                            project_slot(pe, SLOT[name], j, p)
                        elif name in ("sum_q", "sum_kv"):
                            q = name == "sum_q"
                            pe.wait_ge(lat_sq, 2 if q else 3)
                            for half in range(2):
                                at = slice(half * HALF, (half + 1) * HALF)
                                for k in range(2 if q else 1):
                                    last = nc.tensor.matmul(ps[:, 2 * p + half, :], ones[:, :], LSQ[k][:, at],
                                                            start=(k == 0), stop=(k == 1 or not q))
                            last.then_inc(proj_done, 1)
                        elif name[:2] == "vT":
                            src = VF[int(name[-1])]
                            pe.wait_ge(bank_free[JOB[("sbv" if name[3] == "s" else "vv") + name[-1]] % 4],
                                       JOB[("sbv" if name[3] == "s" else "vv") + name[-1]] // 4 + 1)
                            for c in range(TT):
                                last = nc.tensor.transpose(ps[:, 2 * p + c // 4, (c % 4) * P:(c % 4 + 1) * P],
                                                           src[:, c * P:(c + 1) * P], ident)
                            last.then_inc(proj_done, 1)
                        else:
                            kind, pr = name[:2], int(name[-1])
                            n = SLOT[f"mla{pr}"]
                            pe.wait_ge(slot_split, n - 1)
                            pe.wait_ge(lat_lo, 3)
                            off = {"qn": MLA_N, "qp": MLA_PE, "kn": MLA_K, "vv": MLA_V}[kind]
                            if kind in ("qn", "qp"):
                                last = product(pe, 2 * p, slot_lhs(n, off, 256),
                                               lambda k: (CQH[:, k, :], CQL[:, k, :]), 2)
                            else:
                                last = product(pe, 2 * p, slot_lhs(n, off), lambda k: (CKH[:, :], CKL[:, :]), 1)
                            last.then_inc(proj_done, 1)

                @block.scalar
                def _(act):
                    def read(name, to):
                        j = JOB[name]
                        act.wait_ge(proj_done, j)
                        return nc.scalar.activation(to, pair(j % 4), ACT.Copy)

                    def done(name, ins):
                        ins.then_inc(bank_free[JOB[name] % 4], 1)

                    exp_and_ln()
                    def square(name, k, t):
                        act.wait_ge(bank_free[JOB[name] % 4], JOB[name] // 4 + 1)
                        nc.scalar.activation(LSQ[k][:, :], t, ACT.Square).then_inc(lat_sq, 1)

                    def latent_rs(name, width):
                        p, n = JOB[name] % 4, JOB[name] // 4 + 1
                        act.wait_ge(proj_done, JOB[name])
                        nc.scalar.activation(wide(LRS[:, :]), pair(p), ACT.Ln, scale=1.0 / width,
                                             bias=eps[:, 0:1]).then_inc(bank_free[p], 1)
                        act.wait_ge(bank_free[p], n)
                        nc.scalar.activation(LRS[:, :], LRS[:, :], ACT.Exp, scale=-0.5).then_inc(lat_rs, 1)

                    square("cq0", 0, CQ[:, 0, :])
                    square("cq1", 1, CQ[:, 1, :])
                    latent_rs("sum_q", Q_LORA)
                    square("ckv", 0, CKV[:, :])
                    for k in range(2):
                        act.wait_ge(lat_t, k + 1)
                        nc.scalar.activation(CQH[:, k, :], CQ[:, k, :], ACT.Copy).then_inc(lat_hi, 1)
                    latent_rs("sum_kv", KV_LORA)
                    act.wait_ge(lat_t, 3)
                    nc.scalar.activation(CKH[:, :], CKV[:, :], ACT.Copy).then_inc(lat_hi, 1)
                    done("vT_s0", read("vT_s0", SBV[:, 0, :, :].rearrange("p (b c) t -> p b (c t)", b=2)))
                    for pr in range(PAIRS):
                        for name, to in ((f"qn{pr}", QH), (f"kn{pr}", KH)):
                            j = JOB[name]
                            act.wait_ge(proj_done, j)
                            nc.scalar.activation(wide(to[0:64, 2 * pr, :]), pair(j % 4, slice(0, 64)), ACT.Copy)\
                                .then_inc(lat_read, 1)
                            act.wait_ge(lat_read, 6 * pr + (1 if to is QH else 2))
                            nc.scalar.activation(wide(to[0:64, 2 * pr + 1, :]), pair(j % 4, slice(64, P)), ACT.Copy)\
                                .then_inc(bank_free[j % 4], 1)
                        done(f"vv{pr}", read(f"vv{pr}", wide(VF[pr][:, :])))
                        if pr == 0:
                            act.wait_ge(key_rope, 2)
                            for hd in range(4):
                                nc.scalar.activation(KH[64:96, hd, :], RT[64:96, :], ACT.Copy).then_inc(lat_read, 1)
                            done("vT_s1", read("vT_s1", SBV[:, 1, :, :].rearrange("p (b c) t -> p b (c t)", b=2)))
                    for pr in range(PAIRS):
                        done(f"vT_m{pr}", read(f"vT_m{pr}", MV[:, pr, :, :].rearrange(
                            "p (b c) t -> p b (c t)", b=2)))
                @block.vector
                def _(dve):
                    def read(name, to):
                        j = JOB[name]
                        if j:
                            dve.wait_ge(proj_done, j)
                        nc.vector.tensor_tensor(wide(to), pair(j % 4), wide(RS[:, :]), ALU.mult)\
                            .then_inc(bank_free[j % 4], 1)

                    read("cq0", CQ[:, 0, :])
                    read("cq1", CQ[:, 1, :])
                    read("ckv", CKV[:, :])
                    cos, sin = RT[0:32, :], RT[32:64, :]
                    dve.wait_ge(proj_done, JOB["kr"])
                    nc.vector.tensor_tensor(wide(KRS[0:64, :]), pair(3, slice(0, 64)), wide(RS[0:64, :]), ALU.mult)\
                        .then_inc(bank_free[3], 1)
                    dve.wait_ge(bank_free[3], 1)
                    nc.vector.tensor_tensor(RT[64:96, :], KRS[0:32, :], cos, ALU.mult).then_inc(rope_part, 1)
                    nc.vector.tensor_tensor(RTMP[64:96, :], KRS[32:64, :], sin, ALU.mult).then_inc(key_rope, 1)
                    dve.wait_ge(rope_part, 1)
                    dve.wait_ge(key_rope, 1)
                    nc.vector.tensor_tensor(RT[64:96, :], RT[64:96, :], RTMP[64:96, :], ALU.add).then_inc(key_rope, 1)
                    read("sbq0", SBQ[:, 0, :])
                    read("sbk0", SBK[:, 0, :])
                    dve.wait_ge(lat_rs, 1)
                    for k in range(2):
                        nc.vector.scalar_tensor_tensor(CQ[:, k, :], CQ[:, k, :], vecs[:, V_QN + k:V_QN + k + 1],
                                                       LRS[:, :], ALU.mult, ALU.mult).then_inc(lat_t, 1)
                    read("sbv0", VF[0][:, :])
                    for k in range(2):
                        dve.wait_ge(lat_hi, k + 1)
                        nc.vector.tensor_tensor(CQL[:, k, :], CQ[:, k, :], CQH[:, k, :].bitcast(F32),
                                                ALU.subtract).then_inc(lat_lo, 1)
                    dve.wait_ge(lat_rs, 2)
                    nc.vector.scalar_tensor_tensor(CKV[:, :], CKV[:, :], vecs[:, V_KVN:V_KVN + 1],
                                                   LRS[:, :], ALU.mult, ALU.mult).then_inc(lat_t, 1)
                    read("sbq1", SBQ[:, 1, :])
                    dve.wait_ge(lat_hi, 3)
                    nc.vector.tensor_tensor(CKL[:, :], CKV[:, :], CKH[:, :].bitcast(F32),
                                            ALU.subtract).then_inc(lat_lo, 1)
                    read("sbk1", SBK[:, 1, :])
                    read("sbv1", VF[1][:, :])
                    n = 1
                    for pr in range(PAIRS):
                        j = JOB[f"qp{pr}"]
                        dve.wait_ge(proj_done, j)
                        for i in range(2):
                            if pr + i:
                                dve.wait_ge(rope_part, n)
                            else:
                                dve.wait_ge(key_rope, 2)
                            nc.vector.tensor_tensor(wide(QH[64:96, 2 * pr + i, :]), pair(j % 4, slice(32 * i, 32 * i + 32)),
                                                    wide(cos), ALU.mult).then_inc(rope_part, 1)
                            ins = nc.vector.tensor_tensor(wide(RTMP[64:96, :]),
                                                          pair(j % 4, slice(64 + 32 * i, 96 + 32 * i)), wide(sin),
                                                          ALU.mult)
                            if i == 0:
                                ins.then_inc(rope_part, 1)
                                n += 2
                                dve.wait_ge(rope_part, n)
                            else:
                                ins.then_inc(bank_free[j % 4], 1)
                                n += 1
                                dve.wait_ge(rope_part, n)
                                dve.wait_ge(bank_free[j % 4], j // 4 + 1)
                            nc.vector.tensor_tensor(QH[64:96, 2 * pr + i, :], QH[64:96, 2 * pr + i, :],
                                                    RTMP[64:96, :], ALU.add).then_inc(rope_part, 1)
                            n += 1

        TILE_ORDER = list(range(1, TT, 2)) + list(range(TT - 2, -1, -2))
        SQP = at_u("sb_q_pair", 40, [P, S])
        SKP = at_u("sb_k_pair", 44, [P, S])
        QHP = [at_u(f"mla_q_pair{i}", 48 + 4 * i, [P, S]) for i in range(2)]
        KHP = [at_u(f"mla_k_pair{i}", 56 + 4 * i, [P, S]) for i in range(2)]
        ZS = [at_r(f"sb_z{i}", 56 + 4 * i, [P, S]) for i in range(2)]
        TA = [at_r(f"sb_soft{i}", 64 + 4 * i, [P, S]) for i in range(2)]
        RW = [at_r(f"sb_weight{i}", 72 + 4 * i, [P, S]) for i in range(2)]
        PM = [at_r(f"mla_prob{i}", 80 + 4 * i, [P, S]) for i in range(2)]
        PTS = [at_r(f"sb_weight_t{i}", 88 + 4 * i, [P, TT, P]) for i in range(2)]
        PTM = [at_r(f"mla_prob_t{i}", 96 + 4 * i, [P, TT, P]) for i in range(2)]
        sb_copied = sem("sb_copied")
        mla_copied = sem("mla_copied")
        sb_scored = sem("sb_scored")
        mla_scored = sem("mla_scored")
        zs_ready = sem("zs_ready")
        soft_step = sem("soft_step")
        soft_ready = sem("soft_ready")
        sp_ready = sem("sp_ready")
        cum_sp_ready = sem("cum_sp_ready")
        lw_ready = sem("lw_ready")
        w_ready = sem("w_ready")
        m_masked = sem("m_masked")
        nm_part = sem("nm_part")
        nm_ready = sem("nm_ready")
        pm_ready = sem("pm_ready")
        unit_done = sem("unit_done")
        unit_read = sems("unit_read", 3)
        pv_done = sem("pv_done")
        pv_read = sem("pv_read")
        rinv = sem("rinv")

        JOBS = 2 * TT

        def tile_of(i):
            return TILE_ORDER[i // 2]

        def keys_of(i):
            return tile_of(i) + 1

        UNITS = []
        for s_ in range(JOBS + 2):
            for kind, i in (("m", s_ - 1), ("s", s_ - 2)):
                if 0 <= i < JOBS:
                    UNITS += [(kind, i, b) for b in range(0, keys_of(i), 4)]

        def units_of(kind, i):
            return [u for u, unit in enumerate(UNITS) if unit[:2] == (kind, i)]

        def zs_count(i):
            return sum(2 if keys_of(j) > 1 else 1 for j in range(i + 1))

        def group_ac(pr):
            with nc.Block() as block:
                @block.tensor
                def _(pe):
                    def transposes(kind, i, src):
                        for u in units_of(kind, i):
                            if u >= 3:
                                pe.wait_ge(unit_read[u % 3], u // 3)
                            b0 = UNITS[u][2]
                            for b in range(b0, min(b0 + 4, keys_of(i))):
                                last = nc.tensor.transpose(ps[:, u % 3, (b - b0) * P:(b - b0 + 1) * P],
                                                           src[:, b * P:(b + 1) * P], ident)
                            last.then_inc(unit_done, 1)

                    def values(kind, i, pt, v, col):
                        for u in units_of(kind, i):
                            pe.wait_ge(unit_read[u % 3], u // 3 + 1)
                        for b in range(keys_of(i)):
                            last = nc.tensor.matmul(ps[:, 3, col:col + HD], pt[:, b, :],
                                                    v[:, bass.ds(pr, 1), b, (i % 2) * HD:(i % 2 + 1) * HD]
                                                    .rearrange("p o c -> p (o c)"),
                                                    start=(b == 0), stop=(b == keys_of(i) - 1))
                        return last

                    pe.wait_ge(sb_copied, 2)
                    for s in range(JOBS + 3):
                        if s < JOBS:
                            n = keys_of(s) * P
                            q_at = slice(tile_of(s) * P, (tile_of(s) + 1) * P)
                            rows = slice(64 * (s % 2), 64 * (s % 2) + 64)
                            if s >= 1:
                                pe.wait_ge(zs_ready, zs_count(s - 1))
                            for a in range(0, n, HALF):
                                e = min(n, a + HALF)
                                last = nc.tensor.matmul(ps[:, 4 + a // HALF, 0:e - a], SQP[rows, q_at],
                                                        SKP[rows, a:e], start=True, stop=True)
                            last.then_inc(sb_scored, 1)
                        if s >= 3:
                            pe.wait_ge(pv_read, s - 2)
                        if 2 <= s < JOBS + 2:
                            last = values("m", s - 2, PTM[s % 2], MV, 0)
                            if s == 2:
                                last.then_inc(pv_done, 1)
                        if 1 <= s <= JOBS:
                            pe.wait_ge(pm_ready, s)
                            transposes("m", s - 1, PM[(s - 1) % 2])
                        if s < JOBS:
                            if s >= 1:
                                pe.wait_ge(pm_ready, s)
                            else:
                                pe.wait_ge(mla_copied, 4)
                            for a in range(0, n, HALF):
                                e = min(n, a + HALF)
                                last = nc.tensor.matmul(ps[:, 6 + a // HALF, 0:e - a], QHP[s % 2][0:96, q_at],
                                                        KHP[s % 2][0:96, a:e], start=True, stop=True)
                            last.then_inc(mla_scored, 1)
                        if s >= 3:
                            values("s", s - 3, PTS[(s - 3) % 2], SBV, HD).then_inc(pv_done, 1)
                        if 2 <= s < JOBS + 2:
                            pe.wait_ge(w_ready, s - 1)
                            transposes("s", s - 2, RW[s % 2])

                @block.vector
                def _(dve):
                    nc.vector.tensor_copy(SQP[:, :], SBQ[:, bass.ds(pr, 1), :].rearrange("p o s -> p (o s)"))\
                        .then_inc(sb_copied, 1)
                    nc.vector.tensor_copy(SKP[:, :], SBK[:, bass.ds(pr, 1), :].rearrange("p o s -> p (o s)"))\
                        .then_inc(sb_copied, 1)
                    for i in range(2):
                        nc.vector.tensor_copy(KHP[i][0:96, :], KH[0:96, bass.ds(pr * 2 + i, 1), :]
                                              .rearrange("p o s -> p (o s)")).then_inc(mla_copied, 1)
                    for s in range(JOBS + 4):
                        if s >= 3:
                            dve.wait_ge(pv_done, s - 2)
                            if s - 3 < JOBS:
                                i = s - 3
                                nc.vector.reciprocal(RSUM[:, i % 4, 1:2], RSUM[:, i % 4, 0:1]).then_inc(rinv, 1)
                                dve.wait_ge(rinv, i + 1)
                                ins = nc.vector.tensor_scalar(
                                    YA[:, tile_of(i), bass.ds(pr * P + (i % 2) * HD, HD)], ps[:, 3, 0:HD],
                                    RSUM[:, i % 4, 1:2], None, ALU.mult)
                            if s >= 4:
                                if s - 3 < JOBS:
                                    ins.then_inc(dve_step, 1)
                                i = s - 4
                                ins = nc.vector.tensor_copy(YC[:, tile_of(i), bass.ds(pr * P + (i % 2) * HD, HD)],
                                                            ps[:, 3, HD:2 * HD])
                            ins.then_inc(pv_read, 1)
                        if s < JOBS:
                            n = keys_of(s) * P
                            z, sc = ZS[s % 2], pair(2).rearrange("p b n -> p (b n)")
                            dve.wait_ge(sb_scored, s + 1)
                            if s >= 2:
                                dve.wait_ge(lw_ready, s - 1)
                            if n > P:
                                nc.vector.tensor_scalar(z[:, 0:n - P], sc[:, 0:n - P], SB_SCALE, None, ALU.mult)\
                                    .then_inc(zs_ready, 1)
                            nc.vector.scalar_tensor_tensor(z[:, n - P:n], sc[:, n - P:n], SB_SCALE,
                                                           CO[:, K_NEGS:K_NEGS + P], ALU.mult, ALU.add)\
                                .then_inc(zs_ready, 1)
                        if 1 <= s <= JOBS:
                            i = s - 1
                            n = keys_of(i) * P
                            t, z, r = TA[i % 2], ZS[i % 2], RW[i % 2]
                            dve.wait_ge(soft_ready, i + 1)
                            nc.vector.scalar_tensor_tensor(t[:, 0:n], z[:, 0:n], 0.0, t[:, 0:n], ALU.max, ALU.add)\
                                .then_inc(sp_ready, 1)
                            dve.wait_ge(sp_ready, i + 1)
                            if i >= 2:
                                dve.wait_ge(unit_done, units_of("s", i - 2)[-1] + 1)
                            nc.vector.tensor_tensor_scan(r[:, 0:n][:, ::-1], ones[:, 0:1].broadcast_to([P, n]), t[:, 0:n][:, ::-1], 0.0,
                                                         ALU.mult, ALU.add).then_inc(cum_sp_ready, 1)
                        if s < JOBS:
                            n = keys_of(s) * P
                            sc = pair(3).rearrange("p b n -> p (b n)")
                            dve.wait_ge(mla_scored, s + 1)
                            nc.vector.tensor_tensor(sc[:, n - P:n], sc[:, n - P:n], CO[:, K_NEGC:K_NEGC + P],
                                                    ALU.add).then_inc(m_masked, 1)
                            dve.wait_ge(m_masked, s + 1)
                            if s >= 2:
                                dve.wait_ge(pm_ready, s - 1)
                            nc.vector.tensor_reduce(NM[:, s % 2, 0:1], sc[:, 0:n], AX.X, ALU.max, negate=True)\
                                .then_inc(nm_part, 1)
                            dve.wait_ge(nm_part, s + 1)
                            nc.vector.tensor_scalar(NM[:, s % 2, 1:2], NM[:, s % 2, 0:1], MLA_SCALE, None, ALU.mult)\
                                .then_inc(nm_ready, 1)
                        if 2 <= s < JOBS + 2:
                            i = s - 2
                            if i >= 2:
                                dve.wait_ge(pv_done, i)
                            for u in units_of("s", i):
                                dve.wait_ge(unit_done, u + 1)
                                b0 = UNITS[u][2]
                                b1 = min(b0 + 4, keys_of(i))
                                nc.vector.tensor_copy(PTS[i % 2][:, b0:b1, :].rearrange("p b c -> p (b c)"),
                                                      ps[:, u % 3, 0:(b1 - b0) * P]).then_inc(unit_read[u % 3], 1)

                @block.gpsimd
                def _(pool):
                    for i in range(JOBS):
                        n = keys_of(i) * P
                        pool.wait_ge(cum_sp_ready, i + 1)
                        nc.gpsimd.tensor_tensor(RW[i % 2][:, 0:n], ZS[i % 2][:, 0:n], RW[i % 2][:, 0:n],
                                                ALU.subtract).then_inc(lw_ready, 1)

                @block.scalar
                def _(act):
                    exp_and_ln()
                    for i in range(2):
                        nc.scalar.activation(QHP[i][0:96, :], QH[0:96, bass.ds(pr * 2 + i, 1), :]
                                             .rearrange("p o s -> p (o s)"), ACT.Copy).then_inc(mla_copied, 1)
                    for s in range(JOBS + 2):
                        if s >= 2:
                            i = s - 2
                            r = RW[i % 2][:, 0:keys_of(i) * P]
                            act.wait_ge(lw_ready, i + 1)
                            nc.scalar.activation(r, r, ACT.Exp).then_inc(w_ready, 1)
                        if s < JOBS:
                            n = keys_of(s) * P
                            t = TA[s % 2][:, 0:n]
                            act.wait_ge(zs_ready, zs_count(s))
                            if s >= 2:
                                act.wait_ge(cum_sp_ready, s - 1)
                            nc.scalar.activation(t, ZS[s % 2][:, 0:n], ACT.Abs).then_inc(soft_step, 1)
                            act.wait_ge(soft_step, 2 * s + 1)
                            nc.scalar.activation(t, t, ACT.Exp, scale=-1.0).then_inc(soft_step, 1)
                            act.wait_ge(soft_step, 2 * s + 2)
                            nc.scalar.activation(t, t, ACT.Ln, bias=1.0).then_inc(soft_ready, 1)
                        if 1 <= s <= JOBS:
                            i = s - 1
                            if i >= 2:
                                act.wait_ge(pv_done, i - 1)
                            for u in units_of("m", i):
                                act.wait_ge(unit_done, u + 1)
                                b0 = UNITS[u][2]
                                b1 = min(b0 + 4, keys_of(i))
                                nc.scalar.activation(PTM[i % 2][:, b0:b1, :].rearrange("p b c -> p (b c)"),
                                                     ps[:, u % 3, 0:(b1 - b0) * P], ACT.Copy)\
                                    .then_inc(unit_read[u % 3], 1)
                        if s < JOBS:
                            act.wait_ge(nm_ready, s + 1)
                            if s >= 2:
                                act.wait_ge(unit_done, units_of("m", s - 2)[-1] + 1)
                            if s >= 4:
                                act.wait_ge(rinv, s - 3)
                            nc.scalar.activation(PM[s % 2][:, 0:n], pair(3).rearrange("p b n -> p (b n)")[:, 0:n],
                                                 ACT.Exp, scale=MLA_SCALE, bias=NM[:, s % 2, 1:2],
                                                 accum_out=RSUM[:, s % 4, 0:1]).then_inc(pm_ready, 1)

        SQ2 = [at_r(f"sq2_{i}", 64 + 4 * i, [P, S]) for i in range(2)]
        ACC2 = at_r("acc2", 72, [P, S])
        BRS = at_r("b_rs", 76, [P, S])
        BT = [at_r(f"b_t{i}", 80 + 4 * i, [P, S]) for i in range(2)]
        U2H = at_r("u2_hi", 0, [P, KT, S], F32R)
        U2L = [at_r(f"u2_lo{k}", 80 + 4 * k, [P, S], F32R) for k in range(6)] + \
              [at_u(f"u2_lo{k}", 4 * (k - 6), [P, S], F32R) for k in range(6, KT)]
        HIDH = [at_r("hidden_hi0", 64, [P, 2, S], F32R), at_u("hidden_hi1", 8, [P, 2, S], F32R)]
        HIDL = [at_r("hidden_lo0", 72, [P, 2, S], F32R), at_u("hidden_lo1", 16, [P, 2, S], F32R)]
        HT = [at_u(f"hidden{i}", 24 + 4 * i, [P, S]) for i in range(2)]
        DRAW = [at_u(f"down_raw{i}", 32 + 4 * i, [P, D]) for i in range(2)]
        DHI = [at_u(f"down_hi{i}", 40 + 4 * i, [P, D], F32R) for i in range(2)]
        DLO = [at_u(f"down_lo{i}", 48 + 4 * i, [P, D], F32R) for i in range(2)]
        LHI = [at_r(f"last_hi{i}", 4 * i, [P, D], F32R) for i in range(2)]
        LLO = [at_r(f"last_lo{i}", 8 + 4 * i, [P, D], F32R) for i in range(2)]
        SQ3 = [at_r(f"sq3_{i}", 80 + 4 * i, [P, S]) for i in range(2)]
        ACC3 = at_r("acc3", 88, [P, S])
        GSQ = at_r("group_squares", 80, [P, 2 * TT, GROUP_W])
        h_loaded = sem("h_loaded")
        vecs_loaded = sem("vecs_loaded")
        group_sq = sem("group_sq")
        c_sq = sem("c_sq")
        group_part = sem("group_part")
        group_rstd = sem("group_rstd")
        group_scaled = sem("group_scaled")
        mix_hi = sem("mix_hi")
        mix_lo = sem("mix_lo")
        mixD_lo = sem("mixD_lo")
        b_sq = sem("b_sq")
        b_rstd = sem("b_rstd")
        b_t = sem("b_t")
        down_loaded = sems("down_loaded", 2)
        down_hi = sem("down_hi")
        down_split = sem("down_split")
        down_done = sem("down_done")
        silu_done = sem("silu_done")
        ht_ready = sem("ht_ready")
        norm2 = norm_sems("norm2")
        norm3 = norm_sems("norm3")
        hid_hi = sem("hid_hi")
        hid_lo = sem("hid_lo")

        J_B, J_OUT, J_GATE0, J_NORM, J_FFN = 0, 5, 13, 14, 14
        CHUNKS = FFN // 256
        AC_TILES = [(1, YA, 0, 0, 0), (2, YA, 0, 1, 1), (3, YC, 1, 0, 4), (4, YC, 1, 1, 5)]

        def ffn_pair(q, i=None):
            return (J_GATE0 if is_first(i) and q == 0 else J_FFN + q) % 4

        def is_first(i):
            return isinstance(i, int) and i == 0

        def ffn_used(i, q):
            if is_first(i):
                return (J_GATE0 if q == 0 else J_FFN + q) // 4
            return 3 * (i - 1) + (J_FFN + 4 + q) // 4

        def down_read(i):
            return bank_free[ffn_pair(3)], 3 * i + (J_FFN + 11) // 4 + 2

        def ln2(m):
            return vecs[:, V_LN2 + m:V_LN2 + m + 1]

        def output_ffn(l):
            def load_gate_up(sp, i, q):
                src = (w_gate, w_up)[q % 2]
                to = raw[q % 2][:, :].rearrange("p (k c) -> p k c", c=P)
                sp.wait_ge(slot_split, 4 * i + (KT + q - 3))
                sp.dma_start(to, src[bass.ds(l * D, D), bass.ds(i * 256 + (q // 2) * P, P)]
                             .rearrange("(k p) c -> p k c", p=P)).then_inc(raw_loaded[q % 2], 16)

            def load_down(sp, i, t):
                sp.dma_start(DRAW[t][:, :], w_down[bass.ds(l * FFN + i * 256 + t * P, P), :])\
                    .then_inc(down_loaded[t], 16)

            def split_gate_up(pool, i, q):
                pool.wait_ge(raw_loaded[q % 2], 32 * i + 16 * (KT // 2 + q // 2))
                pool.wait_ge(proj_done, J_GATE0 + q - 1 if is_first(i) and q < 2 else 4 * i + (J_FFN + q - 1))
                nc.gpsimd.tensor_tensor(whi[q % 2][:, :], raw[q % 2][:, :],
                                        ones[:, 0:1].broadcast_to([P, 1024]), ALU.mult).then_inc(hi_split, 1)
                pool.wait_ge(hi_split, 4 * i + (KT + q - 1))
                nc.gpsimd.tensor_tensor(wlo[q % 2][:, :], raw[q % 2][:, :], whi[q % 2][:, :].bitcast(F32),
                                        ALU.subtract).then_inc(slot_split, 1)

            def split_down(pool, i, t):
                pool.wait_ge(down_loaded[t], 16 * i + 16)
                pool.wait_ge(*down_read(i - 1))
                nc.gpsimd.tensor_tensor(DHI[t][:, :], DRAW[t][:, :],
                                        ones[:, 0:1].broadcast_to([P, 1024]), ALU.mult).then_inc(down_hi, 1)
                pool.wait_ge(down_hi, 2 * i + (t + 1))
                nc.gpsimd.tensor_tensor(DLO[t][:, :], DRAW[t][:, :], DHI[t][:, :].bitcast(F32),
                                        ALU.subtract).then_inc(down_split, 1)

            def pe_gate_up(pe, i, q, before_k=None):
                p = ffn_pair(q, i)
                pe.wait_ge(bank_free[p], ffn_used(i, q))
                pe.wait_ge(slot_split, 4 * i + (KT + q - 1))
                last = product(pe, 2 * p, slot_lhs(q), lambda k: (U2H[:, k, :], U2L[k][:, :]), KT, before_k)
                last.then_inc(proj_done, 1)

            def pe_down(pe, i, b, last_chunk=0):
                pe.wait_ge(down_split, 2 * i + 2)
                pe.wait_ge(hid_lo, 2 * i + 2)
                for m in range(KT):
                    p = ffn_pair(4 + m)
                    pe.wait_ge(bank_free[p], ffn_used(i + 1, 4 + m) - last_chunk)
                    hi, lo = (LHI, LLO) if last_chunk else (DHI, DLO)
                    last = product(pe, 2 * p, lambda k: (hi[k][:, m * P:(m + 1) * P], lo[k][:, m * P:(m + 1) * P]),
                                   lambda k: (HIDH[b][:, k, :], HIDL[b][:, k, :]), 2)
                    last.then_inc(down_done, 1)

            def act_chunk(act, i, b, first=False):
                for t in range(2):
                    pg = ffn_pair(2 * t, i)
                    act.wait_ge(bank_free[pg], ffn_used(i, 2 * t) + 1)
                    nc.scalar.activation(HT[t][:, :], HT[t][:, :], ACT.Silu).then_inc(silu_done, 1)
                    act.wait_ge(ht_ready, 2 * i + (t + 1))
                    if not first:
                        act.wait_ge(*down_read(i - 2))
                    nc.scalar.activation(HIDH[b][:, t, :], HT[t][:, :], ACT.Copy).then_inc(hid_hi, 1)

            def dve_chunk(dve, i, b, first=False):
                for t in range(2):
                    pg, pu = ffn_pair(2 * t, i), ffn_pair(2 * t + 1)
                    dve.wait_ge(proj_done, 4 * i + (J_FFN + 2 * t + 1))
                    if not first:
                        dve.wait_ge(hid_lo, 2 * i + (t - 1))
                    nc.vector.tensor_tensor(wide(HT[t][:, :]), pair(pg), wide(RS[:, :]), ALU.mult)\
                        .then_inc(bank_free[pg], 1)
                    dve.wait_ge(proj_done, 4 * i + (J_FFN + 2 * t + 2))
                    dve.wait_ge(silu_done, 2 * i + (t + 1))
                    nc.vector.tensor_tensor(wide(HT[t][:, :]), pair(pu), wide(HT[t][:, :]), ALU.mult)\
                        .then_inc(bank_free[pu], 1)
                    dve.wait_ge(bank_free[pu], ffn_used(i, 2 * t + 1) + 1)
                    nc.vector.tensor_tensor(HT[t][:, :], HT[t][:, :], RS[:, :], ALU.mult).then_inc(ht_ready, 1)
                    dve.wait_ge(hid_hi, 2 * i + (t + 1))
                    nc.vector.tensor_tensor(HIDL[b][:, t, :], HT[t][:, :], HIDH[b][:, t, :].bitcast(F32),
                                            ALU.subtract).then_inc(hid_lo, 1)

            def u_at(m):
                return uhi[:, m, :], ulo[:, m, :]

            def dve_down(dve, i, after=None):
                for m in range(KT):
                    p = ffn_pair(4 + m)
                    dve.wait_ge(down_done, KT * i + (m + 1))
                    nc.vector.tensor_tensor(wide(h[:, m, :]), pair(p), wide(h[:, m, :]), ALU.add)\
                        .then_inc(bank_free[p], 1)
                    if after is not None and m >= 1:
                        after(m - 1)

            with nc.Block() as block:
                @block.sync
                def _(sp):
                    for k in range(KT):
                        sp.dma_start(h[:, k, :], h_dram[k * P:(k + 1) * P, :]).then_inc(h_loaded, 16)
                    for m in range(2, KT):
                        src = w_out[bass.ds(l * D, D), m * P:(m + 1) * P].rearrange("(k p) c -> p k c", p=P)
                        load_slot(sp, m, [(raw[m % 2][:, :].rearrange("p (k c) -> p k c", c=P), src)])
                    for q in range(4):
                        load_gate_up(sp, 0, q)
                    sp.wait_ge(proj_done, J_OUT + KT)
                    with sp.Fori(0, (CHUNKS - 1) // 2) as r:
                        for b in range(2):
                            i = 2 * r + (b + 1)
                            load_gate_up(sp, i, 0)
                            load_gate_up(sp, i, 1)
                            load_down(sp, i - 1, 0)
                            load_down(sp, i - 1, 1)
                            load_gate_up(sp, i, 2)
                            load_gate_up(sp, i, 3)
                    sp.wait_ge(down_split, 2 * (CHUNKS - 1))
                    for t in range(2):
                        load_down(sp, CHUNKS - 1, t)
                    sp.wait_ge(slot_split, KT - 2 + 4 * CHUNKS)
                    load_bd_slots(sp, (DEPTH - 1) * D)
                    sp.dma_start(vecs[:, :], vec_table[bass.ds((l + 1) * P, P), :]).then_inc(vecs_loaded, 16)
                    for m in range(KT):
                        sp.wait_ge(bank_free[ffn_pair(4 + m)], ffn_used(CHUNKS, 4 + m))
                        sp.dma_start(h_rows[m], h[:, m, :]).then_inc(h_moved, 16)
                    sp.wait_ge(h_moved, 16 * KT)

                @block.gpsimd
                def _(pool):
                    for t in range(PAIRS):
                        pool.wait_ge(mix_hi, t + 1)
                        nc.gpsimd.tensor_tensor(ulo[:, 6 + t, :], YD[:, t, :], uhi[:, 6 + t, :].bitcast(F32),
                                                ALU.subtract).then_inc(mixD_lo, 1)
                    for m in range(2, KT):
                        split_slot(pool, m, m // 2, J_OUT + m - 1)
                        norm_pool(pool, norm2, m - 2, SQ2, ACC2)
                    for q in range(2):
                        split_gate_up(pool, 0, q)
                    norm_pool(pool, norm2, KT - 2, SQ2, ACC2)
                    norm_pool(pool, norm2, KT - 1, SQ2, ACC2)
                    for q in range(2, 4):
                        split_gate_up(pool, 0, q)
                    with pool.Fori(0, (CHUNKS - 1) // 2) as r:
                        for b in range(2):
                            i = 2 * r + (b + 1)
                            split_gate_up(pool, i, 0)
                            split_gate_up(pool, i, 1)
                            split_down(pool, i - 1, 0)
                            split_down(pool, i - 1, 1)
                            split_gate_up(pool, i, 2)
                            split_gate_up(pool, i, 3)
                    pool.wait_ge(proj_done, J_FFN + 4 * CHUNKS)
                    for t in range(2):
                        pool.wait_ge(down_loaded[t], 16 * CHUNKS)
                        nc.gpsimd.tensor_tensor(LHI[t][:, :], DRAW[t][:, :], ones[:, 0:1].broadcast_to([P, D]),
                                                ALU.mult).then_inc(down_hi, 1)
                        pool.wait_ge(down_hi, 2 * (CHUNKS - 1) + t + 1)
                        nc.gpsimd.tensor_tensor(LLO[t][:, :], DRAW[t][:, :], LHI[t][:, :].bitcast(F32),
                                                ALU.subtract).then_inc(down_split, 1)
                    for n in range(2):
                        pool.wait_ge(raw_loaded[n], 16 * (KT // 2 + 2 * CHUNKS))
                        nc.gpsimd.tensor_tensor(whi[n][:, :], raw[n][:, :], ones[:, 0:1].broadcast_to([P, 1024]),
                                                ALU.mult).then_inc(hi_split, 1)
                        pool.wait_ge(hi_split, KT - 2 + 4 * CHUNKS + n + 1)
                        nc.gpsimd.tensor_tensor(wlo[n][:, :], raw[n][:, :], whi[n][:, :].bitcast(F32),
                                                ALU.subtract).then_inc(slot_split, 1)
                    for m in range(KT):
                        norm_pool(pool, norm3, m, SQ3, ACC3)

                @block.tensor
                def _(pe):
                    for j, y, g, half, _ in AC_TILES:
                        if j == J_B + 1:
                            pe.wait_ge(b_sq, 2)
                            for at in range(2):
                                for t in range(2):
                                    last = nc.tensor.matmul(ps[:, 2 * J_B + at, :], ones[:, :],
                                                            SQ2[t][:, at * HALF:(at + 1) * HALF],
                                                            start=(t == 0), stop=(t == 1))
                            last.then_inc(proj_done, 1)
                        pe.wait_ge(group_scaled, g + 1)
                        if j >= 4:
                            pe.wait_ge(bank_free[j % 4], j // 4)
                        for t in range(TT):
                            last = nc.tensor.transpose(ps[:, 2 * (j % 4) + t // 4, (t % 4) * P:(t % 4 + 1) * P],
                                                       y[:, t, half * P:(half + 1) * P], ident)
                        last.then_inc(proj_done, 1)
                    tile_job = {tile: j for j, _, _, _, tile in AC_TILES}

                    def mix_ready(tile):
                        if tile in tile_job:
                            j = tile_job[tile]
                            pe.wait_ge(bank_free[j % 4], j // 4 + 1)
                        elif tile >= 6:
                            pe.wait_ge(mixD_lo, tile - 5)
                        else:
                            pe.wait_ge(mix_lo, tile - 1)

                    for m in range(KT):
                        j = J_OUT + m
                        pe.wait_ge(bank_free[j % 4], j // 4)
                        if m == 0:
                            project_slot(pe, m, j, j % 4, mix_ready, [6, 7, 0, 1, 4, 5, 2, 3])
                        else:
                            project_slot(pe, m, j, j % 4)
                    pe_gate_up(pe, 0, 0, lambda k: pe.wait_ge(norm2[3], k + 1))
                    pe.wait_ge(bank_free[J_NORM % 4], J_NORM // 4)
                    norm_pe(pe, norm2, ACC2, J_NORM % 4, proj_done)
                    for q in range(1, 4):
                        pe_gate_up(pe, 0, q)
                    with pe.Fori(0, (CHUNKS - 1) // 2) as r:
                        for b in range(2):
                            i = 2 * r + (b + 1)
                            for q in range(4):
                                pe_gate_up(pe, i, q)
                            pe_down(pe, i - 1, b)
                    pe_down(pe, CHUNKS - 1, (CHUNKS - 1) % 2, last_chunk=1)
                    pe.wait_ge(bank_free[0], ffn_used(CHUNKS, 10))
                    pe.wait_ge(slot_split, KT - 2 + 4 * CHUNKS + 1)
                    product(pe, 0, slot_lhs(0), u_rhs, KT, lambda k: pe.wait_ge(norm3[3], k + 1))
                    pe.wait_ge(bank_free[ffn_pair(12)], ffn_used(CHUNKS, 12) - 1)
                    norm_pe(pe, norm3, ACC3, ffn_pair(12), ms_done)

                @block.scalar
                def _(act):
                    exp_and_ln()
                    for t in range(TT):
                        nc.scalar.activation(GSQ[:, t, :], YA[:, t, :], ACT.Square,
                                             accum_out=GMS[:, 0, t:t + 1]).then_inc(group_sq, 1)
                    act.wait_ge(group_sq, TT)
                    for g in range(2):
                        if g == 1:
                            for t in range(PAIRS):
                                nc.scalar.activation(SQ2[t][:, :], YB[:, t, :], ACT.Square).then_inc(b_sq, 1)
                            act.wait_ge(c_sq, 2)
                        nc.scalar.activation(GMS[:, g, :], GMS[:, g, :], ACT.Ln, scale=1.0 / GROUP_W,
                                             bias=eps[:, 0:1]).then_inc(group_part, 1)
                        act.wait_ge(group_part, g + 1)
                        nc.scalar.activation(GMS[:, g, :], GMS[:, g, :], ACT.Exp, scale=-0.5)\
                            .then_inc(group_rstd, 1)
                    for t in range(PAIRS):
                        nc.scalar.activation(uhi[:, 6 + t, :], YD[:, t, :], ACT.Copy).then_inc(mix_hi, 1)
                    act.wait_ge(proj_done, J_B + 1)
                    nc.scalar.activation(wide(BRS[:, :]), pair(J_B), ACT.Ln, scale=1.0 / GROUP_W,
                                         bias=eps[:, 0:1]).then_inc(bank_free[J_B], 1)
                    act.wait_ge(bank_free[J_B], 1)
                    nc.scalar.activation(BRS[:, :], BRS[:, :], ACT.Exp, scale=-0.5).then_inc(b_rstd, 1)
                    for j, _, g, half, tile in AC_TILES:
                        gain = vecs[:, V_GN + 4 * g + half:V_GN + 4 * g + half + 1]
                        act.wait_ge(proj_done, j + 1)
                        nc.scalar.activation(wide(uhi[:, tile, :]), pair(j % 4), ACT.Copy, scale=gain)\
                            .then_inc(mix_hi, 1)
                    for t in range(PAIRS):
                        act.wait_ge(b_t, t + 1)
                        nc.scalar.activation(uhi[:, 2 + t, :], BT[t][:, :], ACT.Copy).then_inc(mix_hi, 1)

                    for m in range(KT):
                        j = J_OUT + m
                        act.wait_ge(bank_free[j % 4], j // 4 + 1)
                        norm_act(act, norm2, m, SQ2, U2H[:, m, :], ln2(m))
                    act.wait_ge(proj_done, J_NORM + 1)
                    norm_rs(act, J_NORM % 4, (bank_free[J_NORM % 4], J_NORM // 4 + 1))
                    act_chunk(act, 0, 0, first=True)
                    with act.Fori(0, (CHUNKS - 1) // 2) as r:
                        for b in range(2):
                            act_chunk(act, 2 * r + (b + 1), (b + 1) % 2)
                    exp_and_ln()
                    act.wait_ge(vecs_loaded, 16)
                    for m in range(KT):
                        p = ffn_pair(4 + m)
                        act.wait_ge(bank_free[p], ffn_used(CHUNKS, 4 + m))
                        norm_act(act, norm3, m, SQ3, uhi[:, m, :], ln1(m))
                    act.wait_ge(ms_done, 1)
                    norm_rs(act, ffn_pair(12), (rs_part, 1))

                @block.vector
                def _(dve):
                    nc.vector.tensor_tensor(GSQ[:, TT:, :], YC[:, :, :], YC[:, :, :], ALU.mult).then_inc(c_sq, 1)
                    dve.wait_ge(c_sq, 1)
                    nc.vector.tensor_reduce(GMS[:, 1, :], GSQ[:, TT:, :], AX.X, ALU.add).then_inc(c_sq, 1)
                    for g, y in enumerate((YA, YC)):
                        dve.wait_ge(group_rstd, g + 1)
                        nc.vector.tensor_tensor(
                            y[:, :, :], y[:, :, :],
                            GMS[:, g, :].rearrange("p (t o) -> p t o", o=1).broadcast_to([P, TT, GROUP_W]),
                            ALU.mult).then_inc(group_scaled, 1)
                    dve.wait_ge(b_rstd, 1)
                    for t in range(PAIRS):
                        nc.vector.scalar_tensor_tensor(BT[t][:, :], YB[:, t, :], vecs[:, V_GN + 2 + t:V_GN + 3 + t],
                                                       BRS[:, :], ALU.mult, ALU.mult).then_inc(b_t, 1)
                    for n, (j, _, g, half, tile) in enumerate(AC_TILES):
                        gain = vecs[:, V_GN + 4 * g + half:V_GN + 4 * g + half + 1]
                        dve.wait_ge(mix_hi, PAIRS + n + 1)
                        nc.vector.scalar_tensor_tensor(wide(ulo[:, tile, :]), pair(j % 4), gain,
                                                       wide(uhi[:, tile, :].bitcast(F32)),
                                                       ALU.mult, ALU.subtract).then_inc(bank_free[j % 4], 1)
                    for t in range(PAIRS):
                        dve.wait_ge(mix_hi, PAIRS + 4 + t + 1)
                        nc.vector.tensor_tensor(ulo[:, 2 + t, :], BT[t][:, :], uhi[:, 2 + t, :].bitcast(F32),
                                                ALU.subtract).then_inc(mix_lo, 1)
                    dve.wait_ge(h_loaded, 16 * KT)
                    for m in range(KT):
                        j = J_OUT + m
                        dve.wait_ge(proj_done, j + 1)
                        nc.vector.tensor_tensor(wide(h[:, m, :]), pair(j % 4), wide(h[:, m, :]), ALU.add)\
                            .then_inc(bank_free[j % 4], 1)
                        if m >= 1:
                            norm_dve(dve, norm2, m - 1, U2H[:, m - 1, :], U2L[m - 1][:, :], ln2(m - 1))
                    norm_dve(dve, norm2, KT - 1, U2H[:, KT - 1, :], U2L[KT - 1][:, :], ln2(KT - 1))
                    dve.wait_ge(rstd_ready, 1)
                    dve_chunk(dve, 0, 0, first=True)
                    with dve.Fori(0, (CHUNKS - 1) // 2) as r:
                        for b in range(2):
                            i = 2 * r + (b + 1)
                            dve_chunk(dve, i, (b + 1) % 2)
                            dve_down(dve, i - 1)

                    def next_lo(m):
                        norm_dve(dve, norm3, m, *u_at(m), ln1(m))

                    dve.wait_ge(vecs_loaded, 16)
                    dve_down(dve, CHUNKS - 1, next_lo)
                    next_lo(KT - 1)

        OT = at_u("out_tokens", 0, [P, TT, D])
        FT = [at_r(f"final_t{i}", 64 + 4 * i, [P, S]) for i in range(3)]
        ft_ready = sem("ft_ready")
        out_ready = sem("out_ready")

        def final():
            with nc.Block() as block:
                @block.sync
                def _(sp):
                    for k in range(KT):
                        sp.wait_ge(out_ready, k + 1)
                        at = slice(k * P, (k + 1) * P)
                        sp.dma_start(out.rearrange("(t p) f -> p t f", p=P)[:, :, at], OT[:, :, at])\
                            .then_inc(stored, 16)
                    sp.wait_ge(stored, 16 * KT)

                @block.tensor
                def _(pe):
                    for k in range(KT):
                        pe.wait_ge(ft_ready, k + 1)
                        if k >= 4:
                            pe.wait_ge(out_ready, k - 3)
                        for t in range(TT):
                            last = nc.tensor.transpose(ps[:, 2 * (k % 4) + t // 4, (t % 4) * P:(t % 4 + 1) * P],
                                                       FT[k % 3][:, t * P:(t + 1) * P], ident)
                        last.then_inc(proj_done, 1)

                @block.scalar
                def _(act):
                    for k in range(KT):
                        act.wait_ge(proj_done, k + 1)
                        nc.scalar.activation(OT[:, :, k * P:(k + 1) * P],
                                             pair(k % 4).rearrange("p b (t c) -> p (b t) c", c=P), ACT.Copy)\
                            .then_inc(out_ready, 1)

                @block.vector
                def _(dve):
                    for k in range(KT):
                        if k >= 3:
                            dve.wait_ge(proj_done, k - 2)
                        nc.vector.scalar_tensor_tensor(FT[k % 3][:, :], h[:, k, :], ln1(k), RS[:, :],
                                                       ALU.mult, ALU.mult).then_inc(ft_ready, 1)

        with nc.Fori(0, DEPTH) as l:
            with nc.Fori(0, PAIRS) as pr:
                group_bd(l, pr)
                end_of_block()

            latents(l)
            end_of_block()

            with nc.Fori(0, PAIRS) as pr:
                group_ac(pr)
                end_of_block()

            output_ffn(l)
            end_of_block()

        final()


def constants():
    c = np.zeros((P, K_N), np.float32)
    q, k = np.arange(P)[:, None], np.arange(P)[None, :]
    c[:, K_ID:K_ID + P] = q == k
    c[:, K_NEGS:K_NEGS + P] = np.where(k < q, 0.0, MASKED)
    c[:, K_NEGC:K_NEGC + P] = np.where(k <= q, 0.0, MASKED)
    c[:, K_HEADS:K_HEADS + P] = q // HD == k // HD
    half = ROPE // 2
    freq = np.float32(10000.0) ** (-np.arange(half, dtype=np.float32) / np.float32(half))
    c[0:64, K_FREQ] = freq[np.arange(64) % 32 % half]
    c[32:64, K_SIGN] = np.where(np.arange(32) < half, -1.0, 1.0)
    lm = np.zeros((P, LEVELS, 64), np.int32)
    for L in range(LEVELS):
        n = 64 >> L
        for j in range(64):
            block = j // n
            lm[block * 2 * n:block * 2 * n + n, L, j] = 1
    return c, lm.reshape(P, LEVELS * 64)


def vector_table(ln1_g, ln2_g, q_norm, kv_norm, group_norm, conv_w, conv_b, b_a, b_x, lam, hg, final_g):
    cols = lambda a, l: np.asarray(a)[l].reshape(-1, P).T
    table = np.zeros((DEPTH + 1, P, V_ROWS), np.float32)
    for l in range(DEPTH):
        for pr in range(PAIRS):
            own = [cols(conv_w, l)[:, pr::PAIRS]] + [cols(a, l)[:, pr:pr + 1] for a in (conv_b, b_a, b_x, lam, hg)]
            table[l, :, pr * PAIR_ROWS:(pr + 1) * PAIR_ROWS] = np.concatenate(own, 1)
        table[l, :, V_LN1:] = np.concatenate([cols(a, l) for a in (ln1_g, ln2_g, q_norm, kv_norm, group_norm)], 1)
    table[DEPTH, :, V_LN1:V_LN1 + KT] = np.asarray(final_g).reshape(KT, P).T
    return table.reshape(-1, V_ROWS)


def kernel(x, positions, ln1_g, w_in, mla_q_norm_g, mla_w_uq, mla_kv_norm_g, mla_w_ukv,
           lru_conv_w, lru_conv_b, lru_w_a, lru_b_a, lru_w_x, lru_b_x, lru_lambda,
           hgrn_lb_logits, hgrn_norm_g, group_norm_g, w_out, ln2_g,
           w_ffn_gate, w_ffn_up, w_ffn_down, final_norm_g):
    import concourse.bacc as bacc
    from concourse.bass_utils import run_bass_kernel_spmd

    arrays = dict(
        x=x.reshape(S, D), positions=positions.reshape(1, S),
        vec_table=vector_table(ln1_g, ln2_g, mla_q_norm_g, mla_kv_norm_g, group_norm_g, lru_conv_w, lru_conv_b,
                               lru_b_a, lru_b_x, lru_lambda, hgrn_norm_g, final_norm_g),
        w_in=w_in.reshape(-1, D_IN), w_uq=mla_w_uq.reshape(-1, mla_w_uq.shape[-1]),
        w_ukv=mla_w_ukv.reshape(-1, mla_w_ukv.shape[-1]),
        w_a=lru_w_a.reshape(-1, 64), w_x=lru_w_x.reshape(-1, 64),
        lb_logits=hgrn_lb_logits.reshape(-1, P).T, w_out=w_out.reshape(-1, D),
        w_gate=w_ffn_gate.reshape(-1, FFN), w_up=w_ffn_up.reshape(-1, FFN), w_down=w_ffn_down.reshape(-1, D))
    arrays["consts"], arrays["level_masks"] = constants()
    arrays = {name: np.ascontiguousarray(a) for name, a in arrays.items()}
    nc = bacc.Bacc("TRN2", target_bir_lowering=False, num_devices=1)
    ap = {name: nc.dram_tensor(name, a.shape, mybir.dt.from_np(a.dtype), kind="ExternalInput").ap()
          for name, a in arrays.items()}
    out = nc.dram_tensor("out", (S, D), F32, kind="ExternalOutput").ap()
    build(nc, out=out, **ap)
    r = run_bass_kernel_spmd(nc, [arrays], core_ids=[0])
    return r.results[0]["out"].reshape(1, S, D)
```
